# Optimizing a Trainium2 kernel written in Bass

```python
import math
import jax
import jax.numpy as jnp
from jax import lax
import numpy as np

D_MODEL = 1024
BATCH = 1
SEQ = 256
DEPTH = 2

N_MIXERS = 3
D_PLE = 256
NORM_EPS = 1e-6
Q_BLOCK = 128
NEG_INF = -1e30

MLA_HEADS = 16
MLA_Q_RANK = 384
MLA_KV_RANK = 256
MLA_NOPE = 64
MLA_ROPE = 32
MLA_V = 64
ROPE_THETA = 10000.0

DIL_PATTERNS = ((128, 1), (512, 4), (2048, 16))
DIL_GROUPS = len(DIL_PATTERNS)
DIL_HEADS = 16
DIL_HEAD_DIM = 64

REL_BUCKETS = 32
REL_MAX_DIST = 2048

FOX_HEADS = 16
FOX_HEAD_DIM = 64

D_FF = -(-8 * D_MODEL // (3 * 256)) * 256


def rms_norm(x, g):
    xf = x.astype(jnp.float32)
    y = xf * lax.rsqrt(jnp.mean(xf * xf, axis=-1, keepdims=True) + NORM_EPS)
    return (y * g.astype(jnp.float32)).astype(x.dtype)

def apply_rope(x, positions):
    half = x.shape[-1] // 2
    inv = ROPE_THETA ** (-jnp.arange(half, dtype=jnp.float32) / half)
    ang = positions.astype(jnp.float32)[:, :, None, None] * inv
    cos, sin = jnp.cos(ang), jnp.sin(ang)
    xf = x.astype(jnp.float32)
    x1, x2 = xf[..., :half], xf[..., half:]
    return jnp.concatenate([x1 * cos - x2 * sin, x2 * cos + x1 * sin], axis=-1).astype(x.dtype)

def causal_block_attention(q, k, v, scale, log_forget_cumsum=None):
    s_len = q.shape[1]
    outs = []
    for b0 in range(0, s_len, Q_BLOCK):
        b1 = b0 + Q_BLOCK
        qb, kb, vb = q[:, b0:b1], k[:, :b1], v[:, :b1]
        logits = jnp.einsum('bqhd,bkhd->bhqk', qb, kb).astype(jnp.float32) * scale
        if log_forget_cumsum is not None:
            c_q = jnp.transpose(log_forget_cumsum[:, b0:b1], (0, 2, 1))
            c_k = jnp.transpose(log_forget_cumsum[:, :b1], (0, 2, 1))
            logits = logits + (c_q[..., :, None] - c_k[..., None, :])
        q_idx = b0 + jnp.arange(Q_BLOCK)
        k_idx = jnp.arange(b1)
        causal = k_idx[None, :] <= q_idx[:, None]
        logits = jnp.where(causal, logits, NEG_INF)
        probs = jax.nn.softmax(logits, axis=-1).astype(v.dtype)
        outs.append(jnp.einsum('bhqk,bkhd->bqhd', probs, vb))
    return jnp.concatenate(outs, axis=1)

def t5_bucket(dist):
    max_exact = REL_BUCKETS // 2
    n = jnp.maximum(dist.astype(jnp.float32), 1.0)
    large = max_exact + (jnp.log(n / max_exact) / math.log(REL_MAX_DIST / max_exact)
                         * (REL_BUCKETS - max_exact)).astype(jnp.int32)
    large = jnp.minimum(large, REL_BUCKETS - 1)
    return jnp.where(dist < max_exact, dist, large)

def dilated_branch(q, k, v, dilation, span, bias_table):
    b, s_len, h, dh = q.shape
    sub_len = s_len // dilation
    n_blk = -(-sub_len // Q_BLOCK)
    pad_len = n_blk * Q_BLOCK

    def to_blocks(t):
        t = t.reshape(b, sub_len, dilation, h, dh).transpose(0, 2, 1, 3, 4)
        t = t.reshape(b * dilation, sub_len, h, dh)
        t = jnp.pad(t, ((0, 0), (0, pad_len - sub_len), (0, 0), (0, 0)))
        return t.reshape(b * dilation, n_blk, Q_BLOCK, h, dh)

    def with_previous(t):
        prev = jnp.concatenate([jnp.zeros_like(t[:, :1]), t[:, :-1]], axis=1)
        return jnp.concatenate([prev, t], axis=2)

    qs = to_blocks(q)
    kb = with_previous(to_blocks(k))
    vb = with_previous(to_blocks(v))

    logits = jnp.einsum('bnqhd,bnkhd->bnhqk', qs, kb).astype(jnp.float32) * (dh ** -0.5)
    i = jnp.arange(Q_BLOCK)
    j = jnp.arange(2 * Q_BLOCK)
    rel = Q_BLOCK + i[:, None] - j[None, :]
    bucket = t5_bucket(jnp.clip(rel, 0) * dilation)
    bias = jnp.transpose(bias_table[bucket].astype(jnp.float32), (2, 0, 1))
    key_pos = jnp.arange(n_blk)[:, None] * Q_BLOCK - Q_BLOCK + j[None, :]
    valid = ((rel >= 0) & (rel <= span))[None] & (key_pos >= 0)[:, None, :]
    logits = jnp.where(valid[None, :, None], logits + bias[None, None], NEG_INF)
    lse = jax.nn.logsumexp(logits, axis=-1, keepdims=True)
    probs = jnp.exp(logits - lse).astype(v.dtype)
    o = jnp.einsum('bnhqk,bnkhd->bnqhd', probs, vb)

    o = o.reshape(b * dilation, pad_len, h, dh)[:, :sub_len]
    o = o.reshape(b, dilation, sub_len, h, dh).transpose(0, 2, 1, 3, 4).reshape(b, s_len, h, dh)
    lse = jnp.transpose(lse[..., 0], (0, 1, 3, 2)).reshape(b * dilation, pad_len, h)[:, :sub_len]
    lse = lse.reshape(b, dilation, sub_len, h).transpose(0, 2, 1, 3).reshape(b, s_len, h)
    return o, lse

def mla_mixer(h, positions, w_a, q_norm, kv_norm, w_uq, w_ukv, w_o):
    b, s_len, _ = h.shape
    a = h @ w_a
    c_q = rms_norm(a[..., :MLA_Q_RANK], q_norm)
    c_kv = rms_norm(a[..., MLA_Q_RANK:MLA_Q_RANK + MLA_KV_RANK], kv_norm)
    k_rot = apply_rope(a[..., MLA_Q_RANK + MLA_KV_RANK:][:, :, None, :], positions)
    q = (c_q @ w_uq).reshape(b, s_len, MLA_HEADS, MLA_NOPE + MLA_ROPE)
    q = jnp.concatenate([q[..., :MLA_NOPE], apply_rope(q[..., MLA_NOPE:], positions)], axis=-1)
    kv = (c_kv @ w_ukv).reshape(b, s_len, MLA_HEADS, MLA_NOPE + MLA_V)
    k = jnp.concatenate([kv[..., :MLA_NOPE],
                         jnp.broadcast_to(k_rot, (b, s_len, MLA_HEADS, MLA_ROPE))], axis=-1)
    v = kv[..., MLA_NOPE:]
    o = causal_block_attention(q, k, v, (MLA_NOPE + MLA_ROPE) ** -0.5)
    return o.reshape(b, s_len, MLA_HEADS * MLA_V) @ w_o

def dilated_mixer(h, w_qkv, w_o, rel_bias):
    b, s_len, _ = h.shape
    qkv = (h @ w_qkv).reshape(b, s_len, DIL_GROUPS, 3, DIL_HEADS, DIL_HEAD_DIM)
    table = rel_bias.reshape(REL_BUCKETS, DIL_GROUPS, DIL_HEADS)
    outs, lses = [], []
    for g, (window, dilation) in enumerate(DIL_PATTERNS):
        o, lse = dilated_branch(qkv[:, :, g, 0], qkv[:, :, g, 1], qkv[:, :, g, 2],
                                dilation, window // dilation, table[:, g])
        outs.append(o)
        lses.append(lse)
    alpha = jax.nn.softmax(jnp.stack(lses, axis=0), axis=0)
    o = jnp.sum(alpha[..., None] * jnp.stack(outs, axis=0).astype(jnp.float32), axis=0).astype(h.dtype)
    return o.reshape(b, s_len, DIL_HEADS * DIL_HEAD_DIM) @ w_o

def fox_mixer(h, w_qkvf, b_f, w_o):
    b, s_len, _ = h.shape
    inner = FOX_HEADS * FOX_HEAD_DIM
    a = h @ w_qkvf
    qkv = a[..., :3 * inner].reshape(b, s_len, 3, FOX_HEADS, FOX_HEAD_DIM)
    log_f = jax.nn.log_sigmoid((a[..., 3 * inner:] + b_f).astype(jnp.float32))
    cum = jnp.cumsum(log_f, axis=1)
    o = causal_block_attention(qkv[:, :, 0], qkv[:, :, 1], qkv[:, :, 2], FOX_HEAD_DIM ** -0.5, cum)
    return o.reshape(b, s_len, inner) @ w_o

def swiglu(h, w_in, w_out):
    gu = h @ w_in
    return (jax.nn.silu(gu[..., :D_FF]) * gu[..., D_FF:]) @ w_out

def first_inputs(seed: int = 0) -> dict:
    key = jax.random.key(seed)
    ks = jax.random.split(key, 20)
    f32 = jnp.float32
    n_a, n_b, n_c = (len(range(m, DEPTH, N_MIXERS)) for m in range(N_MIXERS))

    def dense(k, shape):
        return jax.random.normal(k, shape, f32) * shape[-2] ** -0.5

    def gain(k, shape):
        return 1.0 + 0.1 * jax.random.normal(k, shape, f32)

    x = jax.random.normal(ks[0], (BATCH, SEQ, D_MODEL), f32)
    p = jax.random.normal(ks[1], (DEPTH, BATCH, SEQ, D_PLE), f32)
    offsets = jax.random.randint(ks[2], (BATCH, 1), 0, 4096, jnp.int32)
    positions = (offsets + jnp.arange(SEQ, dtype=jnp.int32)[None, :]).astype(jnp.int32)
    norm_g = gain(ks[3], (DEPTH, 4, D_MODEL))
    ffn_w_in = dense(ks[4], (DEPTH, D_MODEL, 2 * D_FF))
    ffn_w_out = dense(ks[5], (DEPTH, D_FF, D_MODEL))
    ple_w_proj = dense(ks[6], (DEPTH, D_PLE, D_MODEL))
    ple_w_gate = dense(ks[7], (DEPTH, D_MODEL, D_MODEL))
    rel_bias = 0.5 * jax.random.normal(ks[8], (REL_BUCKETS, DIL_GROUPS * DIL_HEADS), f32)
    mla_w_a = dense(ks[9], (n_a, D_MODEL, MLA_Q_RANK + MLA_KV_RANK + MLA_ROPE))
    mla_q_norm = gain(ks[10], (n_a, MLA_Q_RANK))
    mla_kv_norm = gain(ks[11], (n_a, MLA_KV_RANK))
    mla_w_uq = dense(ks[12], (n_a, MLA_Q_RANK, MLA_HEADS * (MLA_NOPE + MLA_ROPE)))
    mla_w_ukv = dense(ks[13], (n_a, MLA_KV_RANK, MLA_HEADS * (MLA_NOPE + MLA_V)))
    mla_w_o = dense(ks[14], (n_a, MLA_HEADS * MLA_V, D_MODEL))
    dil_w_qkv = dense(ks[15], (n_b, D_MODEL, DIL_GROUPS * 3 * DIL_HEADS * DIL_HEAD_DIM))
    dil_w_o = dense(ks[16], (n_b, DIL_HEADS * DIL_HEAD_DIM, D_MODEL))
    fox_w_qkvf = dense(ks[17], (n_c, D_MODEL, 3 * FOX_HEADS * FOX_HEAD_DIM + FOX_HEADS))
    fox_b_f = jax.random.uniform(ks[18], (n_c, FOX_HEADS), f32, 1.0, 5.0)
    fox_w_o = dense(ks[19], (n_c, FOX_HEADS * FOX_HEAD_DIM, D_MODEL))
    return {'x': x, 'p': p, 'positions': positions, 'norm_g': norm_g,
            'ffn_w_in': ffn_w_in, 'ffn_w_out': ffn_w_out,
            'ple_w_proj': ple_w_proj, 'ple_w_gate': ple_w_gate, 'rel_bias': rel_bias,
            'mla_w_a': mla_w_a, 'mla_q_norm': mla_q_norm, 'mla_kv_norm': mla_kv_norm,
            'mla_w_uq': mla_w_uq, 'mla_w_ukv': mla_w_ukv, 'mla_w_o': mla_w_o,
            'dil_w_qkv': dil_w_qkv, 'dil_w_o': dil_w_o,
            'fox_w_qkvf': fox_w_qkvf, 'fox_b_f': fox_b_f, 'fox_w_o': fox_w_o}

def first_block(x, p, positions, norm_g, ffn_w_in, ffn_w_out, ple_w_proj, ple_w_gate, rel_bias,
              mla_w_a, mla_q_norm, mla_kv_norm, mla_w_uq, mla_w_ukv, mla_w_o,
              dil_w_qkv, dil_w_o, fox_w_qkvf, fox_b_f, fox_w_o):
    h = x
    for i in range(DEPTH):
        mixer, j = i % N_MIXERS, i // N_MIXERS
        g = norm_g[i]
        hn = rms_norm(h, g[0])
        if mixer == 0:
            y = mla_mixer(hn, positions, mla_w_a[j], mla_q_norm[j], mla_kv_norm[j],
                          mla_w_uq[j], mla_w_ukv[j], mla_w_o[j])
        elif mixer == 1:
            y = dilated_mixer(hn, dil_w_qkv[j], dil_w_o[j], rel_bias)
        else:
            y = fox_mixer(hn, fox_w_qkvf[j], fox_b_f[j], fox_w_o[j])
        h = h + rms_norm(y, g[1])
        h = h + rms_norm(swiglu(rms_norm(h, g[2]), ffn_w_in[i], ffn_w_out[i]), g[3])
        h = h + (p[i] @ ple_w_proj[i]) * jax.nn.sigmoid(h @ ple_w_gate[i])
    return h


GRID_W = 64
CTX_LEN = 256
EPS = 1e-6
NEG_INF_2 = -1e30

DA_HEADS = 4
DA_HEAD_DIM = 64
DA_QK_WIDTH = DA_HEADS * 2 * DA_HEAD_DIM
DA_V_WIDTH = DA_HEADS * 2 * DA_HEAD_DIM
ROPE_AXIS = DA_HEAD_DIM // 2
ROPE_HALF = ROPE_AXIS // 2

SG_CHUNK = 128
SG_GROUPS = 4
SG_WIDTH = 512
SG_GROUP_DIM = SG_WIDTH // SG_GROUPS

NA_HEADS = 8
NA_HEAD_DIM = 64
NA_WIDTH = NA_HEADS * NA_HEAD_DIM
NA_ROWS_MAX = 8
NA_COLS = 16

N_BRANCH = 3
BRANCH_WIDTH = 512

OFF_KA = 0
OFF_VA = OFF_KA + DA_QK_WIDTH
OFF_KC = OFF_VA + DA_V_WIDTH
OFF_VC = OFF_KC + NA_WIDTH
KV_COLS = OFF_VC + NA_WIDTH
OFF_QA = KV_COLS
OFF_QC = OFF_QA + DA_QK_WIDTH
OFF_ZB = OFF_QC + NA_WIDTH
OFF_GATE = OFF_ZB + 2 * SG_WIDTH
IN_COLS = OFF_GATE + N_BRANCH * D_MODEL

N_GROUPS = 4
EXPERTS_PER_GROUP = 8
N_EXPERTS = N_GROUPS * EXPERTS_PER_GROUP
TOP_K = 2
D_EXPERT = 512
MOE_BLOCK = 128


def rms_norm_2(x, g):
    xf = x.astype(jnp.float32)
    y = xf * lax.rsqrt(jnp.mean(xf * xf, axis=-1, keepdims=True) + EPS)
    return (y * g.astype(jnp.float32)).astype(x.dtype)

def layer_norm(x, g, b):
    xf = x.astype(jnp.float32)
    mu = jnp.mean(xf, axis=-1, keepdims=True)
    var = jnp.mean(jnp.square(xf - mu), axis=-1, keepdims=True)
    y = (xf - mu) * lax.rsqrt(var + EPS)
    return (y * g.astype(jnp.float32) + b.astype(jnp.float32)).astype(x.dtype)

def ada_modulation(cond, w, b):
    m = cond @ w + b
    return jnp.split(m[:, None, :], 6, axis=-1)

def modulate(xn, shift, scale):
    return xn * (1.0 + scale) + shift

def da_qk_heads(t):
    return t.reshape(*t.shape[:-1], DA_HEADS, 2, DA_HEAD_DIM)

def da_v_heads(t):
    return t.reshape(*t.shape[:-1], DA_HEADS, 2 * DA_HEAD_DIM)

def na_heads(t):
    return t.reshape(*t.shape[:-1], NA_HEADS, NA_HEAD_DIM)

def axial_rope_tables(n_tok):
    t = jnp.arange(n_tok, dtype=jnp.int32)
    row = (t // GRID_W).astype(jnp.float32)
    col = (t % GRID_W).astype(jnp.float32)
    inv = ROPE_THETA ** (-jnp.arange(ROPE_HALF, dtype=jnp.float32) / ROPE_HALF)
    ar = row[:, None] * inv
    ac = col[:, None] * inv
    ang = jnp.concatenate([ar, ar, ac, ac], axis=-1)
    return jnp.cos(ang), jnp.sin(ang)

def apply_axial_rope(x, cos, sin):
    x1, x2, x3, x4 = jnp.split(x, 4, axis=-1)
    rot = jnp.concatenate([-x2, x1, -x4, x3], axis=-1)
    cos = cos[None, :, None, None, :].astype(x.dtype)
    sin = sin[None, :, None, None, :].astype(x.dtype)
    return x * cos + rot * sin

def diff_softmax_mix(q, k, v, lam):
    s = jnp.einsum('bqhmd,bkhmd->bhmqk', q, k).astype(jnp.float32) * (DA_HEAD_DIM ** -0.5)
    p = jax.nn.softmax(s, axis=-1)
    w = (p[:, :, 0] - lam * p[:, :, 1]).astype(v.dtype)
    return jnp.einsum('bhqk,bkhe->bqhe', w, v)

def diff_attention_latent(q, k, v, k_ctx, v_ctx, lam):
    b, n = q.shape[:2]
    k_all = jnp.concatenate([k_ctx, k], axis=1)
    v_all = jnp.concatenate([v_ctx, v], axis=1)
    qb = q.reshape(b, n // Q_BLOCK, Q_BLOCK, DA_HEADS, 2, DA_HEAD_DIM).swapaxes(0, 1)
    o = lax.map(lambda qq: diff_softmax_mix(qq, k_all, v_all, lam), qb)
    return o.swapaxes(0, 1).reshape(b, n, DA_HEADS, 2 * DA_HEAD_DIM)

def diff_post(o, g, lam_init):
    y = rms_norm_2(o, g) * (1.0 - lam_init)
    return y.reshape(*o.shape[:2], DA_V_WIDTH)

def spatial_gating(z, ln_g, ln_b, w_s, b_s):
    z = jax.nn.gelu(z)
    u, vv = jnp.split(z, 2, axis=-1)
    vv = layer_norm(vv, ln_g, ln_b)
    b, n, _ = vv.shape
    vv = vv.reshape(b, n // SG_CHUNK, SG_CHUNK, SG_GROUPS, SG_GROUP_DIM)
    s = jnp.einsum('gpq,bnqgc->bnpgc', w_s, vv) + b_s.T[None, None, :, :, None]
    return u * s.reshape(b, n, SG_WIDTH)

def neighbourhood_attention(q, k, v, k_ctx, v_ctx, rpb, rows):
    b, n, nh, dh = q.shape
    kr = min(NA_ROWS_MAX, rows)
    n_cb = GRID_W // NA_COLS
    half = NA_COLS // 2
    band_w = 2 * NA_COLS
    scale = dh ** -0.5

    def grid_padded(t):
        t = t.reshape(b, rows, GRID_W, nh, dh)
        return jnp.pad(t, ((0, 0), (0, 0), (half, half), (0, 0), (0, 0)))

    kg, vg = grid_padded(k), grid_padded(v)
    qcol = np.arange(GRID_W).reshape(n_cb, NA_COLS)
    kcol = np.arange(n_cb)[:, None] * NA_COLS - half + np.arange(band_w)[None, :]
    cstart = np.clip(qcol - half, 0, GRID_W - NA_COLS)
    col_ok = jnp.asarray((kcol[:, None, :] >= cstart[..., None]) & (kcol[:, None, :] < cstart[..., None] + NA_COLS))
    dc_idx = np.clip(kcol[:, None, :] - qcol[:, :, None] + NA_COLS - 1, 0, 2 * NA_COLS - 2)
    rpb_c = rpb.astype(jnp.float32)[:, :, dc_idx]

    def row_step(args):
        r, qr = args
        rs = jnp.clip(r - kr // 2, 0, rows - kr)

        def band(t):
            t = lax.dynamic_slice_in_dim(t, rs, kr, axis=1).reshape(b, kr, n_cb + 1, NA_COLS, nh, dh)
            return jnp.concatenate([t[:, :, :-1], t[:, :, 1:]], axis=3)

        kb, vb = band(kg), band(vg)
        qb = qr.reshape(b, n_cb, NA_COLS, nh, dh)
        s_win = jnp.einsum('bjqhd,brjkhd->bhjqrk', qb, kb).astype(jnp.float32) * scale
        dr_idx = rs + jnp.arange(kr) - r + NA_ROWS_MAX - 1
        bias = jnp.take(rpb_c, dr_idx, axis=1).transpose(0, 2, 3, 1, 4)
        s_win = jnp.where(col_ok[:, :, None, :], s_win + bias[None], NEG_INF_2)
        s_ctx = jnp.einsum('bjqhd,bkhd->bhjqk', qb, k_ctx).astype(jnp.float32) * scale
        nw = kr * band_w
        s = jnp.concatenate([s_win.reshape(b, nh, n_cb, NA_COLS, nw), s_ctx], axis=-1)
        p = jax.nn.softmax(s, axis=-1).astype(v.dtype)
        p_win = p[..., :nw].reshape(b, nh, n_cb, NA_COLS, kr, band_w)
        o = (jnp.einsum('bhjqrk,brjkhd->bjqhd', p_win, vb)
             + jnp.einsum('bhjqk,bkhd->bjqhd', p[..., nw:], v_ctx))
        return o.reshape(b, GRID_W, nh, dh)

    q_rows = q.reshape(b, rows, GRID_W, nh, dh).swapaxes(0, 1)
    o = lax.map(row_step, (jnp.arange(rows, dtype=jnp.int32), q_rows))
    return o.swapaxes(0, 1).reshape(b, n, nh * dh)

def ctx_attention(q, k, v):
    s = jnp.einsum('bqhd,bkhd->bhqk', q, k).astype(jnp.float32) * (q.shape[-1] ** -0.5)
    p = jax.nn.softmax(s, axis=-1).astype(v.dtype)
    o = jnp.einsum('bhqk,bkhd->bqhd', p, v)
    return o.reshape(*o.shape[:2], -1)

def merge_branches(p_gate, y_a, y_b, y_c, w_branch, w_out):
    ys = jnp.stack([y_a, y_b, y_c], axis=2)
    yb = jnp.einsum('bnie,ied->bnid', ys, w_branch)
    g = jax.nn.sigmoid(p_gate.reshape(*p_gate.shape[:-1], N_BRANCH, D_MODEL))
    return jnp.sum(g * yb, axis=2) @ w_out

def hier_moe(x, w_group, b_group, w_router, b_router, w_gate, w_up, w_down):
    t = x.shape[0]
    g_logits = (x @ w_group).astype(jnp.float32) + b_group.astype(jnp.float32)
    g_prob = jax.nn.softmax(g_logits, axis=-1)
    g_idx = jnp.argmax(g_logits, axis=-1)
    g_w = jnp.take_along_axis(g_prob, g_idx[:, None], axis=1)
    e_logits = ((x @ w_router).astype(jnp.float32) + b_router.astype(jnp.float32)).reshape(t, N_GROUPS, EXPERTS_PER_GROUP)
    e_logits = e_logits[jnp.arange(t), g_idx]
    top_l, top_i = lax.top_k(e_logits, TOP_K)
    top_w = jax.nn.softmax(top_l, axis=-1) * g_w
    expert = (g_idx[:, None] * EXPERTS_PER_GROUP + top_i).astype(jnp.int32)

    a = t * TOP_K
    flat_e = expert.reshape(a)
    order = jnp.argsort(flat_e).astype(jnp.int32)
    sorted_e = flat_e[order]
    counts = jnp.bincount(flat_e, length=N_EXPERTS)
    padded = (counts + MOE_BLOCK - 1) // MOE_BLOCK * MOE_BLOCK
    pad_end = jnp.cumsum(padded)
    pad_start = pad_end - padded
    start = jnp.cumsum(counts) - counts
    dest = pad_start[sorted_e] + jnp.arange(a, dtype=jnp.int32) - start[sorted_e]
    n_blocks = -(-(a + N_EXPERTS * (MOE_BLOCK - 1)) // MOE_BLOCK)
    n_slots = n_blocks * MOE_BLOCK
    slot_token = jnp.full((n_slots,), t, jnp.int32).at[dest].set(order // TOP_K)
    x_pad = jnp.concatenate([x, jnp.zeros((1, x.shape[1]), x.dtype)], axis=0)
    xs = x_pad[slot_token].reshape(n_blocks, MOE_BLOCK, x.shape[1])
    block_expert = jnp.minimum(jnp.searchsorted(pad_end, jnp.arange(n_blocks) * MOE_BLOCK, side='right'), N_EXPERTS - 1)

    def expert_block(args):
        xb, e = args
        hdn = jax.nn.silu(xb @ w_gate[e]) * (xb @ w_up[e])
        return hdn @ w_down[e]

    ys = lax.map(expert_block, (xs, block_expert)).reshape(n_slots, -1)
    w_sorted = top_w.reshape(a)[order].astype(ys.dtype)
    return jax.ops.segment_sum(ys[dest] * w_sorted[:, None], order // TOP_K, num_segments=t)

def second_inputs(seed: int = 0) -> dict:
    key = jax.random.key(seed)
    ks = jax.random.split(key, 32)
    f32 = jnp.float32
    D = D_MODEL

    def nrm(k, shape, scale):
        return jax.random.normal(k, shape, f32) * scale

    return {
        'x': nrm(ks[0], (BATCH, SEQ, D), 1.0),
        'c': nrm(ks[1], (BATCH, D), 1.0),
        'ctx': nrm(ks[2], (BATCH, CTX_LEN, D), 1.0),
        'c_ctx': nrm(ks[3], (D,), 1.0),
        'w_ada': nrm(ks[4], (DEPTH, D, 6 * D), 0.5 * D ** -0.5),
        'b_ada': nrm(ks[5], (DEPTH, 6 * D), 0.02),
        'g_norm_mix': 1.0 + nrm(ks[6], (DEPTH, D), 0.02),
        'g_norm_ffn': 1.0 + nrm(ks[7], (DEPTH, D), 0.02),
        'w_in': nrm(ks[8], (DEPTH, D, IN_COLS), D ** -0.5),
        'da_lambda': nrm(ks[9], (DEPTH, 4, DA_HEAD_DIM), 0.1),
        'da_subln_g': 1.0 + nrm(ks[10], (DEPTH, 2 * DA_HEAD_DIM), 0.02),
        'sg_ln_g': 1.0 + nrm(ks[11], (DEPTH, SG_WIDTH), 0.02),
        'sg_ln_b': nrm(ks[12], (DEPTH, SG_WIDTH), 0.02),
        'sg_w': nrm(ks[13], (DEPTH, SG_GROUPS, SG_CHUNK, SG_CHUNK), SG_CHUNK ** -0.5),
        'sg_b': 1.0 + nrm(ks[14], (DEPTH, SG_GROUPS, SG_CHUNK), 0.02),
        'na_rpb': nrm(ks[15], (DEPTH, NA_HEADS, 2 * NA_ROWS_MAX - 1, 2 * NA_COLS - 1), 0.1),
        'w_branch': nrm(ks[16], (DEPTH, N_BRANCH, BRANCH_WIDTH, D), BRANCH_WIDTH ** -0.5),
        'w_out': nrm(ks[17], (DEPTH, D, D), D ** -0.5),
        'moe_w_group': nrm(ks[18], (DEPTH, D, N_GROUPS), D ** -0.5),
        'moe_b_group': nrm(ks[19], (DEPTH, N_GROUPS), 0.01),
        'moe_w_router': nrm(ks[20], (DEPTH, D, N_EXPERTS), D ** -0.5),
        'moe_b_router': nrm(ks[21], (DEPTH, N_EXPERTS), 0.01),
        'moe_w_gate': nrm(ks[22], (DEPTH, N_EXPERTS, D, D_EXPERT), D ** -0.5),
        'moe_w_up': nrm(ks[23], (DEPTH, N_EXPERTS, D, D_EXPERT), D ** -0.5),
        'moe_w_down': nrm(ks[24], (DEPTH, N_EXPERTS, D_EXPERT, D), D_EXPERT ** -0.5),
        'g_final': 1.0 + nrm(ks[25], (D,), 0.02),
    }

def second_block(x, c, ctx, c_ctx, w_ada, b_ada, g_norm_mix, g_norm_ffn, w_in, da_lambda, da_subln_g,
              sg_ln_g, sg_ln_b, sg_w, sg_b, na_rpb, w_branch, w_out, moe_w_group, moe_b_group,
              moe_w_router, moe_b_router, moe_w_gate, moe_w_up, moe_w_down, g_final):
    b, n_lat, _ = x.shape
    n_ctx = ctx.shape[1]
    rows = n_lat // GRID_W
    cos, sin = axial_rope_tables(n_lat)
    cond_lat = jax.nn.silu(c)
    cond_ctx = jax.nn.silu(c_ctx)[None]
    h, hc = x, ctx
    for l in range(DEPTH):
        last = l == DEPTH - 1
        lam_init = 0.8 - 0.6 * math.exp(-0.3 * l)
        lq1, lk1, lq2, lk2 = da_lambda[l].astype(jnp.float32)
        lam = jnp.exp(jnp.sum(lq1 * lk1)) - jnp.exp(jnp.sum(lq2 * lk2)) + lam_init
        sh1, sc1, gt1, sh2, sc2, gt2 = ada_modulation(cond_lat, w_ada[l], b_ada[l])
        csh1, csc1, cgt1, csh2, csc2, cgt2 = ada_modulation(cond_ctx, w_ada[l], b_ada[l])

        xn = modulate(rms_norm_2(h, g_norm_mix[l]), sh1, sc1)
        xc = modulate(rms_norm_2(hc, g_norm_mix[l]), csh1, csc1)
        p = xn @ w_in[l]
        pc = xc @ (w_in[l][:, :KV_COLS] if last else w_in[l])
        ka_c = da_qk_heads(pc[..., OFF_KA:OFF_VA])
        va_c = da_v_heads(pc[..., OFF_VA:OFF_KC])
        kc_c = na_heads(pc[..., OFF_KC:OFF_VC])
        vc_c = na_heads(pc[..., OFF_VC:KV_COLS])

        qa = apply_axial_rope(da_qk_heads(p[..., OFF_QA:OFF_QC]), cos, sin)
        ka = apply_axial_rope(da_qk_heads(p[..., OFF_KA:OFF_VA]), cos, sin)
        va = da_v_heads(p[..., OFF_VA:OFF_KC])
        y_a = diff_post(diff_attention_latent(qa, ka, va, ka_c, va_c, lam), da_subln_g[l], lam_init)
        y_b = spatial_gating(p[..., OFF_ZB:OFF_GATE], sg_ln_g[l], sg_ln_b[l], sg_w[l], sg_b[l])
        y_c = neighbourhood_attention(na_heads(p[..., OFF_QC:OFF_ZB]), na_heads(p[..., OFF_KC:OFF_VC]),
                                      na_heads(p[..., OFF_VC:KV_COLS]), kc_c, vc_c, na_rpb[l], rows)
        h = h + gt1 * merge_branches(p[..., OFF_GATE:], y_a, y_b, y_c, w_branch[l], w_out[l])
        if not last:
            ya_c = diff_post(diff_softmax_mix(da_qk_heads(pc[..., OFF_QA:OFF_QC]), ka_c, va_c, lam), da_subln_g[l], lam_init)
            yb_c = spatial_gating(pc[..., OFF_ZB:OFF_GATE], sg_ln_g[l], sg_ln_b[l], sg_w[l], sg_b[l])
            yc_c = ctx_attention(na_heads(pc[..., OFF_QC:OFF_ZB]), kc_c, vc_c)
            hc = hc + cgt1 * merge_branches(pc[..., OFF_GATE:], ya_c, yb_c, yc_c, w_branch[l], w_out[l])

        xn2 = modulate(rms_norm_2(h, g_norm_ffn[l]), sh2, sc2).reshape(b * n_lat, D_MODEL)
        if last:
            y = hier_moe(xn2, moe_w_group[l], moe_b_group[l], moe_w_router[l], moe_b_router[l],
                         moe_w_gate[l], moe_w_up[l], moe_w_down[l])
            h = h + gt2 * y.reshape(b, n_lat, D_MODEL)
        else:
            xc2 = modulate(rms_norm_2(hc, g_norm_ffn[l]), csh2, csc2).reshape(b * n_ctx, D_MODEL)
            y = hier_moe(jnp.concatenate([xn2, xc2], axis=0), moe_w_group[l], moe_b_group[l],
                         moe_w_router[l], moe_b_router[l], moe_w_gate[l], moe_w_up[l], moe_w_down[l])
            h = h + gt2 * y[:b * n_lat].reshape(b, n_lat, D_MODEL)
            hc = hc + cgt2 * y[b * n_lat:].reshape(b, n_ctx, D_MODEL)
    return rms_norm_2(h, g_final)


def setup_inputs(seed=0):
    out = dict(first_inputs(seed))
    for name, value in second_inputs(seed + 1).items():
        if name != "x":
            out[name + "_2"] = value
    return out


def reference(
    x, p, positions, norm_g, ffn_w_in, ffn_w_out, ple_w_proj, ple_w_gate, rel_bias, mla_w_a,
    mla_q_norm, mla_kv_norm, mla_w_uq, mla_w_ukv, mla_w_o, dil_w_qkv, dil_w_o, fox_w_qkvf,
    fox_b_f, fox_w_o, c_2, ctx_2, c_ctx_2, w_ada_2, b_ada_2, g_norm_mix_2, g_norm_ffn_2, w_in_2,
    da_lambda_2, da_subln_g_2, sg_ln_g_2, sg_ln_b_2, sg_w_2, sg_b_2, na_rpb_2, w_branch_2,
    w_out_2, moe_w_group_2, moe_b_group_2, moe_w_router_2, moe_b_router_2, moe_w_gate_2,
    moe_w_up_2, moe_w_down_2, g_final_2,
):
    x = first_block(
        x, p, positions, norm_g, ffn_w_in, ffn_w_out, ple_w_proj, ple_w_gate, rel_bias, mla_w_a,
        mla_q_norm, mla_kv_norm, mla_w_uq, mla_w_ukv, mla_w_o, dil_w_qkv, dil_w_o, fox_w_qkvf,
        fox_b_f, fox_w_o,
    )
    return second_block(
        x, c_2, ctx_2, c_ctx_2, w_ada_2, b_ada_2, g_norm_mix_2, g_norm_ffn_2, w_in_2,
        da_lambda_2, da_subln_g_2, sg_ln_g_2, sg_ln_b_2, sg_w_2, sg_b_2, na_rpb_2, w_branch_2,
        w_out_2, moe_w_group_2, moe_b_group_2, moe_w_router_2, moe_b_router_2, moe_w_gate_2,
        moe_w_up_2, moe_w_down_2, g_final_2,
    )


_drawn_inputs = setup_inputs


def setup_inputs(seed=0):
    import zlib

    import numpy as np

    out = dict(_drawn_inputs(seed))
    spreads = {}
    factors = {'b_ada_2': 4.078,
     'g_norm_mix_2': 8.0,
     'g_norm_ffn_2': 8.0,
     'da_lambda_2': 8.0,
     'da_subln_g_2': 8.0,
     'sg_ln_g_2': 8.0,
     'sg_ln_b_2': 8.0,
     'sg_b_2': 8.0,
     'na_rpb_2': 8.0,
     'moe_b_group_2': 8.0,
     'moe_b_router_2': 8.0,
     'g_final_2': 2.823}
    for name, (base, spread) in spreads.items():
        noise = np.random.default_rng([zlib.crc32(name.encode()), seed]).standard_normal(out[name].shape)
        drawn = base * np.exp(spread * noise) if base else spread * noise
        out[name] = jnp.asarray(drawn.astype(out[name].dtype))
    for name, factor in factors.items():
        out[name] = (out[name] * factor).astype(out[name].dtype)
    return out
```

```python
import math
from contextlib import ExitStack

import numpy as np
import concourse.bass as bass
from concourse import mybir

F32 = mybir.dt.float32
I32 = mybir.dt.int32
U32 = mybir.dt.uint32
ALU = mybir.AluOpType
ACT = mybir.ActivationFunctionType
X = mybir.AxisListType.X

P = 128
D = 1024
KD = D // P
SEQ = 256
LT = SEQ // P
CT = 256 // P
DEPTH = 2
EPS = 1e-6
NEG = -1e30
BANK = 512

MLA_H, MLA_QR, MLA_KVR, NOPE, ROT, MLA_V = 16, 384, 256, 64, 32, 64
MLA_DK = NOPE + ROT
D_PLE = 256
D_FF = 2816
DIL_G, DIL_H = 3, 16
DILATION = (1, 4, 16)
SPAN = 128
BUCKETS, MAX_DIST = 32, 2048
BIAS_LEN = 384
FF_PIECE = 256

OFF_KA, OFF_VA, OFF_KC, OFF_VC, OFF_QA, OFF_QC, OFF_ZB, OFF_GATE = 0, 512, 1024, 1536, 2048, 2560, 3072, 4096
GRID_W, NA_COLS, NA_H, RPB_R, RPB_C = 64, 16, 8, 15, 31
RPB_W = 2 * GRID_W - 1

NE, NGRP, EPG, D_EXP = 32, 4, 8, 512
CAP = 64
MAX_TILES = LT + CT
MAX_OVER = MAX_TILES * P * 2 // CAP
RING = 6
KG = 4

C_IDENT, C_FLIP, C_CAUSAL, C_NAMASK, C_UPPER = 0, 128, 256, 512, 576
C_COS, C_SIN, C_INV, C_EIDX, C_OIDX, C_SEL, C_END = 704, 832, 960, 976, 1008, 1024, 1280
V_NG0, V_NG2, V_QN, V_KVN, V_MIX, V_FFN, V_COND, V_SGB, V_END = 0, 16, 32, 35, 37, 53, 69, 85, 93


def constants():
    c = np.zeros((P, C_END), np.float32)
    i = np.arange(P)
    c[:, C_IDENT:C_IDENT + P] = np.eye(P)
    c[:, C_FLIP:C_FLIP + P] = np.eye(P)[::-1]
    col = np.arange(2 * P)
    c[:, C_CAUSAL:C_CAUSAL + 2 * P] = np.where(P + i[:, None] - col[None, :] >= 0, 0.0, NEG)
    qc = GRID_W - 1 - i % GRID_W
    start = np.clip(qc - NA_COLS // 2, 0, GRID_W - NA_COLS)
    kc = np.arange(GRID_W)
    ok = (kc[None] >= start[:, None]) & (kc[None] < start[:, None] + NA_COLS)
    c[:, C_NAMASK:C_NAMASK + GRID_W] = np.where(ok, 0.0, NEG)
    c[:, C_UPPER:C_UPPER + P] = i[:, None] < i[None, :]
    half = 16
    inv = (np.float32(10000.0) ** (-np.arange(half, dtype=np.float32) / np.float32(half))).astype(np.float32)
    t = np.arange(SEQ)
    ar = (t // GRID_W).astype(np.float32)[:, None] * inv
    ac = (t % GRID_W).astype(np.float32)[:, None] * inv
    cos = np.cos(np.concatenate([ar, ar, ac, ac], 1)).astype(np.float32)
    sin = np.concatenate([-np.sin(ar), np.sin(ar), -np.sin(ac), np.sin(ac)], 1).astype(np.float32)
    for n in range(LT):
        c[:, C_COS + 64 * n:C_COS + 64 * n + 64] = cos[n * P:(n + 1) * P]
        c[:, C_SIN + 64 * n:C_SIN + 64 * n + 64] = sin[n * P:(n + 1) * P]
    c[:, C_INV:C_INV + half] = inv
    c[:, C_EIDX:C_EIDX + NE] = np.arange(NE)
    c[:, C_OIDX:C_OIDX + MAX_OVER] = np.arange(MAX_OVER)
    c[0, C_SEL:C_SEL + P] = 1.0
    c[1, C_SEL + P:C_SEL + 2 * P] = 1.0
    hot = np.zeros((64, DIL_G, BIAS_LEN), np.float32)
    exact = BUCKETS // 2
    for g, dil in enumerate(DILATION):
        for m in range(BIAS_LEN):
            dist = 2 * P - 1 - m
            if dist >= 0 and dist % dil == 0 and dist // dil <= SPAN:
                n = np.float32(max(dist, 1))
                large = exact + int(np.float32(np.log(n / np.float32(exact)) / np.float32(math.log(MAX_DIST / exact))
                                               * np.float32(BUCKETS - exact)))
                hot[dist if dist < exact else min(large, BUCKETS - 1), g, m] = 1.0
            else:
                hot[BUCKETS, g, m] = NEG
    return c, hot.reshape(64, DIL_G * BIAS_LEN)


class Tally:

    def __init__(self):
        self.n = {}

    def next(self, sem, by=1):
        self.n[sem.name] = self.n.get(sem.name, 0) + by
        return self.n[sem.name]

    def now(self, sem):
        return self.n.get(sem.name, 0)


class Gemm:

    def __init__(self, w, k_tiles, chunks, tiles):
        self.w, self.k_tiles, self.chunks, self.tiles = w, k_tiles, chunks, tiles
        self.groups = [(k, min(KG, k_tiles - k)) for k in range(0, k_tiles, KG)]


def columns(c0, c1, width=BANK):
    return [(c, min(width, c1 - c)) for c in range(c0, c1, width)]


def build_program(nc, I, out):
    ctx = ExitStack()
    with ctx:
        def sb(name, cols, dt=F32, rows=P):
            return ctx.enter_context(nc.sbuf_tensor(name, [rows, cols], dt))

        def sem(name):
            return ctx.enter_context(nc.semaphore(name))

        ring = sb("weight_ring", RING * KG * BANK)
        H = sb("hidden", MAX_TILES * D)
        XT = sb("x_transposed", KD * MAX_TILES * P)
        Y = sb("tokens_out", MAX_TILES * D)
        A = sb("arena", 18432)
        GT = sb("gates", 4 * D)
        C = sb("constants", C_END)
        V = sb("vectors", V_END)
        hs = sb("scaled_rows", 2 * D)
        brow = sb("broadcast_row", D)
        small = sb("small", 256)
        mcol = sb("mod_columns", 2 * KD * 4)
        ccol = sb("scale_columns", 2 * KD * 2)
        posi = sb("positions", LT, I32)
        ones = sb("ones", P)
        vrow = sb("vector_rows", 64)
        ada_row = A[:, 8192:8192 + 2 * BANK]
        pair = [ctx.enter_context(nc.psum_tensor(f"banks{2 * i}", [P, 2 * BANK], F32)) for i in range(4)]
        ps = [pair[i // 2][:, i % 2 * BANK:(i % 2 + 1) * BANK] for i in range(8)]
        route = sb("route", 64)
        route_u = sb("route_rows", 16, U32)
        route_i = sb("route_over", 32, I32)

        xs_dram = nc.dram_tensor("moe_x", [(NE + MAX_OVER) * CAP, D], F32, kind="Internal").ap()
        ys_dram = nc.dram_tensor("moe_y", [(NE + MAX_OVER) * CAP, D], F32, kind="Internal").ap()
        rel_dram = nc.dram_tensor("rel_rows", [DIL_G * DIL_H, BIAS_LEN], F32, kind="Internal").ap()
        rpb_dram = nc.dram_tensor("rpb_rows", [DEPTH, NA_H * RPB_R, RPB_W], F32, kind="Internal").ap()

        ident = C[:, C_IDENT:C_IDENT + P]
        flip = C[:, C_FLIP:C_FLIP + P]
        causal = C[:, C_CAUSAL:C_CAUSAL + 2 * P]
        upper = C[:, C_UPPER:C_UPPER + P]

        def h_tile(t):
            return H[:, t * D:(t + 1) * D]

        def y_tile(t):
            return Y[:, t * D:(t + 1) * D]

        def xT(kt, t, tiles=MAX_TILES):
            a = (kt * tiles + t) * P
            return XT[:, a:a + P]

        def xT4(g, t, tiles, n):
            return XT[:, :KD * tiles * P].rearrange("p (k t c) -> p k t c", k=KD, t=tiles)[:, 4 * g:4 * g + n, t, :]

        def rows(n):
            return hs[:, n % 2 * D:n % 2 * D + D]

        def ar(a, n):
            return A[:, a:a + n]

        def slot(c, kn, width):
            a = c % RING * KG * BANK
            return ring[:, a:a + kn * width].rearrange("p (k n) -> p k n", k=kn)

        w_in = [sem(f"weights_arrived_{i}") for i in range(RING)]
        w_used = sem("weights_used")
        acc_ready, acc_used = sem("product_ready"), sem("product_used")
        tr_ready, tr_used = sem("transpose_ready"), sem("transpose_used")
        src_ready = sem("rows_ready")
        x_ready = sem("x_ready")
        act_req, act_rep = sem("scalar_asked"), sem("scalar_answered")
        sig_ready = sem("sigmoid_ready")
        const_in, vec_in = sem("constants_in"), sem("vectors_in")
        misc_in = [sem(f"misc_in_{i}") for i in range(4)]
        misc_ask = sem("misc_asked")
        dve_step, act_step, pool_step = sem("vector_step"), sem("scalar_step"), sem("pool_step")
        s_ready, max_ready, p_ready = sem("scores_ready"), sem("max_ready"), sem("probs_ready")
        exp_ready = sem("exp_ready")
        pT_ready, pTs_ready = sem("probsT_ready"), sem("probsT_copied")
        o_ready, o_used = sem("attn_out_ready"), sem("attn_out_used")
        bias_in = [sem("bias_in_0"), sem("bias_in_1")]
        bias_ready = sem("bias_masked")
        xs_in = [sem("expert_x_in_0"), sem("expert_x_in_1")]
        ys_out = [sem("expert_y_out_0"), sem("expert_y_out_1")]
        xt_ready, xg_ready = sem("expert_xT_ready"), sem("expert_xT_copied")
        gu_ready, esig_ready, hd_ready = sem("expert_gate_up"), sem("expert_sigmoid"), sem("expert_hidden")
        hT_ready, hTs_ready = sem("expert_hiddenT"), sem("expert_hiddenT_copied")
        d_ready, y_ready = sem("expert_down"), sem("expert_y_copied")
        route_ready = sem("route_ready")
        zero_out, scatter_out = sem("zero_out"), sem("scatter_out")
        gather_in = [sem("gather_in_0"), sem("gather_in_1")]
        gated, halves_ready, summed, y_half = (sem("expert_" + n) for n in ("gated", "halves", "summed", "y_half"))
        ov = [{n: sem(f"over{i}_{n}") for n in ("x_in", "w_in", "xT", "xT_copied", "gate_up", "halves", "summed", "sigmoid", "gated", "y_half", "hidden",
                                               "hiddenT", "hiddenT_copied", "down", "y_copied", "y_out")}
              for i in range(DEPTH)]
        final_ready = sem("final_ready")
        result_out = sem("result_out")
        scratch_out = sem("scratch_out")

        g_mla_a = Gemm(I["mla_w_a"][0], KD, columns(0, MLA_QR + MLA_KVR + ROT), LT)
        g_uq = Gemm(I["mla_w_uq"][0], MLA_QR // P, columns(0, MLA_H * MLA_DK), LT)
        g_ukv = Gemm(I["mla_w_ukv"][0], MLA_KVR // P, columns(0, MLA_H * (NOPE + MLA_V)), LT)
        g_mla_o = Gemm(I["mla_w_o"][0], KD, columns(0, D), LT)
        g_ff_in = [Gemm(I["ffn_w_in"][i], KD, columns(0, 2 * D_FF),
                        LT) for i in range(DEPTH)]
        g_ff_out = [Gemm(I["ffn_w_out"][i], D_FF // P, columns(0, D), LT) for i in range(DEPTH)]
        g_ple_g = [Gemm(I["ple_w_gate"][i], KD, columns(0, D), LT) for i in range(DEPTH)]
        g_ple_p = [Gemm(I["ple_w_proj"][i], D_PLE // P, columns(0, D), LT) for i in range(DEPTH)]
        g_dil = Gemm(I["dil_w_qkv"][0], KD, columns(0, DIL_G * 3 * D), LT)
        g_dil_o = Gemm(I["dil_w_o"][0], KD, columns(0, D), LT)
        ctx_tiles = [CT, 0]
        all_tiles = [LT + CT, LT]
        g_ada = [Gemm(I["w_ada_2"][i], KD, columns(0, 6 * D), 1) for i in range(DEPTH)]
        g_kv = [Gemm(I["w_in_2"][i], KD, columns(0, OFF_QA), MAX_TILES) for i in range(DEPTH)]
        g_qz = [Gemm(I["w_in_2"][i], KD, columns(OFF_QA, OFF_GATE), all_tiles[i]) for i in range(DEPTH)]
        g_gate = [[Gemm(I["w_in_2"][i], KD, columns(OFF_GATE + b * D + n * BANK, OFF_GATE + b * D + (n + 1) * BANK),
                        all_tiles[i]) for n in range(2) for b in range(3)] for i in range(DEPTH)]
        g_branch = [[Gemm(I["w_branch_2"][i, b], BANK // P, columns(n * BANK, (n + 1) * BANK), all_tiles[i])
                     for n in range(2) for b in range(3)] for i in range(DEPTH)]
        g_out = [Gemm(I["w_out_2"][i], KD, columns(0, D), all_tiles[i]) for i in range(DEPTH)]

        STREAM = [g_mla_a, g_uq, g_ukv, g_mla_o, g_ff_in[0], g_ff_out[0], g_ple_g[0], g_ple_p[0],
                  g_dil, g_dil_o, g_ff_in[1], g_ff_out[1], g_ple_g[1], g_ple_p[1]]
        for i in range(DEPTH):
            STREAM += [g_ada[i], g_kv[i], g_qz[i]]
            for a, b in zip(g_gate[i], g_branch[i]):
                STREAM += [a, b]
            STREAM += [g_out[i], ("experts", i)]

        KV, QT, KT, QROW, KROW, AROW = 0, 4096, 8192, 12288, 15360, 4096
        DQT, DKT, DV = 0, 6144, 12288
        HT = 0
        PSIG = 0
        KAT, QAT, KCT, QCT, VA, VC, U, VV, YC = (2048 * n for n in range(9))
        YA = VV
        YT = KAT
        MERGED_SIG = VC
        SG_W = YC
        BADA = 0
        E_X, E_XG, E_HD, E_HT, E_Y, E_SG, XTOK, RT = 0, 2048, 3072, 4096, 4608, 6656, 7168, 11264
        E_UP, E_SUM, E_YR = XTOK, XTOK + 1024, XTOK + 2048
        YG = 14336
        ROUTER = YC
        TMP = 5504

        class Unit:
            def __init__(self, maps, n_keys, scale, values, width, dest, bias=None, kind="", head=0, tile=0):
                self.maps, self.n_keys, self.scale, self.values = maps, n_keys, scale, values
                self.width, self.dest, self.bias, self.kind, self.head, self.tile = width, dest, bias, kind, head, tile

        def mla_units():
            units = []
            qT = ar(QT, 4096).rearrange("p (h t) -> p h t", h=MLA_H)
            kT = ar(KT, 4096).rearrange("p (h t) -> p h t", h=MLA_H)
            kv = ar(KV, 4096).rearrange("p (t h e) -> p t h e", t=LT, h=MLA_H)
            for h in range(MLA_H):
                for t in range(LT):
                    n = (t + 1) * P
                    maps = [[(0, n, qT[0:MLA_DK, h, t * P:(t + 1) * P], kT[0:MLA_DK, h, 0:n],
                              ident, causal[:, 2 * P - n:2 * P])]]
                    values = [kv[:, k, h, NOPE:NOPE + MLA_V] for k in range(t + 1)]
                    units.append(Unit(maps, n, MLA_DK ** -0.5, values, MLA_V,
                                      y_tile(t)[:, h * MLA_V:(h + 1) * MLA_V], head=h, tile=t))
            return place(units, True)

        def dil_units():
            units = []
            qT = ar(DQT, 6144).rearrange("p (g h t) -> p g h t", g=DIL_G, h=8)
            kT = ar(DKT, 6144).rearrange("p (g h t) -> p g h t", g=DIL_G, h=8)
            vv = ar(DV, 6144).rearrange("p (t g h e) -> p t g h e", t=LT, g=DIL_G, h=DIL_H)
            for h in range(DIL_H):
                a = 64 * (h % 2)
                bias = XT[:, 2048 + h % 2 * 768:2048 + h % 2 * 768 + 768].rearrange("p (g c) -> p g c", g=DIL_G)
                for t in range(LT):
                    n = (t + 1) * P
                    maps = [[(g * n, n,
                              qT[a:a + 64, g, h // 2, t * P:(t + 1) * P], kT[a:a + 64, g, h // 2, 0:n],
                              flip, bias[:, g, 2 * P - n:2 * P]) for g in range(DIL_G)]]
                    values = [vv[:, k, g, h, :] for g in range(DIL_G) for k in range(t + 1)]
                    units.append(Unit(maps, DIL_G * n, 1.0, values, 64, y_tile(t)[:, h * 64:(h + 1) * 64],
                                      bias="dil", head=h, tile=t))
            return place(units, True)

        qaT = ar(QAT, 2048).rearrange("p (h t) -> p h t", h=4)
        kaT = ar(KAT, 2048).rearrange("p (h t) -> p h t", h=4)
        qcT = ar(QCT, 2048).rearrange("p (h t) -> p h t", h=4)
        kcT = ar(KCT, 2048).rearrange("p (h t) -> p h t", h=4)
        va = ar(VA, 2048).rearrange("p (t h e) -> p t h e", t=4, h=4)
        vc = ar(VC, 2048).rearrange("p (t h e) -> p t h e", t=4, h=8)

        def second_units(layer):
            units = []
            tiles = list(range(all_tiles[layer]))
            for h in range(4):
                for t in tiles:
                    k0 = 0 if t < LT else LT * P
                    n = MAX_TILES * P - k0
                    maps = [[(m * BANK, n, qaT[64 * m:64 * m + 64, h, t * P:(t + 1) * P],
                              kaT[64 * m:64 * m + 64, h, k0:], None, None)] for m in range(2)]
                    values = [va[:, k, h, :] for k in range(k0 // P, MAX_TILES)]
                    units.append(Unit(maps, n, 1.0, values, P,
                                      ar(YA + t * 512, 512)[:, h * P:(h + 1) * P], kind="diff", head=h, tile=t))
            for h in range(NA_H):
                a = 64 * (h % 2)
                for t in tiles:
                    k0 = 0 if t < LT else LT * P
                    n = MAX_TILES * P - k0
                    if t < LT:
                        b = Y[:, 3584 + t * 256:3584 + t * 256 + 256]
                        maps = [[(0, SEQ, qcT[a:a + 64, h // 2, t * P:(t + 1) * P], kcT[a:a + 64, h // 2, 0:SEQ],
                                  flip, b),
                                 (SEQ, SEQ, qcT[a:a + 64, h // 2, t * P:(t + 1) * P],
                                  kcT[a:a + 64, h // 2, SEQ:2 * SEQ], None, None)]]
                    else:
                        maps = [[(0, n, qcT[a:a + 64, h // 2, t * P:(t + 1) * P], kcT[a:a + 64, h // 2, k0:],
                                  None, None)]]
                    values = [vc[:, k, h, :] for k in range(k0 // P, MAX_TILES)]
                    units.append(Unit(maps, n, 1.0, values, 64,
                                      ar(YC + t * 512, 512)[:, h * 64:(h + 1) * 64],
                                      bias="na" if t < LT else None, head=h, tile=t))
            return place(units, False)

        def place(units, first):
            for u, unit in enumerate(units):
                a = (2048 if first else 0) + u % 2 * 1024
                unit.probs = Y[:, a:a + 1024]
                unit.pT = XT[:, u % 2 * 768:u % 2 * 768 + 768] if first else Y[:, 2048 + u % 2 * 768:2816 + u % 2 * 768]
            return units

        def counted(engine, value):
            if not isinstance(value, int):
                value = engine.snap(value)
                engine.wait_ge(const_in, 48)
            return value

        block = ctx.enter_context(nc.Block())

        @block.sync
        def _(sp):
            seen = Tally()
            freed = []

            def take_slot(c, i=0, per=None):
                if c >= RING:
                    s, v, k = freed[c - RING]
                    sp.wait_ge(s, counted(sp, v + (k * i if per else 0)))

            def stream(g):
                for col, width in g.chunks:
                    for n, (k0, kn) in enumerate(g.groups):
                        c = len(freed)
                        take_slot(c)
                        src = g.w[k0 * P:(k0 + kn) * P, :].rearrange("(k p) n -> p k n", p=P)[:, :, col:col + width]
                        dst = slot(c, kn, width)
                        sp.dma_start(dst, src).then_inc(w_in[c % RING], 16)
                        if n == len(g.groups) - 1:
                            freed.append((acc_ready, seen.next(acc_ready, g.tiles), 0))
                        else:
                            freed.append((w_used, seen.next(w_used), 0))

            def load_gate_up(layer, e, c, waits):
                for w, name in enumerate(("moe_w_gate_2", "moe_w_up_2")):
                    for half in range(2):
                        waits(c)
                        src = I[name][layer].rearrange("e (g k p) n -> e g p k n", p=P, k=KG)
                        sp.dma_start(slot(c, KG, BANK), src[e, half]).then_inc(w_in[c % RING], 16)
                        c += 1
                return c

            def load_down(layer, e, c, waits):
                for half in range(2):
                    waits(c)
                    src = I["moe_w_down_2"][layer].rearrange("e (k p) (g n) -> e g p k n", p=P, g=2)
                    sp.dma_start(slot(c, KG, BANK), src[e, half]).then_inc(w_in[c % RING], 16)
                    c += 1
                return c

            def experts(layer):
                c0 = len(freed)
                used0 = seen.now(w_used)
                gu0, d0 = layer * NE, layer * NE
                order = []
                for e in range(NE + 1):
                    if e < NE:
                        order += [("w", e), ("w", e), ("w", e), ("gu", e)]
                    if e > 0:
                        order += [("w", e - 1), ("d", e - 1)]
                used = used0
                for kind, e in order:
                    if kind == "w":
                        used += 1
                        freed.append((w_used, used, 8))
                    elif kind == "gu":
                        freed.append((gu_ready, gu0 + e + 1, 2))
                    else:
                        freed.append((d_ready, d0 + e + 1, 2))
                seen.next(w_used, used - used0)
                c = load_gate_up(layer, 0, c0, lambda c: take_slot(c))
                c = load_gate_up(layer, 1, c, lambda c: take_slot(c))
                c = load_down(layer, 0, c, lambda c: take_slot(c))
                c = load_gate_up(layer, 2, c, lambda c: take_slot(c))
                c = load_down(layer, 1, c, lambda c: take_slot(c))
                with sp.Fori(0, 14) as i:
                    k = load_gate_up(layer, 2 * i + 3, c, lambda c: take_slot(c, i, True))
                    k = load_down(layer, 2 * i + 2, k, lambda c: take_slot(c, i, True))
                    k = load_gate_up(layer, 2 * i + 4, k, lambda c: take_slot(c, i, True))
                    load_down(layer, 2 * i + 3, k, lambda c: take_slot(c, i, True))
                c += 14 * 12
                c = load_gate_up(layer, NE - 1, c, lambda c: take_slot(c))
                c = load_down(layer, NE - 2, c, lambda c: take_slot(c))
                load_down(layer, NE - 1, c, lambda c: take_slot(c))

                over, n_over = ov[layer], all_tiles[layer] * P * 2 // CAP
                sp.wait_ge(route_ready, layer + 1)
                some = sp.value_load(route_i[0:1, 0:1], min_val=0, max_val=n_over)
                with sp.If(some > 0):
                    sp.wait_ge(d_ready, (layer + 1) * NE)
                    with sp.Fori(0, n_over) as j:
                        e = sp.value_load(route_i[0:1, bass.ds(j + 1, 1)], min_val=0, max_val=NE - 1)
                        for n, name in enumerate(("moe_w_gate_2", "moe_w_up_2")):
                            src = I[name][layer].rearrange("e (g k p) n -> e g p k n", p=P, k=KG)
                            for half in range(2):
                                sp.dma_start(slot(2 * n + half, KG, BANK),
                                             src[bass.ds(e, 1), half][0]).then_inc(over["w_in"], 16)
                        src = I["moe_w_down_2"][layer].rearrange("e (k p) (g n) -> e g p k n", p=P, g=2)
                        for half in range(2):
                            sp.dma_start(slot(4 + half, KG, BANK),
                                         src[bass.ds(e, 1), half][0]).then_inc(over["w_in"], 16)
                        sp.wait_ge(over["down"], counted(sp, j + 1))

            sp.dma_start(C[:], I["constants"]).then_inc(const_in, 16)
            sp.dma_start(V[:], I["vectors"]).then_inc(const_in, 16)
            sp.dma_start(posi[:], I["positions"]).then_inc(const_in, 16)
            sp.dma_start(H[:, :LT * D].rearrange("p (t d) -> p t d", t=LT),
                         I["x"][0].rearrange("(t p) d -> p t d", p=P)).then_inc(vec_in, 16)
            sp.dma_start(H[:, LT * D:].rearrange("p (t d) -> p t d", t=CT),
                         I["ctx_2"][0].rearrange("(t p) d -> p t d", p=P)).then_inc(vec_in, 16)
            for g in STREAM:
                if isinstance(g, tuple):
                    experts(g[1])
                else:
                    stream(g)
            sp.wait_ge(final_ready, 1)
            for t in range(LT):
                sp.dma_start(out[0, t * P:(t + 1) * P, :], y_tile(t)).then_inc(result_out, 16)
            sp.wait_ge(result_out, 16 * LT)

        @block.tensor
        def _(pe):
            seen, made = Tally(), Tally()
            chunk = [0]

            def next_chunk(i=0, per_turn=0):
                c = chunk[0]
                pe.wait_ge(w_in[c % RING], 16 * (c // RING + 1) + 16 * (per_turn // RING) * i)
                chunk[0] += 1
                return c

            def acc_bank():
                n = made.next(acc_ready) - 1
                if n >= 4:
                    pe.wait_ge(acc_used, n - 3)
                return ps[n % 4]

            def tr_bank():
                n = made.next(tr_ready) - 1
                if n >= 4:
                    pe.wait_ge(tr_used, n - 3)
                return ps[4 + n % 4]

            def copied():
                pe.wait_ge(tr_used, made.now(tr_ready))

            def product(g, lhs, after=None, m=P):
                for n, (col, width) in enumerate(g.chunks):
                    banks = []
                    for k0, kn in g.groups:
                        c = next_chunk()
                        w = slot(c, kn, width)
                        for t in range(g.tiles):
                            if k0 == 0:
                                banks.append(acc_bank())
                            for k in range(kn):
                                last = nc.tensor.matmul(banks[t][0:m, 0:width], lhs(k0 + k, t), w[:, k, :],
                                                        start=k0 + k == 0, stop=k0 + k == g.k_tiles - 1)
                            if k0 + kn == g.k_tiles:
                                last.then_inc(acc_ready, 1)
                        if k0 + kn < g.k_tiles:
                            last.then_inc(w_used, 1)
                    if after is not None and n > 0:
                        after(n - 1, made.now(acc_ready) - g.tiles)
                if after is not None:
                    after(len(g.chunks) - 1, made.now(acc_ready))

            def transposes(srcs, m=P):
                bank = tr_bank()
                for n, src in enumerate(srcs):
                    last = nc.tensor.transpose(bank[0:m, n * P:(n + 1) * P], src, ident)
                last.then_inc(tr_ready, 1)

            def turn_rows(tiles, k_tiles=KD):
                for t in range(tiles):
                    pe.wait_ge(src_ready, seen.next(src_ready))
                    for k in range(0, k_tiles, 4):
                        transposes([rows(t)[:, j * P:(j + 1) * P] for j in range(k, min(k + 4, k_tiles))])

            def turn_chunk(tiles, wanted):
                def after(n, done):
                    if wanted(n):
                        for t in range(tiles):
                            pe.wait_ge(acc_used, done - tiles + t + 1)
                            src = hs[:, (n * tiles + t) % 4 * BANK:((n * tiles + t) % 4 + 1) * BANK]
                            transposes([src[:, j * P:(j + 1) * P] for j in range(4)])
                return after

            def two_tiles(kt, t):
                return xT(kt, t, LT)

            def attention(units, copied_bias=None):
                base = {s.name: made.now(s) for s in (s_ready, pT_ready, o_ready)}
                pe.wait_ge(acc_used, made.now(acc_ready))
                pe.wait_ge(tr_used, made.now(tr_ready))

                def scores(u):
                    unit = units[u]
                    if u >= 2:
                        pe.wait_ge(exp_ready, base[s_ready.name] + u - 1)
                    if unit.bias == "dil" and unit.tile == 0:
                        s = bias_in[unit.head % 2]
                        pe.wait_ge(s, seen.next(s, 16))
                    if unit.bias == "na":
                        pe.wait_ge(bias_ready, seen.next(bias_ready))
                    for parts in unit.maps:
                        for col, n, q, k, turn, bias in parts:
                            dst = pair[u % 2][:, col:col + n]
                            last = nc.tensor.matmul(dst, q, k, start=True, stop=bias is None)
                            if bias is not None:
                                last = nc.tensor.matmul(dst, turn, bias, start=False, stop=True)
                    last.then_inc(s_ready, 1)
                    made.next(s_ready)

                def values(u):
                    unit = units[u]
                    pe.wait_ge(pTs_ready, base[pT_ready.name] + u + 1)
                    if u >= 2:
                        pe.wait_ge(o_used, base[o_ready.name] + u - 1)
                    src = unit.pT
                    for k, v in enumerate(unit.values):
                        last = nc.tensor.matmul(ps[6 + u % 2][:, 0:unit.width], src[:, k * P:(k + 1) * P], v,
                                                start=k == 0, stop=k == len(unit.values) - 1)
                    last.then_inc(o_ready, 1)
                    made.next(o_ready)

                def turn_probs(u):
                    unit = units[u]
                    pe.wait_ge(exp_ready, base[s_ready.name] + u + 1)
                    if unit.kind == "diff":
                        pe.wait_ge(p_ready, seen.next(p_ready))
                    if u >= 1:
                        pe.wait_ge(pTs_ready, base[pT_ready.name] + u)
                    for k in range(len(unit.values)):
                        last = nc.tensor.transpose(pair[2][:, k * P:(k + 1) * P],
                                                   unit.probs[:, k * P:(k + 1) * P], ident)
                    last.then_inc(pT_ready, 1)
                    made.next(pT_ready)

                scores(0)
                for u in range(len(units)):
                    if u + 1 < len(units):
                        scores(u + 1)
                    if u >= 1:
                        values(u - 1)
                    turn_probs(u)
                values(len(units) - 1)
                pe.wait_ge(o_used, made.now(o_ready))

            def experts(layer):
                tiles = all_tiles[layer]
                pe.wait_ge(acc_used, made.now(acc_ready))
                pe.wait_ge(tr_used, made.now(tr_ready))
                b = layer * NE

                def waiting_turn(dst, src):
                    return nc.tensor.matmul(dst, src, ident[0:CAP, 0:CAP], start=True, stop=True)

                def turn_x(e, i):
                    par = e % 2
                    pe.wait_ge(xs_in[par], counted(pe, 16 * (layer * NE // 2 + e // 2 + 1) + 16 * i))
                    if e >= 1:
                        pe.wait_ge(xg_ready, b + e + 2 * i)
                    last = waiting_turn(ps[4][:, 0:CAP], A[0:CAP, E_X + par * D:E_X + par * D + P])
                    for k in range(1, KD):
                        last = nc.tensor.transpose(ps[4][:, k * CAP:(k + 1) * CAP],
                                                   A[0:CAP, E_X + par * D + k * P:E_X + par * D + (k + 1) * P],
                                                   ident[0:CAP, 0:CAP])
                    last.then_inc(xt_ready, 1)

                def halves(bank, kt):
                    return bank[kt % 2 * CAP:(kt % 2 + 1) * CAP, :]

                def gate_up(e, m, i, per_turn):
                    par = e % 2
                    if m == 0:
                        pe.wait_ge(xg_ready, b + e + 1 + 2 * i)
                        if e >= 1:
                            pe.wait_ge(summed, b + e + 2 * i)
                    for half in range(2):
                        w = slot(next_chunk(i, per_turn), KG, BANK)
                        for k in range(KG):
                            kt = half * KG + k
                            x = A[:, E_XG + par * 512 + kt * CAP:E_XG + par * 512 + (kt + 1) * CAP]
                            last = nc.tensor.matmul(halves(ps[m], kt), x, w[:, k, :], start=kt < 2, stop=kt >= KD - 2)
                        last.then_inc(gu_ready if m == 1 and half == 1 else w_used, 1)

                def turn_hidden(e, i):
                    par = e % 2
                    pe.wait_ge(hd_ready, counted(pe, b + e + 1 + 2 * i))
                    last = waiting_turn(ps[5][:, 0:CAP], A[0:CAP, E_HD + par * 512:E_HD + par * 512 + P])
                    for k in range(1, 4):
                        last = nc.tensor.transpose(ps[5][:, k * CAP:(k + 1) * CAP],
                                                   A[0:CAP, E_HD + par * 512 + k * P:E_HD + par * 512 + (k + 1) * P],
                                                   ident[0:CAP, 0:CAP])
                    last.then_inc(hT_ready, 1)

                def down(e, i, per_turn):
                    par = e % 2
                    pe.wait_ge(hTs_ready, b + e + 1 + 2 * i)
                    if e >= 1:
                        pe.wait_ge(y_ready, b + e + 2 * i)
                    for half in range(2):
                        w = slot(next_chunk(i, per_turn), KG, BANK)
                        for k in range(4):
                            h = A[:, E_HT + par * 256 + k * CAP:E_HT + par * 256 + (k + 1) * CAP]
                            last = nc.tensor.matmul(halves(ps[2 + half], k), h, w[:, k, :], start=k < 2, stop=k >= 2)
                        last.then_inc(d_ready if half == 1 else w_used, 1)

                def stage(e, i, per_turn):
                    gate_up(e, 0, i, per_turn)
                    turn_hidden(e - 1, i)
                    gate_up(e, 1, i, per_turn)
                    if e < NE - 1:
                        turn_x(e + 1, i)
                    down(e - 1, i, per_turn)

                turn_x(0, 0)
                gate_up(0, 0, 0, 0)
                gate_up(0, 1, 0, 0)
                turn_x(1, 0)
                stage(1, 0, 0)
                stage(2, 0, 0)
                c0 = chunk[0]
                with pe.Fori(0, 14) as i:
                    stage(3, i, 12)
                    stage(4, i, 12)
                chunk[0] = c0 + 14 * 12
                stage(NE - 1, 0, 0)
                turn_hidden(NE - 1, 0)
                down(NE - 1, 0, 0)
                pe.wait_ge(y_ready, b + NE)
                made.next(w_used, 4 * NE)

                over, n_over = ov[layer], tiles * P * 2 // CAP
                pe.wait_ge(route_ready, layer + 1)
                some = pe.value_load(route_i[0:1, 0:1], min_val=0, max_val=n_over)
                with pe.If(some > 0):
                    with pe.Fori(0, n_over) as j:
                        pe.wait_ge(over["x_in"], counted(pe, 16 * j + 16))
                        last = waiting_turn(ps[4][:, 0:CAP], A[0:CAP, E_X:E_X + P])
                        for k in range(1, KD):
                            last = nc.tensor.transpose(ps[4][:, k * CAP:(k + 1) * CAP],
                                                       A[0:CAP, E_X + k * P:E_X + (k + 1) * P], ident[0:CAP, 0:CAP])
                        last.then_inc(over["xT"], 1)
                        pe.wait_ge(over["xT_copied"], j + 1)
                        pe.wait_ge(over["w_in"], 96 * j + 96)
                        for m in range(2):
                            for kt in range(KD):
                                w = slot(2 * m + kt // KG, KG, BANK)
                                last = nc.tensor.matmul(halves(ps[m], kt), A[:, E_XG + kt * CAP:E_XG + (kt + 1) * CAP],
                                                        w[:, kt % KG, :], start=kt < 2, stop=kt >= KD - 2)
                        last.then_inc(over["gate_up"], 1)
                        pe.wait_ge(over["hidden"], counted(pe, j + 1))
                        last = waiting_turn(ps[5][:, 0:CAP], A[0:CAP, E_HD:E_HD + P])
                        for k in range(1, 4):
                            last = nc.tensor.transpose(ps[5][:, k * CAP:(k + 1) * CAP],
                                                       A[0:CAP, E_HD + k * P:E_HD + (k + 1) * P], ident[0:CAP, 0:CAP])
                        last.then_inc(over["hiddenT"], 1)
                        pe.wait_ge(over["hiddenT_copied"], j + 1)
                        for half in range(2):
                            w = slot(4 + half, KG, BANK)
                            for k in range(4):
                                last = nc.tensor.matmul(halves(ps[2 + half], k),
                                                        A[:, E_HT + k * CAP:E_HT + (k + 1) * CAP],
                                                        w[:, k, :], start=k < 2, stop=k >= 2)
                        last.then_inc(over["down"], 1)
                        pe.wait_ge(over["y_copied"], j + 1)

            pe.wait_ge(const_in, 48)
            pe.wait_ge(src_ready, seen.next(src_ready))
            for g in range(DIL_G):
                bank = tr_bank()
                nc.tensor.matmul(bank[0:DIL_H, 0:BIAS_LEN], A[0:64, 256 + g * DIL_H:256 + (g + 1) * DIL_H],
                                 A[0:64, 512 + g * BIAS_LEN:512 + (g + 1) * BIAS_LEN],
                                 start=True, stop=True).then_inc(tr_ready, 1)

            turn_rows(LT)
            copied()
            product(g_mla_a, two_tiles)
            turn_rows(LT, MLA_QR // P)
            turn_rows(LT, MLA_KVR // P)
            copied()
            product(g_uq, lambda kt, t: XT[:, 2048 + (kt * LT + t) * P:2048 + (kt * LT + t + 1) * P])
            product(g_ukv, lambda kt, t: XT[:, 2816 + (kt * LT + t) * P:2816 + (kt * LT + t + 1) * P])
            for place in (QROW, KROW):
                pe.wait_ge(src_ready, seen.next(src_ready))
                for t in range(LT):
                    for h in range(0, MLA_H, 4):
                        row = ar(place + t * MLA_H * MLA_DK, MLA_H * MLA_DK)
                        transposes([row[:, (h + j) * MLA_DK:(h + j + 1) * MLA_DK] for j in range(4)], m=MLA_DK)
            attention(mla_units())

            def close_block(i, g_o):
                turn_rows(LT)
                copied()
                product(g_o, two_tiles)
                turn_rows(LT)
                copied()

                def turn_hidden(n, done):
                    pe.wait_ge(acc_used, done)
                    transposes([hs[:, (n % 2 * 2 + t) * BANK + k * P:(n % 2 * 2 + t) * BANK + (k + 1) * P]
                                for k in range(2) for t in range(LT)])
                product(g_ff_in[i], two_tiles, turn_hidden)
                copied()
                product(g_ff_out[i], lambda kt, t: A[:, HT + (kt * LT + t) * P:HT + (kt * LT + t + 1) * P])
                turn_rows(LT)
                copied()
                product(g_ple_g[i], two_tiles)
                pe.wait_ge(src_ready, seen.next(src_ready))
                product(g_ple_p[i], lambda kt, t: XT[:, 2048 + kt * SEQ + t * P:2048 + kt * SEQ + (t + 1) * P])

            close_block(0, g_mla_o)

            turn_rows(LT)
            copied()
            product(g_dil, two_tiles, turn_chunk(LT, lambda n: n % 6 < 4))
            attention(dil_units())
            close_block(1, g_dil_o)

            for i in range(DEPTH):
                tiles = all_tiles[i]
                pe.wait_ge(src_ready, seen.next(src_ready))

                def spread_ada(n, done):
                    pe.wait_ge(acc_used, done)
                    row = ada_row[0:2, n % 2 * BANK:(n % 2 + 1) * BANK]
                    if n // 2 in (2, 5):
                        for j in range(2):
                            bank = tr_bank()
                            nc.tensor.matmul(bank[:, :], C[0:2, C_SEL + j * P:C_SEL + (j + 1) * P], row,
                                             start=True, stop=True).then_inc(tr_ready, 1)
                    else:
                        bank = tr_bank()
                        for j in range(4):
                            last = nc.tensor.transpose(bank[:, 2 * j:2 * j + 2], row[:, j * P:(j + 1) * P],
                                                       ident[0:2, 0:2])
                        last.then_inc(tr_ready, 1)
                product(g_ada[i], lambda kt, t: small[:, 128 + 2 * kt:130 + 2 * kt], spread_ada, m=2)
                turn_rows(MAX_TILES)
                copied()
                product(g_kv[i], xT, turn_chunk(MAX_TILES, lambda n: n in (0, 2)))
                product(g_qz[i], xT, turn_chunk(tiles, lambda n: n < 2))
                for t in range(tiles):
                    pe.wait_ge(src_ready, seen.next(src_ready))
                    bank = tr_bank()
                    for g in range(4):
                        last = nc.tensor.matmul(bank[:, g * P:(g + 1) * P], ar(SG_W + g * P, P),
                                                ar(VV + t * 512 + g * P, P), start=True, stop=True)
                    last.then_inc(tr_ready, 1)
                attention(second_units(i))
                for t in range(tiles):
                    for b in range(3):
                        pe.wait_ge(src_ready, seen.next(src_ready))
                        transposes([ar((YA, U, YC)[b] + t * 512 + j * P, P) for j in range(4)])
                copied()
                for n in range(6):
                    b = n % 3
                    product(g_gate[i][n], xT)
                    product(g_branch[i][n], lambda kt, t, b=b: ar(YT + ((b * 4 + kt) * MAX_TILES + t) * P, P))
                turn_rows(tiles)
                copied()
                product(g_out[i], xT)
                turn_rows(tiles)
                copied()
                for t in range(tiles):
                    for g in range(2):
                        transposes([xT(4 * g + j, t) for j in range(4)])
                pe.wait_ge(src_ready, seen.next(src_ready))
                bank = tr_bank()
                for t in range(tiles):
                    for kt in range(KD):
                        last = nc.tensor.matmul(bank[:, t * 36:(t + 1) * 36], xT(kt, t),
                                                ar(ROUTER + kt * 36, 36), start=kt == 0, stop=kt == KD - 1)
                last.then_inc(tr_ready, 1)
                pe.wait_ge(src_ready, seen.next(src_ready))
                bank = tr_bank()
                for t in range(tiles + 1):
                    for before in range(t):
                        last = nc.tensor.matmul(bank[:, t * NE:(t + 1) * NE], ones[:, :],
                                                ar(RT + before * NE, NE), start=before == 0,
                                                stop=t == tiles and before == t - 1)
                    if t < tiles:
                        last = nc.tensor.matmul(bank[:, t * NE:(t + 1) * NE], upper, ar(RT + t * NE, NE),
                                                start=t == 0, stop=True)
                last.then_inc(tr_ready, 1)
                experts(i)

        @block.scalar
        def _(act):
            seen, made = Tally(), Tally()
            steps = [0]
            u_base = [0]

            def link(ins):
                steps[0] += 1
                ins.then_inc(act_step, 1)
                act.wait_ge(act_step, steps[0])

            def answer(dst, src, func, scale=1.0):
                act.wait_ge(act_req, seen.next(act_req))
                nc.scalar.activation(dst, src, func, scale=scale).then_inc(act_rep, 1)

            def roots(n):
                answer(small[:, 32:32 + n], small[:, 16:16 + n], ACT.Sqrt)

            def attention(units):
                base = u_base[0]
                for u, unit in enumerate(units):
                    act.wait_ge(max_ready, base + u + 1)
                    if u >= 2:
                        act.wait_ge(pT_ready, base + u - 1)
                    for m in range(len(unit.maps)):
                        c = 2 * (u % 4) + m
                        last = nc.scalar.activation(unit.probs[:, m * BANK:m * BANK + unit.n_keys],
                                                    pair[u % 2][:, m * BANK:m * BANK + unit.n_keys], ACT.Exp,
                                                    bias=small[:, 64 + c:65 + c], scale=unit.scale,
                                                    accum_out=small[:, 80 + c:81 + c])
                    last.then_inc(exp_ready, 1)
                u_base[0] += len(units)

            def close_block():
                roots(LT)
                roots(LT)
                for n in range(D_FF // FF_PIECE * LT):
                    a = seen.next(acc_ready)
                    act.wait_ge(acc_ready, a)
                    c = (a - 1) % 4
                    nc.scalar.activation(ada_row[:, c * FF_PIECE:(c + 1) * FF_PIECE], ps[c][:, 0:FF_PIECE],
                                         ACT.Sigmoid).then_inc(sig_ready, 1)
                seen.next(acc_ready, 2 * LT)
                roots(LT)
                for n in range(2 * LT):
                    answer(ar(PSIG + n * BANK, BANK), ar(PSIG + n * BANK, BANK), ACT.Sigmoid)
                seen.next(acc_ready, 4 * LT)

            roots(LT)
            seen.next(acc_ready, 2 * LT)
            roots(LT)
            roots(LT)
            seen.next(acc_ready, (3 + 4) * LT)
            answer(ar(TMP + 64, 64), ar(TMP + 64, 64), ACT.Sin)
            act.wait_ge(zero_out, 32)
            attention(mla_units())
            seen.next(acc_ready, 2 * LT)
            close_block()
            roots(LT)
            seen.next(acc_ready, 18 * LT)
            attention(dil_units())
            seen.next(acc_ready, 2 * LT)
            close_block()

            def expert_halves(layer, e, i):
                act.wait_ge(gu_ready, layer * NE + e + 1 + 2 * i)
                if e >= 1:
                    act.wait_ge(summed, layer * NE + e + 2 * i)
                nc.scalar.activation(A[0:CAP, E_UP:E_UP + 2 * BANK], pair[0][CAP:2 * CAP, :],
                                     ACT.Copy).then_inc(halves_ready, 1)

            def expert_sigmoid(layer, e, i):
                act.wait_ge(summed, layer * NE + e + 1 + 2 * i)
                if e >= 1:
                    act.wait_ge(hd_ready, layer * NE + e + 2 * i)
                nc.scalar.activation(A[0:CAP, E_SG:E_SG + 512], A[0:CAP, E_SUM:E_SUM + 512],
                                     ACT.Sigmoid).then_inc(esig_ready, 1)

            def expert_y(layer, e, i):
                act.wait_ge(d_ready, layer * NE + e + 1 + 2 * i)
                if e >= 1:
                    act.wait_ge(y_ready, layer * NE + e + 2 * i)
                nc.scalar.activation(A[0:CAP, E_YR:E_YR + D], pair[1][CAP:2 * CAP, :],
                                     ACT.Copy).then_inc(y_half, 1)

            def expert_stage(layer, e, i):
                expert_halves(layer, e, i)
                expert_sigmoid(layer, e, i)
                expert_y(layer, e - 1, i)

            for layer in range(DEPTH):
                tiles = all_tiles[layer]
                if layer == 0:
                    answer(small[:, 144:160], V[:, V_COND:V_COND + 16], ACT.Sigmoid)
                answer(small[:, 98:100], small[:, 98:100], ACT.Exp)
                roots(MAX_TILES)
                for n in range(2 * tiles):
                    answer(rows(1)[:, 0:BANK], rows(1)[:, 0:BANK], ACT.Sigmoid)
                roots(tiles)
                attention(second_units(layer))
                roots(4 * tiles)
                for n in range(6):
                    for t in range(tiles):
                        answer(ar(MERGED_SIG + t * 512, BANK), ar(MERGED_SIG + t * 512, BANK), ACT.Sigmoid)
                roots(tiles)
                answer(ar(RT + 128, tiles * 4), ar(RT + 128, tiles * 4), ACT.Exp)
                answer(small[:, 104:104 + tiles], small[:, 104:104 + tiles], ACT.Exp)
                expert_halves(layer, 0, 0)
                expert_sigmoid(layer, 0, 0)
                expert_stage(layer, 1, 0)
                expert_stage(layer, 2, 0)
                with act.Fori(0, 14) as i:
                    expert_stage(layer, 3, i)
                    expert_stage(layer, 4, i)
                expert_stage(layer, NE - 1, 0)
                expert_y(layer, NE - 1, 0)
                over, n_over = ov[layer], tiles * P * 2 // CAP
                act.wait_ge(route_ready, layer + 1)
                some = act.value_load(route_i[0:1, 0:1], min_val=0, max_val=n_over)
                with act.If(some > 0):
                    with act.Fori(0, n_over) as j:
                        act.wait_ge(over["gate_up"], j + 1)
                        nc.scalar.activation(A[0:CAP, E_UP:E_UP + 2 * BANK], pair[0][CAP:2 * CAP, :],
                                             ACT.Copy).then_inc(over["halves"], 1)
                        act.wait_ge(over["summed"], j + 1)
                        nc.scalar.activation(A[0:CAP, E_SG:E_SG + 512], A[0:CAP, E_SUM:E_SUM + 512],
                                             ACT.Sigmoid).then_inc(over["sigmoid"], 1)
                        act.wait_ge(over["down"], j + 1)
                        nc.scalar.activation(A[0:CAP, E_YR:E_YR + D], pair[1][CAP:2 * CAP, :],
                                             ACT.Copy).then_inc(over["y_half"], 1)
                        act.wait_ge(over["y_out"], 16 * j + 16)
            roots(LT)

        @block.gpsimd
        def _(pool):
            seen = Tally()
            u_base, loads = [0], [2]

            def load(dst, src):
                pool.wait_ge(misc_ask, seen.next(misc_ask))
                nc.gpsimd.dma_start(dst, src).then_inc(misc_in[loads[0] % 4], 16)
                loads[0] += 1

            def row(src, width=D, at=0):
                load(brow[:, at:at + width], src.partition_broadcast(P))

            pool.wait_ge(misc_ask, seen.next(misc_ask))
            nc.gpsimd.dma_start(A[0:BUCKETS, 256:256 + DIL_G * DIL_H], I["rel_bias"]).then_inc(misc_in[0], 16)
            nc.gpsimd.dma_start(A[0:64, 512:512 + DIL_G * BIAS_LEN], I["hot"]).then_inc(misc_in[1], 16)
            for l in range(DEPTH):
                nc.gpsimd.dma_start(A[0:NA_H * RPB_R, l * P + 48:l * P + 48 + RPB_C],
                                    I["na_rpb_2"][l].rearrange("h a c -> (h a) c")).then_inc(pool_step, 16)
            pool.wait_ge(pool_step, 32)
            for l in range(DEPTH):
                nc.gpsimd.dma_start(rpb_dram[l], A[0:NA_H * RPB_R, l * P:l * P + RPB_W]).then_inc(scratch_out, 16)
            nc.gpsimd.dma_start(xs_dram.rearrange("(r p) d -> p r d", p=P),
                                Y[:, 2048:2048 + D].unsqueeze(1).broadcast_to([P, xs_dram.shape[0] // P, D])
                                ).then_inc(zero_out, 16)
            nc.gpsimd.dma_start(ys_dram[NE * CAP:, :].rearrange("(r p) d -> p r d", p=P),
                                Y[:, 2048:2048 + D].unsqueeze(1).broadcast_to([P, MAX_OVER * CAP // P, D])
                                ).then_inc(zero_out, 16)
            pool.wait_ge(misc_ask, seen.next(misc_ask))
            for g in range(DIL_G):
                nc.gpsimd.dma_start(rel_dram[g * DIL_H:(g + 1) * DIL_H, :],
                                    A[0:DIL_H, 3072 + g * BIAS_LEN:3072 + (g + 1) * BIAS_LEN]).then_inc(scratch_out, 16)
            pool.wait_ge(scratch_out, 16 * (DEPTH + DIL_G))

            def close_block(i):
                row(I["norm_g"][i, 3])
                load(XT[:, 2048:2560].rearrange("p (k t) -> p k t", k=2), I["p_t"][i].rearrange("(k p) t -> p k t", p=P))

            u_base[0] += 2 * MLA_H
            row(I["norm_g"][0, 1])
            close_block(0)
            row(I["norm_g"][1, 1])
            for h in range(DIL_H):
                if h >= 2:
                    pool.wait_ge(s_ready, u_base[0] + 2 * (h - 1))
                else:
                    pool.wait_ge(misc_ask, seen.next(misc_ask))
                dst = XT[:, 2048 + h % 2 * 768:2048 + h % 2 * 768 + 768].rearrange("p (g c) -> p g c", g=DIL_G)
                src = bass.AP(tensor=rel_dram.tensor, offset=h * BIAS_LEN,
                              ap=[[1, P], [DIL_H * BIAS_LEN, DIL_G], [1, 2 * P]])
                nc.gpsimd.dma_start(dst, src).then_inc(bias_in[h % 2], 16)
            u_base[0] += 2 * DIL_H
            close_block(1)

            for layer in range(DEPTH):
                tiles = all_tiles[layer]
                load(A[0:2, 0:6 * D], I["b_ada_2"][layer].partition_broadcast(2))
                row(I["da_lambda_2"][layer].rearrange("a b -> (a b)"), 256)
                row(I["sg_ln_g_2"][layer], 512)
                row(I["sg_ln_b_2"][layer], 512, 512)
                load(ar(SG_W, 512).rearrange("q (g p) -> q g p", g=4), I["sg_wt"][layer].rearrange("g q p -> q g p"))
                n_diff = 4 * tiles
                for h in range(NA_H):
                    for t in range(LT):
                        if h == 0:
                            pool.wait_ge(misc_ask, seen.next(misc_ask))
                        else:
                            pool.wait_ge(s_ready, u_base[0] + n_diff + (h - 1) * tiles + t + 1)
                        for half in range(2):
                            dst = Y[half * 64:(half + 1) * 64, 3584 + t * 256:3840 + t * 256]
                            src = bass.AP(tensor=rpb_dram.tensor,
                                          offset=((layer * NA_H + h) * RPB_R + 6 - 2 * t + half) * RPB_W,
                                          ap=[[1, 64], [RPB_W, 4], [1, 64]])
                            nc.gpsimd.dma_start(dst.rearrange("p (r c) -> p r c", r=4), src).then_inc(bias_in[t], 16)
                u_base[0] += n_diff + NA_H * tiles
                row(I["da_subln_g_2"][layer], P)
                load(ar(ROUTER, 36 * KD).rearrange("p (k n) -> p k n", k=KD), I["router_w"][layer].rearrange("(k p) n -> p k n", p=P))
                load(vrow[:, 0:36], I["router_b"][layer].partition_broadcast(P))
                pool.wait_ge(route_ready, layer + 1)
                if layer == 0:
                    pool.wait_ge(zero_out, 32)
                for t in range(tiles):
                    for k in range(2):
                        c = k * MAX_TILES + t
                        nc.gpsimd.indirect_dma_start(
                            out=xs_dram[:, :], out_offset=bass.IndirectOffsetOnAxis(ap=route_u[:, c:c + 1], axis=0),
                            in_=ar(XTOK + t * D, D), in_offset=None).then_inc(scatter_out, 16)
                pool.wait_ge(scatter_out, 16 * 2 * sum(all_tiles[:layer + 1]))
                b = layer * NE

                def fetch(e, i):
                    par = e % 2
                    if e >= 2:
                        pool.wait_ge(xt_ready, counted(pool, b + e - 1 + 2 * i))
                    nc.gpsimd.dma_start(A[0:CAP, E_X + par * D:E_X + (par + 1) * D],
                                        xs_dram.rearrange("(b s) d -> b s d", s=CAP)[e + 2 * i]
                                        if isinstance(i, int) else
                                        xs_dram.rearrange("(b s) d -> b s d", s=CAP)[bass.ds(2 * i + e, 1)][0]
                                        ).then_inc(xs_in[par], 16)

                def store(e, i):
                    par = e % 2
                    pool.wait_ge(y_ready, counted(pool, b + e + 1 + 2 * i))
                    nc.gpsimd.dma_start(ys_dram.rearrange("(b s) d -> b s d", s=CAP)[e + 2 * i]
                                        if isinstance(i, int) else
                                        ys_dram.rearrange("(b s) d -> b s d", s=CAP)[bass.ds(2 * i + e, 1)][0],
                                        A[0:CAP, E_Y + par * D:E_Y + (par + 1) * D]).then_inc(ys_out[par], 16)

                fetch(0, 0)
                fetch(1, 0)
                for e in (1, 2):
                    fetch(e + 1, 0)
                    store(e - 1, 0)
                with pool.Fori(0, 14) as i:
                    for e in (3, 4):
                        fetch(e + 1, i)
                        store(e - 1, i)
                store(NE - 2, 0)
                store(NE - 1, 0)
                for par in range(2):
                    pool.wait_ge(ys_out[par], 16 * (layer + 1) * NE // 2)
                over, n_over = ov[layer], tiles * P * 2 // CAP
                some = pool.value_load(route_i[0:1, 0:1], min_val=0, max_val=n_over)
                with pool.If(some > 0):
                    with pool.Fori(0, n_over) as j:
                        nc.gpsimd.dma_start(A[0:CAP, E_X:E_X + D],
                                            xs_dram.rearrange("(b s) d -> b s d", s=CAP)[bass.ds(j + NE, 1)][0]
                                            ).then_inc(over["x_in"], 16)
                        pool.wait_ge(over["y_copied"], counted(pool, j + 1))
                        nc.gpsimd.dma_start(ys_dram[bass.ds(j * CAP + NE * CAP, CAP), :],
                                            A[0:CAP, E_Y:E_Y + D]).then_inc(over["y_out"], 16)
                        pool.wait_ge(over["y_out"], counted(pool, 16 * j + 16))
                for t in range(tiles):
                    if t >= 2:
                        pool.wait_ge(misc_ask, seen.next(misc_ask))
                    for k in range(2):
                        c = k * MAX_TILES + t
                        nc.gpsimd.indirect_dma_start(
                            out=ar(YG + (t % 2 * 2 + k) * D, D), out_offset=None, in_=ys_dram[:, :],
                            in_offset=bass.IndirectOffsetOnAxis(ap=route_u[:, c:c + 1], axis=0)
                        ).then_inc(gather_in[t % 2], 16)
            row(I["g_final_2"])

        @block.vector
        def _(dve):
            seen, made = Tally(), Tally()
            tt, ts, stt = nc.vector.tensor_tensor, nc.vector.tensor_scalar, nc.vector.scalar_tensor_tensor
            copy, red = nc.vector.tensor_copy, nc.vector.tensor_reduce

            def v(ins, signal=dve_step):
                ins.then_inc(signal, 1)
                dve.wait_ge(signal, made.next(signal))

            def say(signal):
                v(nc.vector.memset(small[:, 255:256], 0.0), signal)

            def product_bank():
                n = seen.next(acc_ready)
                dve.wait_ge(acc_ready, n)
                return ps[(n - 1) % 4]

            def turned_bank():
                n = seen.next(tr_ready)
                dve.wait_ge(tr_ready, n)
                return ps[4 + (n - 1) % 4]

            loads = [0]

            def loaded(n=1):
                for _ in range(n):
                    s = misc_in[loads[0] % 4]
                    dve.wait_ge(s, seen.next(s, 16))
                    loads[0] += 1

            def answered():
                dve.wait_ge(act_rep, seen.next(act_rep))

            def answered_all(n):
                dve.wait_ge(act_rep, seen.next(act_rep, n))

            def spread(col, n, width):
                return col.unsqueeze(2).broadcast_to([P, n, width])

            def square_sum(src, col, width):
                v(nc.vector.tensor_tensor_reduce(out=rows(1)[:, :width], in0=src, in1=src, scale=1.0, scalar=0.0,
                                                 op0=ALU.mult, op1=ALU.add, accum_out=small[:, col:col + 1]))

            def rstd(n, width):
                v(ts(small[:, 16:16 + n], small[:, 0:n], 1.0 / width, EPS, ALU.mult, ALU.add), act_req)
                answered()
                v(nc.vector.reciprocal(small[:, 48:48 + n], small[:, 32:32 + n]))

            def copy_turned(dst):
                bank = turned_bank()
                n = dst.shape[1]
                v(copy(dst, bank[0:dst.shape[0], 0:n * P].rearrange("p (k c) -> p k c", k=n)), tr_used)

            def turn(tiles, src, dst, k_tiles=KD, scaled=True, gain=None, shift=None):
                width = k_tiles * P
                for step in range(tiles + 1):
                    if step < tiles:
                        r = rows(step)[:, :width]
                        if scaled:
                            v(ts(r, src(step), small[:, 48 + step:49 + step], None, ALU.mult), src_ready)
                        else:
                            v(copy(r, src(step)), src_ready)
                    if step == 0:
                        continue
                    t = step - 1
                    for g in range(0, k_tiles, 4):
                        n = min(4, k_tiles - g)
                        d = dst(g // 4, t, n)
                        if gain is None:
                            copy_turned(d)
                            continue
                        bank = turned_bank()[:, 0:n * P].rearrange("p (k c) -> p k c", k=n)
                        done = dve_step if shift is not None else tr_used
                        v(tt(d, bank, spread(gain(t)[:, g:g + n], n, P), ALU.mult), done)
                        if shift is not None:
                            v(tt(d, d, spread(shift(t)[:, g:g + n], n, P), ALU.add), tr_used)

            def norm_turn(tiles, src, dst, k_tiles=KD, gain=None, shift=None):
                for t in range(tiles):
                    square_sum(src(t), t, k_tiles * P)
                rstd(tiles, k_tiles * P)
                turn(tiles, src, dst, k_tiles, True, gain, shift)

            def x2(g, t, n):
                return xT4(g, t, LT, n)

            def x4(g, t, n):
                return xT4(g, t, MAX_TILES, n)

            def attention(units):
                def mask_bias(u):
                    unit = units[u]
                    if unit.bias == "na":
                        dve.wait_ge(bias_in[unit.tile], seen.next(bias_in[unit.tile], 32))
                        b = Y[:, 3584 + unit.tile * 256:3840 + unit.tile * 256].rearrange("p (r c) -> p r c", r=4)
                        m = C[:, C_NAMASK:C_NAMASK + GRID_W].unsqueeze(1).broadcast_to([P, 4, GRID_W])
                        v(tt(b, b, m, ALU.add), bias_ready)

                def row_max(u):
                    unit = units[u]
                    dve.wait_ge(s_ready, seen.next(s_ready))
                    for m in range(len(unit.maps)):
                        c = 64 + 2 * (u % 4) + m
                        last = m == len(unit.maps) - 1
                        scores = pair[u % 2][:, m * BANK:m * BANK + unit.n_keys]
                        v(red(small[:, c:c + 1], scores, X, ALU.max, negate=True),
                          max_ready if last and unit.scale == 1.0 else dve_step)
                        if unit.scale != 1.0:
                            v(ts(small[:, c:c + 1], small[:, c:c + 1], unit.scale, None, ALU.mult), max_ready)

                def combine(u):
                    unit = units[u]
                    dve.wait_ge(exp_ready, seen.next(exp_ready))
                    c = 80 + 2 * (u % 4)
                    n = len(unit.maps)
                    v(nc.vector.reciprocal(small[:, c:c + n], small[:, c:c + n]))
                    if unit.kind == "diff":
                        n = unit.n_keys
                        v(tt(small[:, c + 1:c + 2], small[:, c + 1:c + 2], small[:, 96:97], ALU.mult))
                        v(ts(unit.probs[:, BANK:BANK + n], unit.probs[:, BANK:BANK + n], small[:, c + 1:c + 2], None,
                             ALU.mult))
                        v(stt(unit.probs[:, 0:n], unit.probs[:, 0:n], small[:, c:c + 1],
                              unit.probs[:, BANK:BANK + n], ALU.mult, ALU.add), p_ready)

                def copy_probs(u):
                    unit = units[u]
                    dve.wait_ge(pT_ready, seen.next(pT_ready))
                    if u >= 2:
                        dve.wait_ge(o_ready, o_base + u - 1)
                    n = len(unit.values) * P
                    v(copy(unit.pT[:, 0:n], pair[2][:, 0:n]), pTs_ready)

                def finish(u):
                    unit = units[u]
                    dve.wait_ge(o_ready, seen.next(o_ready))
                    src = ps[6 + u % 2][:, 0:unit.width]
                    if unit.kind == "diff":
                        v(copy(unit.dest, src), o_used)
                    else:
                        c = 80 + 2 * (u % 4)
                        v(ts(unit.dest, src, small[:, c:c + 1], None, ALU.mult), o_used)

                o_base = seen.now(o_ready)
                mask_bias(0)
                row_max(0)
                for u in range(len(units)):
                    if u + 1 < len(units):
                        mask_bias(u + 1)
                        row_max(u + 1)
                    if u >= 1:
                        finish(u - 1)
                    combine(u)
                    copy_probs(u)
                finish(len(units) - 1)

            def copy_product(g, dst):
                for n, (_, width) in enumerate(g.chunks):
                    for t in range(g.tiles):
                        bank = product_bank()
                        v(copy(dst(n, t), bank[:, 0:width]), acc_used)

            def residual():
                for t in range(LT):
                    square_sum(y_tile(t), t, D)
                rstd(LT, D)
                loaded()
                for t in range(LT):
                    v(stt(rows(0), y_tile(t), small[:, 48 + t:49 + t], brow[:, :], ALU.mult, ALU.mult))
                    v(tt(h_tile(t), h_tile(t), rows(0), ALU.add))

            def close_block(i, g_o):
                turn(LT, y_tile, x2, scaled=False)
                copy_product(g_o, lambda n, t: y_tile(t)[:, n * BANK:(n + 1) * BANK])
                residual()
                say(misc_ask)
                say(misc_ask)
                norm_turn(LT, h_tile, x2, gain=lambda t: V[:, V_NG2 + i * 8:V_NG2 + i * 8 + 8])
                n_pieces = D_FF // FF_PIECE
                for n in range(n_pieces + 1):
                    if n < n_pieces:
                        for t in range(LT):
                            c = seen.now(acc_ready) % 4
                            bank = product_bank()
                            dve.wait_ge(sig_ready, seen.next(sig_ready))
                            r = hs[:, (n % 2 * 2 + t) * BANK:]
                            sg = ada_row[:, c * FF_PIECE:(c + 1) * FF_PIECE]
                            v(tt(r[:, FF_PIECE:2 * FF_PIECE], bank[:, 0:FF_PIECE], sg, ALU.mult))
                            v(tt(r[:, 0:FF_PIECE], bank[:, FF_PIECE:2 * FF_PIECE], r[:, FF_PIECE:2 * FF_PIECE],
                                 ALU.mult), acc_used)
                    if n > 0:
                        v(copy(A[:, HT + (n - 1) * 512:HT + n * 512], turned_bank()[:, :]), tr_used)
                copy_product(g_ff_out[i], lambda n, t: y_tile(t)[:, n * BANK:(n + 1) * BANK])
                residual()
                if i == 0:
                    say(misc_ask)
                turn(LT, h_tile, x2, scaled=False)
                for n in range(2):
                    for t in range(LT):
                        bank = product_bank()
                        v(copy(ar(PSIG + (n * LT + t) * BANK, BANK), bank[:, :]), acc_used)
                        say(act_req)
                loaded()
                say(src_ready)
                answered_all(2 * LT)
                for n in range(2):
                    for t in range(LT):
                        bank = product_bank()
                        v(tt(rows(0)[:, 0:BANK], bank[:, :], ar(PSIG + (n * LT + t) * BANK, BANK), ALU.mult), acc_used)
                        part = h_tile(t)[:, n * BANK:(n + 1) * BANK]
                        v(tt(part, part, rows(0)[:, 0:BANK], ALU.add))

            v(nc.vector.memset(A[:, 0:256], 0.0))
            v(nc.vector.memset(A[0:64, 256:256 + DIL_G * DIL_H], 0.0))
            v(nc.vector.memset(A[BUCKETS:BUCKETS + 1, 256:256 + DIL_G * DIL_H], 1.0))
            v(nc.vector.memset(ones[:, :], 1.0))
            v(nc.vector.memset(Y[:, 2048:2048 + D], 0.0), misc_ask)
            loaded(2)
            say(src_ready)
            for g in range(DIL_G):
                v(copy(A[0:DIL_H, 3072 + g * BIAS_LEN:3072 + (g + 1) * BIAS_LEN], turned_bank()[0:DIL_H, 0:BIAS_LEN]),
                  tr_used)
            say(misc_ask)
            say(misc_ask)

            dve.wait_ge(const_in, 48)
            dve.wait_ge(vec_in, 32)
            norm_turn(LT, h_tile, x2, gain=lambda t: V[:, V_NG0:V_NG0 + 8])
            dve.wait_ge(scratch_out, 16 * (DEPTH + DIL_G))
            wide = MLA_QR + MLA_KVR + ROT
            copy_product(g_mla_a, lambda n, t: ar(AROW + t * wide + n * BANK, min(BANK, wide - n * BANK)))
            norm_turn(LT, lambda t: ar(AROW + t * wide, MLA_QR),
                      lambda g, t, n: XT[:, 2048:2816].rearrange("p (k t c) -> p k t c", k=3, t=LT)[:, 0:3, t, :],
                      3, gain=lambda t: V[:, V_QN:V_QN + 3])
            norm_turn(LT, lambda t: ar(AROW + t * wide + MLA_QR, MLA_KVR),
                      lambda g, t, n: XT[:, 2816:3328].rearrange("p (k t c) -> p k t c", k=2, t=LT)[:, 0:2, t, :],
                      2, gain=lambda t: V[:, V_KVN:V_KVN + 2])
            copy_product(g_uq, lambda n, t: ar(QROW + t * 1536 + n * BANK, BANK))
            copy_product(g_ukv, lambda n, t: ar(KV + t * 2048 + n * BANK, BANK))
            pos, ang, n_turns = ar(TMP, 2), ar(TMP + 64, 32), ar(TMP + 32, 32)
            v(copy(pos, posi[:, :]))
            for t in range(LT):
                v(ts(ang[:, t * 16:(t + 1) * 16], C[:, C_INV:C_INV + 16], pos[:, t:t + 1], None, ALU.mult))
            whole = 1.5 * 2.0 ** 23
            v(ts(n_turns, ang, 1.0 / (2 * math.pi), None, ALU.mult))
            v(ts(n_turns, n_turns, whole, None, ALU.add))
            v(ts(n_turns, n_turns, whole, None, ALU.subtract))
            c1 = 6.28125
            c2 = float(np.float32(np.float32((2 * math.pi - c1) * 2 ** 20).astype(np.int32)) * 2.0 ** -20)
            c3 = 2 * math.pi - c1 - c2
            for part in (c1, c2, c3):
                v(stt(ang, n_turns, -part, ang, ALU.mult, ALU.add))
            cosa = ar(TMP + 96, 32)
            v(ts(cosa, ang, math.pi / 2, None, ALU.add))
            v(ts(n_turns, cosa, math.pi, -2 * math.pi, ALU.is_gt, ALU.mult))
            v(tt(cosa, cosa, n_turns, ALU.add))
            pi = 3.1415925
            v(ts(ar(TMP + 64, 64), ar(TMP + 64, 64), pi, -pi, ALU.min, ALU.max), act_req)
            answered()
            for t in range(LT):
                sin = ang[:, t * 16:(t + 1) * 16]
                cos = cosa[:, t * 16:(t + 1) * 16]
                q = ar(QROW + t * 1536, 1536).rearrange("p (h e) -> p h e", h=MLA_H)
                s3, c3_ = (a.unsqueeze(1).broadcast_to([P, MLA_H, 16]) for a in (sin, cos))
                t1, t2 = (rows(0)[:, n * 256:(n + 1) * 256].rearrange("p (h e) -> p h e", h=MLA_H) for n in range(2))
                x1, x2_ = q[:, :, NOPE:NOPE + 16], q[:, :, NOPE + 16:MLA_DK]
                v(tt(t1, x1, c3_, ALU.mult))
                v(tt(t2, x2_, s3, ALU.mult))
                v(tt(t1, t1, t2, ALU.subtract))
                v(tt(t2, x1, s3, ALU.mult))
                v(copy(x1, t1))
                v(tt(t1, x2_, c3_, ALU.mult))
                v(tt(x2_, t1, t2, ALU.add))
                a = ar(AROW + t * wide + MLA_QR + MLA_KVR, ROT)
                r = rows(1)
                v(tt(r[:, 0:16], a[:, 0:16], cos, ALU.mult))
                v(tt(r[:, 16:32], a[:, 16:32], sin, ALU.mult))
                v(tt(r[:, 32:48], r[:, 0:16], r[:, 16:32], ALU.subtract))
                v(tt(r[:, 0:16], a[:, 16:32], cos, ALU.mult))
                v(tt(r[:, 16:32], a[:, 0:16], sin, ALU.mult))
                v(tt(r[:, 48:64], r[:, 0:16], r[:, 16:32], ALU.add))
                k = ar(KROW + t * 1536, 1536).rearrange("p (h e) -> p h e", h=MLA_H)
                kv = ar(KV + t * 2048, 2048).rearrange("p (h e) -> p h e", h=MLA_H)
                v(copy(k[:, :, 0:NOPE], kv[:, :, 0:NOPE]))
                v(copy(k[:, :, NOPE:MLA_DK], r[:, 32:64].unsqueeze(1).broadcast_to([P, MLA_H, ROT])))
            say(src_ready)
            say(src_ready)
            for place in (QT, KT):
                for t in range(LT):
                    for h in range(0, MLA_H, 4):
                        dst = ar(place, 4096).rearrange("p (h t) -> p h t", h=MLA_H)
                        copy_turned(dst[0:MLA_DK, h:h + 4, t * P:(t + 1) * P])
            attention(mla_units())
            close_block(0, g_mla_o)

            norm_turn(LT, h_tile, x2, gain=lambda t: V[:, V_NG0 + 8:V_NG0 + 16])

            def dil_copy(n):
                g, part, half = n // 6, n % 6 // 2, n % 2
                if part < 2:
                    for t in range(LT):
                        dst = ar((DQT, DKT)[part], 6144).rearrange("p (g h t) -> p g h t", g=DIL_G, h=8)
                        copy_turned(dst[:, g, half * 4:half * 4 + 4, t * P:(t + 1) * P])
            for n in range(19):
                if n < 18:
                    g, part, half = n // 6, n % 6 // 2, n % 2
                    for t in range(LT):
                        bank = product_bank()
                        if part == 2:
                            v(copy(ar(DV + t * 3072 + g * D + half * BANK, BANK), bank[:, :]), acc_used)
                        else:
                            c = (n * LT + t) % 4 * BANK
                            v(ts(hs[:, c:c + BANK], bank[:, :], 0.125 if part == 0 else 1.0, None, ALU.mult), acc_used)
                if n > 0:
                    dil_copy(n - 1)
            say(misc_ask)
            say(misc_ask)
            attention(dil_units())
            for par in range(2):
                seen.next(bias_in[par], 16 * DIL_H // 2)
            close_block(1, g_dil_o)

            def rope_axial(dst, bank, t, scale):
                x = bank.rearrange("p (m a b e) -> p m a b e", m=8, a=2, b=2)
                r = rows(t % 2)
                t1 = brow[:, 0:512]
                t2 = brow[:, 512:1024].rearrange("p (m a b e) -> p m a b e", m=8, a=2, b=2)
                cos = C[:, C_COS + 64 * t:C_COS + 64 * t + 64].unsqueeze(1).broadcast_to([P, 8, 64])
                sin = C[:, C_SIN + 64 * t:C_SIN + 64 * t + 64].rearrange("p (a b e) -> p a b e", a=2, b=2)
                v(tt(t1.rearrange("p (m e) -> p m e", m=8), bank.rearrange("p (m e) -> p m e", m=8), cos, ALU.mult))
                for a in range(2):
                    for b in range(2):
                        s = sin[:, a, b, :].unsqueeze(1).broadcast_to([P, 8, 16])
                        v(tt(t2[:, :, a, b, :], x[:, :, a, 1 - b, :], s, ALU.mult))
                if scale == 1.0:
                    v(tt(dst, t1, brow[:, 512:1024], ALU.add), acc_used)
                else:
                    v(tt(t1, t1, brow[:, 512:1024], ALU.add))
                    v(ts(dst, t1, scale, None, ALU.mult), acc_used)

            def first_max(dst, src, iota, tiles, n, tmp, col):
                mx = small[:, col:col + tiles]
                v(red(mx, src, X, ALU.max))
                v(tt(tmp, src, spread(mx, tiles, n), ALU.is_equal))
                v(tt(tmp, tmp, iota, ALU.mult))
                mn = small[:, 160:160 + tiles]
                v(red(mn, tmp, X, ALU.min))
                v(tt(dst, spread(mn, tiles, n), iota, ALU.is_equal))

            def experts(layer):
                b = layer * NE

                def turned(e, i):
                    dve.wait_ge(xt_ready, b + e + 1 + 2 * i)
                    if e >= 2:
                        dve.wait_ge(gu_ready, b + e - 1 + 2 * i)
                    copy(A[:, E_XG + e % 2 * 512:E_XG + e % 2 * 512 + 512], ps[4][:, :]).then_inc(xg_ready, 1)

                def sums(e, i):
                    dve.wait_ge(halves_ready, b + e + 1 + 2 * i)
                    if e >= 1:
                        dve.wait_ge(hd_ready, b + e + 2 * i)
                    tt(A[0:CAP, E_SUM:E_SUM + 2 * BANK], pair[0][0:CAP, :], A[0:CAP, E_UP:E_UP + 2 * BANK],
                       ALU.add).then_inc(summed, 1)

                def hidden(e, i):
                    hd = A[0:CAP, E_HD + e % 2 * 512:E_HD + e % 2 * 512 + 512]
                    dve.wait_ge(summed, b + e + 1 + 2 * i)
                    dve.wait_ge(esig_ready, b + e + 1 + 2 * i)
                    if e >= 2:
                        dve.wait_ge(hT_ready, b + e - 1 + 2 * i)
                    tt(hd, A[0:CAP, E_SUM:E_SUM + 512], A[0:CAP, E_SG:E_SG + 512], ALU.mult).then_inc(gated, 1)
                    dve.wait_ge(gated, b + e + 1 + 2 * i)
                    tt(hd, A[0:CAP, E_SUM + 512:E_SUM + 1024], hd, ALU.mult).then_inc(hd_ready, 1)

                def y_sum(e, i):
                    par = e % 2
                    dve.wait_ge(y_half, b + e + 1 + 2 * i)
                    if e >= 2 or layer:
                        dve.wait_ge(ys_out[par], 16 * (b // 2 + e // 2) + 16 * i)
                    tt(A[0:CAP, E_Y + par * D:E_Y + (par + 1) * D], pair[1][0:CAP, :], A[0:CAP, E_YR:E_YR + D],
                       ALU.add).then_inc(y_ready, 1)

                def hidden_turned(e, i):
                    dve.wait_ge(hT_ready, b + e + 1 + 2 * i)
                    if e >= 2:
                        dve.wait_ge(d_ready, b + e - 1 + 2 * i)
                    copy(A[:, E_HT + e % 2 * 256:E_HT + e % 2 * 256 + 256], ps[5][:, 0:256]).then_inc(hTs_ready, 1)

                def stage(e, i):
                    hidden_turned(e - 1, i)
                    sums(e, i)
                    if e < NE - 1:
                        turned(e + 1, i)
                    hidden(e, i)
                    y_sum(e - 1, i)

                turned(0, 0)
                sums(0, 0)
                turned(1, 0)
                hidden(0, 0)
                stage(1, 0)
                stage(2, 0)
                with dve.Fori(0, 14) as i:
                    stage(3, i)
                    stage(4, i)
                stage(NE - 1, 0)
                hidden_turned(NE - 1, 0)
                y_sum(NE - 1, 0)
                over, n_over = ov[layer], all_tiles[layer] * P * 2 // CAP
                some = dve.value_load(route_i[0:1, 0:1], min_val=0, max_val=n_over)
                with dve.If(some > 0):
                    dve.wait_ge(y_ready, b + NE)
                    with dve.Fori(0, n_over) as j:
                        dve.wait_ge(over["xT"], j + 1)
                        copy(A[:, E_XG:E_XG + 512], ps[4][:, :]).then_inc(over["xT_copied"], 1)
                        dve.wait_ge(over["halves"], j + 1)
                        tt(A[0:CAP, E_SUM:E_SUM + 2 * BANK], pair[0][0:CAP, :], A[0:CAP, E_UP:E_UP + 2 * BANK],
                           ALU.add).then_inc(over["summed"], 1)
                        dve.wait_ge(over["summed"], j + 1)
                        dve.wait_ge(over["sigmoid"], j + 1)
                        hd = A[0:CAP, E_HD:E_HD + 512]
                        tt(hd, A[0:CAP, E_SUM:E_SUM + 512], A[0:CAP, E_SG:E_SG + 512],
                           ALU.mult).then_inc(over["gated"], 1)
                        dve.wait_ge(over["gated"], j + 1)
                        tt(hd, A[0:CAP, E_SUM + 512:E_SUM + 1024], hd, ALU.mult).then_inc(over["hidden"], 1)
                        dve.wait_ge(over["hiddenT"], j + 1)
                        copy(A[:, E_HT:E_HT + 256], ps[5][:, 0:256]).then_inc(over["hiddenT_copied"], 1)
                        dve.wait_ge(over["y_half"], j + 1)
                        tt(A[0:CAP, E_Y:E_Y + D], pair[1][0:CAP, :], A[0:CAP, E_YR:E_YR + D],
                           ALU.add).then_inc(over["y_copied"], 1)

            for layer in range(DEPTH):
                tiles = all_tiles[layer]
                lam_init = 0.8 - 0.6 * math.exp(-0.3 * layer)
                say(misc_ask)
                say(misc_ask)
                if layer == 0:
                    say(act_req)
                    answered()
                    v(tt(small[:, 128:144], V[:, V_COND:V_COND + 16], small[:, 144:160], ALU.mult))
                say(src_ready)
                loaded(2)
                for n in range(2):
                    v(tt(rows(0)[:, 0:64], brow[:, n * 128:n * 128 + 64], brow[:, n * 128 + 64:n * 128 + 128], ALU.mult))
                    v(red(small[:, 98 + n:99 + n], rows(0)[:, 0:64], X, ALU.add), act_req if n else dve_step)
                answered()
                v(tt(small[:, 96:97], small[:, 99:100], small[:, 98:99], ALU.subtract))
                v(ts(small[:, 96:97], small[:, 96:97], lam_init, None, ALU.subtract))
                def spread_ada(n):
                    part = n // 2
                    if part in (2, 5):
                        for j in range(2):
                            a = ((part // 5) * 2 + j) * D + n % 2 * BANK
                            v(copy(GT[:, a:a + BANK], turned_bank()[:, :]), tr_used)
                    else:
                        pi_ = (0, 1, None, 2, 3)[part]
                        a = (pi_ * 8 + n % 2 * 4) * 2
                        v(copy(mcol[:, a:a + 8], turned_bank()[:, 0:8]), tr_used)
                for n in range(12):
                    bank = product_bank()
                    v(tt(ada_row[0:2, n % 2 * BANK:(n % 2 + 1) * BANK], bank[0:2, :],
                         A[0:2, n * BANK:(n + 1) * BANK], ALU.add), acc_used)
                    if n > 0:
                        spread_ada(n - 1)
                spread_ada(11)
                for which in range(2):
                    gain = V[:, (V_MIX, V_FFN)[which] + layer * 8:(V_MIX, V_FFN)[which] + layer * 8 + 8]
                    m = mcol[:, :].rearrange("p (w k c) -> p w k c", w=4, k=8)
                    for cond in range(2):
                        c = ccol[:, (which * 2 + cond) * 8:(which * 2 + cond) * 8 + 8]
                        v(tt(c, m[:, 2 * which + 1, :, cond], gain, ALU.mult))
                        v(tt(c, c, gain, ALU.add))

                def gains(which):
                    return lambda t: ccol[:, (which * 2 + t // LT) * 8:(which * 2 + t // LT) * 8 + 8]

                def shifts(which):
                    return lambda t: mcol[:, :].rearrange("p (w k c) -> p w k c", w=4, k=8)[:, 2 * which, :, t // LT]

                norm_turn(MAX_TILES, h_tile, x4, gain=gains(0), shift=shifts(0))
                for n in range(4):
                    if n in (1, 3):
                        for t in range(MAX_TILES):
                            copy_turned((kaT if n == 1 else kcT)[:, :, t * P:(t + 1) * P])
                    for t in range(MAX_TILES):
                        bank = product_bank()
                        r = hs[:, (n * MAX_TILES + t) % 4 * BANK:(n * MAX_TILES + t) % 4 * BANK + BANK]
                        if n == 0 and t < LT:
                            rope_axial(r, bank, t, 1.0)
                        elif n in (0, 2):
                            v(copy(r, bank[:, :]), acc_used)
                        else:
                            v(copy(ar((VA if n == 1 else VC) + t * 512, 512), bank[:, :]), acc_used)
                for n in range(4):
                    if n in (1, 2):
                        for t in range(tiles):
                            copy_turned((qaT if n == 1 else qcT)[:, :, t * P:(t + 1) * P])
                    if n == 2:
                        say(misc_ask)
                        say(misc_ask)
                    for t in range(tiles):
                        bank = product_bank()
                        r = hs[:, (n * tiles + t) % 4 * BANK:(n * tiles + t) % 4 * BANK + BANK]
                        if n == 0 and t < LT:
                            rope_axial(r, bank, t, 0.125)
                        elif n < 2:
                            v(ts(r, bank[:, :], 0.125, None, ALU.mult), acc_used)
                        else:
                            x, y = rows(0)[:, 0:BANK], rows(1)[:, 0:BANK]
                            v(copy(x, bank[:, :]), acc_used)
                            v(tt(y, x, x, ALU.mult))
                            k = 2 * math.sqrt(2 / math.pi)
                            v(ts(y, y, k * 0.044715, k, ALU.mult, ALU.add))
                            v(tt(y, y, x, ALU.mult), act_req)
                            answered()
                            v(tt(ar((U if n == 2 else VV) + t * 512, BANK), x, y, ALU.mult))
                for t in range(tiles):
                    vt = ar(VV + t * 512, BANK)
                    v(red(small[:, 112 + t:113 + t], vt, X, ALU.add))
                    v(ts(small[:, 112 + t:113 + t], small[:, 112 + t:113 + t], 1.0 / BANK, None, ALU.mult))
                    v(ts(vt, vt, small[:, 112 + t:113 + t], None, ALU.subtract))
                    square_sum(vt, t, BANK)
                rstd(tiles, BANK)
                loaded(2)
                say(misc_ask)
                loaded()
                for t in range(tiles):
                    vt = ar(VV + t * 512, BANK)
                    v(stt(vt, vt, small[:, 48 + t:49 + t], brow[:, 0:512], ALU.mult, ALU.mult))
                    v(tt(vt, vt, brow[:, 512:1024], ALU.add), src_ready)
                for t in range(tiles):
                    bank = turned_bank()
                    sgb = V[:, V_SGB + layer * 4:V_SGB + layer * 4 + 4]
                    r = rows(0)[:, 0:BANK]
                    v(tt(r.rearrange("p (g c) -> p g c", g=4), bank[:, :].rearrange("p (g c) -> p g c", g=4),
                         spread(sgb, 4, P), ALU.add), tr_used)
                    ut = ar(U + t * 512, BANK)
                    v(tt(ut, ut, r, ALU.mult))
                say(misc_ask)
                say(misc_ask)
                attention(second_units(layer))
                say(misc_ask)
                for t in range(tiles):
                    for h in range(4):
                        square_sum(ar(YA + t * 512 + h * P, P), t * 4 + h, P)
                rstd(4 * tiles, P)
                loaded()
                v(ts(brow[:, 0:P], brow[:, 0:P], 1.0 - lam_init, None, ALU.mult))
                for t in range(tiles):
                    for h in range(4):
                        y = ar(YA + t * 512 + h * P, P)
                        v(stt(y, y, small[:, 48 + t * 4 + h:49 + t * 4 + h], brow[:, 0:P], ALU.mult, ALU.mult))
                say_n = 3 * tiles
                for _ in range(say_n):
                    say(src_ready)
                for t in range(tiles):
                    for b in range(3):
                        dst = ar(YT, 6144).rearrange("p (k t c) -> p k t c", k=12, t=MAX_TILES)
                        copy_turned(dst[:, b * 4:b * 4 + 4, t, :])
                say(misc_ask)
                say(misc_ask)
                for n in range(6):
                    half, b = n // 3, n % 3
                    for t in range(tiles):
                        bank = product_bank()
                        v(copy(ar(MERGED_SIG + t * 512, BANK), bank[:, :]), acc_used)
                        say(act_req)
                    for t in range(tiles):
                        bank = product_bank()
                        answered()
                        y = y_tile(t)[:, half * BANK:(half + 1) * BANK]
                        sg = ar(MERGED_SIG + t * 512, BANK)
                        if b == 0:
                            v(tt(y, bank[:, :], sg, ALU.mult), acc_used)
                        else:
                            v(tt(rows(0)[:, 0:BANK], bank[:, :], sg, ALU.mult), acc_used)
                            v(tt(y, y, rows(0)[:, 0:BANK], ALU.add))
                turn(tiles, y_tile, x4, scaled=False)

                def gate(which, t, half):
                    a = (which * 2 + t // LT) * D + half * BANK
                    return GT[:, a:a + BANK]
                for n in range(2):
                    for t in range(tiles):
                        bank = product_bank()
                        v(tt(rows(0)[:, 0:BANK], bank[:, :], gate(0, t, n), ALU.mult), acc_used)
                        part = h_tile(t)[:, n * BANK:(n + 1) * BANK]
                        v(tt(part, part, rows(0)[:, 0:BANK], ALU.add))
                norm_turn(tiles, h_tile, x4, gain=gains(1), shift=shifts(1))
                for t in range(tiles):
                    for g in range(2):
                        v(copy(ar(XTOK + t * D + g * BANK, BANK), turned_bank()[:, :]), tr_used)
                loaded(2)
                say(src_ready)

                def rt(n, width=NE):
                    return ar(RT + 128 * n, tiles * width).rearrange("p (t e) -> p t e", t=tiles)
                logits = ar(RT + 128 * 22, 144)[:, 0:tiles * 36].rearrange("p (t e) -> p t e", t=tiles)
                bank = turned_bank()
                v(tt(logits, bank[:, 0:tiles * 36].rearrange("p (t e) -> p t e", t=tiles),
                     vrow[:, 0:36].unsqueeze(1).broadcast_to([P, tiles, 36]), ALU.add), tr_used)
                iota = rt(2)
                e_idx = C[:, C_EIDX:C_EIDX + NE].unsqueeze(1).broadcast_to([P, tiles, NE])
                v(ts(iota, e_idx, -64.0, None, ALU.add))
                g_log = logits[:, :, 0:NGRP]
                hot_g, tmp_g = rt(3, NGRP), rt(4, NGRP)
                first_max(hot_g, g_log, iota[:, :, 0:NGRP], tiles, NGRP, tmp_g, 164)
                v(tt(rt(1, NGRP), g_log, spread(small[:, 164:164 + tiles], tiles, NGRP), ALU.subtract), act_req)
                answered()
                v(red(small[:, 168:168 + tiles], rt(1, NGRP), X, ALU.add))
                v(nc.vector.reciprocal(small[:, 168:168 + tiles], small[:, 168:168 + tiles]))
                masked, floor = rt(5), rt(6, NGRP)
                v(ts(floor, hot_g, -NEG, NEG, ALU.mult, ALU.add))
                for t in range(tiles):
                    m4 = masked[:, t, :].rearrange("p (g e) -> p g e", g=NGRP)
                    v(tt(m4, logits[:, t, NGRP:].rearrange("p (g e) -> p g e", g=NGRP),
                         spread(hot_g[:, t, :], NGRP, EPG), ALU.mult))
                    v(tt(m4, m4, spread(floor[:, t, :], NGRP, EPG), ALU.add))
                first, second, tmp, both = rt(7), rt(8), rt(9), rt(0)
                first_max(first, masked, iota, tiles, NE, tmp, 172)
                v(stt(masked, first, 2 * NEG, masked, ALU.mult, ALU.add))
                first_max(second, masked, iota, tiles, NE, tmp, 176)
                v(tt(both, first, second, ALU.add), src_ready)
                v(tt(small[:, 104:104 + tiles], small[:, 176:176 + tiles], small[:, 172:172 + tiles], ALU.subtract),
                  act_req)
                answered()
                v(ts(small[:, 180:180 + tiles], small[:, 104:104 + tiles], 1.0, None, ALU.add))
                v(nc.vector.reciprocal(small[:, 180:180 + tiles], small[:, 180:180 + tiles]))
                v(tt(route[:, 0:tiles], small[:, 180:180 + tiles], small[:, 168:168 + tiles], ALU.mult))
                v(tt(route[:, 4:4 + tiles], route[:, 0:tiles], small[:, 104:104 + tiles], ALU.mult))
                before, count = rt(10), ar(RT + 128 * 11, NE)
                bank = turned_bank()
                v(copy(ar(RT + 128 * 12, 160)[:, 0:(tiles + 1) * NE], bank[:, 0:(tiles + 1) * NE]), tr_used)
                before = ar(RT + 128 * 12, tiles * NE).rearrange("p (t e) -> p t e", t=tiles)
                count = ar(RT + 128 * 12 + tiles * NE, NE)
                n_blocks = tiles * P // CAP
                blocks, run, run2, t32 = (ar(RT + 128 * 15 + 32 * n, NE) for n in range(4))
                v(nc.vector.memset(blocks, 0.0))
                for j in range(1, n_blocks):
                    v(stt(blocks, count, float(j * CAP), blocks, ALU.is_gt, ALU.add))
                v(copy(run, blocks))
                a, b_ = run, run2
                for s in (1, 2, 4, 8, 16):
                    v(copy(b_[:, 0:s], a[:, 0:s]))
                    v(tt(b_[:, s:NE], a[:, s:NE], a[:, 0:NE - s], ALU.add))
                    a, b_ = b_, a
                run = a
                start = t32
                v(tt(start, run, blocks, ALU.subtract))
                for k, hot in enumerate((first, second)):
                    picked = small[:, 184 + 12 * k:196 + 12 * k]
                    for m, table in enumerate((before, e_idx, start.unsqueeze(1).broadcast_to([P, tiles, NE]))):
                        v(tt(tmp, hot, table, ALU.mult))
                        v(red(picked[:, 4 * m:4 * m + tiles], tmp, X, ALU.add))
                    place, expert_, begin = (picked[:, 4 * m:4 * m + tiles] for m in range(3))
                    q, past, row_ = (small[:, 208 + 4 * m:208 + 4 * m + tiles] for m in range(3))
                    v(nc.vector.memset(q, 0.0))
                    for j in range(1, n_blocks):
                        v(stt(q, place, float(j * CAP), q, ALU.is_ge, ALU.add))
                    v(tt(row_, expert_, q, ALU.subtract))
                    v(ts(row_, row_, float(CAP), None, ALU.mult))
                    v(tt(row_, row_, place, ALU.add))
                    v(tt(past, begin, expert_, ALU.subtract))
                    v(tt(past, past, q, ALU.add))
                    v(ts(past, past, float(NE - 1), float(CAP), ALU.add, ALU.mult))
                    v(ts(q, q, 0.0, None, ALU.is_gt))
                    v(tt(past, past, q, ALU.mult))
                    v(tt(row_, row_, past, ALU.add))
                    v(copy(route_u[:, k * MAX_TILES:k * MAX_TILES + tiles], row_))
                n_over = 2 * tiles * P // CAP
                table = ar(RT + 128 * 16, n_over * NE).rearrange("p (j e) -> p j e", j=n_over)
                v(tt(table, run.unsqueeze(1).broadcast_to([P, n_over, NE]),
                     spread(C[:, C_OIDX:C_OIDX + n_over], n_over, NE), ALU.is_le))
                ofs = small[:, 224:224 + n_over]
                v(red(ofs, table, X, ALU.add))
                v(ts(ofs, ofs, float(NE - 1), None, ALU.min))
                v(copy(route_i[:, 1:1 + n_over], ofs))
                v(copy(route_i[:, 0:1], run[:, NE - 1:NE]), route_ready)
                experts(layer)
                for t in range(tiles):
                    dve.wait_ge(gather_in[t % 2], seen.next(gather_in[t % 2], 32))
                    y1, y2 = (ar(YG + (t % 2 * 2 + k) * D, D) for k in range(2))
                    v(ts(y1, y1, route[:, t:t + 1], None, ALU.mult))
                    v(stt(y1, y2, route[:, 4 + t:5 + t], y1, ALU.mult, ALU.add))
                    v(tt(y1, y1, GT[:, (2 + t // LT) * D:(3 + t // LT) * D], ALU.mult))
                    v(tt(h_tile(t), h_tile(t), y1, ALU.add))
                    if t < tiles - 2:
                        say(misc_ask)
            say(misc_ask)
            for t in range(LT):
                square_sum(h_tile(t), t, D)
            rstd(LT, D)
            loaded()
            for t in range(LT):
                v(stt(y_tile(t), h_tile(t), small[:, 48 + t:49 + t], brow[:, :], ALU.mult, ALU.mult),
                  final_ready if t == LT - 1 else dve_step)


def kernel(**inputs):
    import concourse.bacc as bacc
    from concourse.bass_utils import run_bass_kernel_spmd

    a = {k: np.asarray(v) for k, v in inputs.items()}
    c, hot = constants()

    def cols(x):
        return x.reshape(-1, P).T

    v = [cols(a["norm_g"][i, 0]) for i in range(DEPTH)] + [cols(a["norm_g"][i, 2]) for i in range(DEPTH)]
    v += [cols(a["mla_q_norm"][0]), cols(a["mla_kv_norm"][0])]
    v += [cols(a["g_norm_mix_2"][i]) for i in range(DEPTH)] + [cols(a["g_norm_ffn_2"][i]) for i in range(DEPTH)]
    v += [np.stack([cols(a["c_2"][0]), cols(a["c_ctx_2"])], axis=2).reshape(P, 2 * KD)]
    v += [a["sg_b_2"][i].T for i in range(DEPTH)]
    arrays = {
        "constants": c,
        "hot": hot,
        "vectors": np.concatenate(v, axis=1),
        "positions": a["positions"].reshape(LT, P).T,
        "ffn_w_in": a["ffn_w_in"].reshape(DEPTH, D, 2, D_FF // FF_PIECE, FF_PIECE).transpose(0, 1, 3, 2, 4)
                                 .reshape(DEPTH, D, 2 * D_FF),
        "p_t": a["p"][:, 0].transpose(0, 2, 1),
        "sg_wt": a["sg_w_2"].transpose(0, 1, 3, 2),
        "router_w": np.concatenate([a["moe_w_group_2"], a["moe_w_router_2"]], axis=2),
        "router_b": np.concatenate([a["moe_b_group_2"], a["moe_b_router_2"]], axis=1),
    }
    for name in ("x", "ctx_2", "norm_g", "ffn_w_out", "ple_w_proj", "ple_w_gate", "rel_bias", "mla_w_a",
                 "mla_w_uq", "mla_w_ukv", "mla_w_o", "dil_w_qkv", "dil_w_o", "w_ada_2", "b_ada_2", "w_in_2",
                 "da_lambda_2", "da_subln_g_2", "sg_ln_g_2", "sg_ln_b_2", "na_rpb_2", "w_branch_2", "w_out_2",
                 "moe_w_gate_2", "moe_w_up_2", "moe_w_down_2", "g_final_2"):
        arrays[name] = a[name]

    nc = bacc.Bacc("TRN2", target_bir_lowering=False, num_devices=1)
    ins, feed = {}, {}
    for name, x in arrays.items():
        x = np.ascontiguousarray(x)
        feed[f"in_{name}"] = x
        ins[name] = nc.dram_tensor(f"in_{name}", x.shape, mybir.dt.from_np(x.dtype), kind="ExternalInput").ap()
    result = nc.dram_tensor("result", [1, SEQ, D], F32, kind="ExternalOutput").ap()
    build_program(nc, ins, result)
    r = run_bass_kernel_spmd(nc, [feed], core_ids=[0])
    return r.results[0]["result"]
```

```python
import math
from contextlib import ExitStack

import numpy as np
import concourse.bass as bass
from concourse import mybir

F32 = mybir.dt.float32
F32R = mybir.dt.float32r
I32 = mybir.dt.int32
U32 = mybir.dt.uint32
ALU = mybir.AluOpType
ACT = mybir.ActivationFunctionType
X = mybir.AxisListType.X

P = 128
D = 1024
KD = D // P
SEQ = 256
LT = SEQ // P
CT = 256 // P
DEPTH = 2
EPS = 1e-6
NEG = -1e30
BANK = 512

MLA_H, MLA_QR, MLA_KVR, NOPE, ROT, MLA_V = 16, 384, 256, 64, 32, 64
MLA_DK = NOPE + ROT
D_PLE = 256
D_FF = 2816
DIL_G, DIL_H = 3, 16
DILATION = (1, 4, 16)
SPAN = 128
BUCKETS, MAX_DIST = 32, 2048
BIAS_LEN = 384
FF_PIECE = 256

OFF_KA, OFF_VA, OFF_KC, OFF_VC, OFF_QA, OFF_QC, OFF_ZB, OFF_GATE = 0, 512, 1024, 1536, 2048, 2560, 3072, 4096
GRID_W, NA_COLS, NA_H, RPB_R, RPB_C = 64, 16, 8, 15, 31
RPB_W = 2 * GRID_W - 1

NE, NGRP, EPG, D_EXP = 32, 4, 8, 512
CAP = 64
MAX_TILES = LT + CT
MAX_OVER = MAX_TILES * P * 2 // CAP
RING = 4
KG = 4

C_IDENT, C_FLIP, C_CAUSAL, C_NAMASK, C_UPPER = 0, 128, 256, 512, 576
C_COS, C_SIN, C_INV, C_EIDX, C_OIDX, C_SEL, C_END = 704, 832, 960, 976, 1008, 1024, 1280
V_NG0, V_NG2, V_QN, V_KVN, V_MIX, V_FFN, V_COND, V_SGB, V_END = 0, 16, 32, 35, 37, 53, 69, 85, 93


def constants():
    c = np.zeros((P, C_END), np.float32)
    i = np.arange(P)
    c[:, C_IDENT:C_IDENT + P] = np.eye(P)
    c[:, C_FLIP:C_FLIP + P] = np.eye(P)[::-1]
    col = np.arange(2 * P)
    c[:, C_CAUSAL:C_CAUSAL + 2 * P] = np.where(P + i[:, None] - col[None, :] >= 0, 0.0, NEG)
    qc = GRID_W - 1 - i % GRID_W
    start = np.clip(qc - NA_COLS // 2, 0, GRID_W - NA_COLS)
    kc = np.arange(GRID_W)
    ok = (kc[None] >= start[:, None]) & (kc[None] < start[:, None] + NA_COLS)
    c[:, C_NAMASK:C_NAMASK + GRID_W] = np.where(ok, 0.0, NEG)
    c[:, C_UPPER:C_UPPER + P] = i[:, None] < i[None, :]
    half = 16
    inv = (np.float32(10000.0) ** (-np.arange(half, dtype=np.float32) / np.float32(half))).astype(np.float32)
    t = np.arange(SEQ)
    ar = (t // GRID_W).astype(np.float32)[:, None] * inv
    ac = (t % GRID_W).astype(np.float32)[:, None] * inv
    cos = np.cos(np.concatenate([ar, ar, ac, ac], 1)).astype(np.float32)
    sin = np.concatenate([-np.sin(ar), np.sin(ar), -np.sin(ac), np.sin(ac)], 1).astype(np.float32)
    for n in range(LT):
        c[:, C_COS + 64 * n:C_COS + 64 * n + 64] = cos[n * P:(n + 1) * P]
        c[:, C_SIN + 64 * n:C_SIN + 64 * n + 64] = sin[n * P:(n + 1) * P]
    c[:, C_INV:C_INV + half] = inv
    c[:, C_EIDX:C_EIDX + NE] = np.arange(NE)
    c[:, C_OIDX:C_OIDX + MAX_OVER] = np.arange(MAX_OVER)
    c[0, C_SEL:C_SEL + P] = 1.0
    c[1, C_SEL + P:C_SEL + 2 * P] = 1.0
    hot = np.zeros((64, DIL_G, BIAS_LEN), np.float32)
    exact = BUCKETS // 2
    for g, dil in enumerate(DILATION):
        for m in range(BIAS_LEN):
            dist = 2 * P - 1 - m
            if dist >= 0 and dist % dil == 0 and dist // dil <= SPAN:
                n = np.float32(max(dist, 1))
                large = exact + int(np.float32(np.log(n / np.float32(exact)) / np.float32(math.log(MAX_DIST / exact))
                                               * np.float32(BUCKETS - exact)))
                hot[dist if dist < exact else min(large, BUCKETS - 1), g, m] = 1.0
            else:
                hot[BUCKETS, g, m] = NEG
    return c, hot.reshape(64, DIL_G * BIAS_LEN)


class Tally:

    def __init__(self):
        self.n = {}

    def next(self, sem, by=1):
        self.n[sem.name] = self.n.get(sem.name, 0) + by
        return self.n[sem.name]

    def now(self, sem):
        return self.n.get(sem.name, 0)


class Gemm:

    def __init__(self, w, k_tiles, chunks, tiles, split=False):
        self.w, self.k_tiles, self.chunks, self.tiles, self.split = w, k_tiles, chunks, tiles, split
        self.groups = [(k, min(KG, k_tiles - k)) for k in range(0, k_tiles, KG)]


def columns(c0, c1, width=BANK):
    return [(c, min(width, c1 - c)) for c in range(c0, c1, width)]


def build_program(nc, I, out):
    ctx = ExitStack()
    with ctx:
        def sb(name, cols, dt=F32, rows=P):
            return ctx.enter_context(nc.sbuf_tensor(name, [rows, cols], dt))

        def sb_twin(name, cols):
            base = -(-nc.sbuf_base // 32) * 32
            t = sb(name, cols)
            return t, nc.alloc_sbuf_tensor_at(name + "_r", [P, cols], F32R, offset=base)

        def sem(name):
            return ctx.enter_context(nc.semaphore(name))

        ring, ring_r = sb_twin("weight_ring", RING * KG * BANK)
        spare, highs = sb_twin("weights_high", 2 * KG * BANK)
        H = sb("hidden", MAX_TILES * D)
        XT, XT_r = sb_twin("x_transposed", KD * MAX_TILES * P)
        Y, Y_r = sb_twin("tokens_out", MAX_TILES * D)
        A, A_r = sb_twin("arena", 18432)
        GT, GT_r = sb_twin("gates", 4 * D)
        C = sb("constants", C_END)
        V = sb("vectors", V_END)
        hs = sb("scaled_rows", 2 * D)
        brow = sb("broadcast_row", D)
        small = sb("small", 256)
        mcol = sb("mod_columns", 2 * KD * 4)
        ccol = sb("scale_columns", 2 * KD * 2)
        posi = sb("positions", LT, I32)
        ones = sb("ones", P)
        vrow = sb("vector_rows", 64)
        ada_row = A[:, 8192:8192 + 2 * BANK]
        pair = [ctx.enter_context(nc.psum_tensor(f"banks{2 * i}", [P, 2 * BANK], F32)) for i in range(4)]
        ps = [pair[i // 2][:, i % 2 * BANK:(i % 2 + 1) * BANK] for i in range(8)]
        route = sb("route", 64)
        route_u = sb("route_rows", 16, U32)
        route_i = sb("route_over", 32, I32)

        xs_dram = nc.dram_tensor("moe_x", [(NE + MAX_OVER) * CAP, D], F32, kind="Internal").ap()
        ys_dram = nc.dram_tensor("moe_y", [(NE + MAX_OVER) * CAP, D], F32, kind="Internal").ap()
        low_dram = nc.dram_tensor("x_low", [P, KD * MAX_TILES * P], F32R, kind="Internal").ap()
        rel_dram = nc.dram_tensor("rel_rows", [DIL_G * DIL_H, BIAS_LEN], F32, kind="Internal").ap()
        rpb_dram = nc.dram_tensor("rpb_rows", [DEPTH, NA_H * RPB_R, RPB_W], F32, kind="Internal").ap()

        ident = C[:, C_IDENT:C_IDENT + P]
        flip = C[:, C_FLIP:C_FLIP + P]
        causal = C[:, C_CAUSAL:C_CAUSAL + 2 * P]
        upper = C[:, C_UPPER:C_UPPER + P]

        def h_tile(t):
            return H[:, t * D:(t + 1) * D]

        def y_tile(t):
            return Y[:, t * D:(t + 1) * D]

        def xT(kt, t, tiles=MAX_TILES):
            a = (kt * tiles + t) * P
            return XT[:, a:a + P]

        def xT4(g, t, tiles, n):
            return XT[:, :KD * tiles * P].rearrange("p (k t c) -> p k t c", k=KD, t=tiles)[:, 4 * g:4 * g + n, t, :]

        def rows(n):
            return hs[:, n % 2 * D:n % 2 * D + D]

        def ar(a, n):
            return A[:, a:a + n]

        def slot(c, kn, width, memory=None):
            a = c % RING * KG * BANK
            return (memory or ring)[:, a:a + kn * width].rearrange("p (k n) -> p k n", k=kn)

        def high(s, kn, width):
            b = high_place[s]
            a = b % 2 * KG * BANK
            return (highs if b < 2 else GT_r)[:, a:a + kn * width].rearrange("p (k n) -> p k n", k=kn)

        def over_down(half):
            return spare[:, half * KG * BANK:(half + 1) * KG * BANK].rearrange("p (k n) -> p k n", k=KG)

        w_in = [sem(f"weights_arrived_{i}") for i in range(RING)]
        w_used = sem("weights_used")
        high_ready, low_ready = sem("weights_high_ready"), sem("weights_low_ready")
        acc_ready, acc_used = sem("product_ready"), sem("product_used")
        tr_ready, tr_used = sem("transpose_ready"), sem("transpose_used")
        src_ready = sem("rows_ready")
        x_ready = sem("x_ready")
        act_req, act_rep = sem("scalar_asked"), sem("scalar_answered")
        sig_ready = sem("sigmoid_ready")
        const_in, vec_in = sem("constants_in"), sem("vectors_in")
        misc_in = [sem(f"misc_in_{i}") for i in range(4)]
        misc_ask = sem("misc_asked")
        dve_step, act_step, pool_step = sem("vector_step"), sem("scalar_step"), sem("pool_step")
        s_ready, max_ready, p_ready = sem("scores_ready"), sem("max_ready"), sem("probs_ready")
        exp_ready = sem("exp_ready")
        pT_ready, pTs_ready = sem("probsT_ready"), sem("probsT_copied")
        o_ready, o_used = sem("attn_out_ready"), sem("attn_out_used")
        bias_in = [sem("bias_in_0"), sem("bias_in_1")]
        na_bias_in = [sem(f"na_bias_in_{i}") for i in range(8)]
        bias_ready = sem("bias_masked")
        xs_in = [sem("expert_x_in_0"), sem("expert_x_in_1")]
        ys_out = [sem("expert_y_out_0"), sem("expert_y_out_1")]
        xt_ready, xg_ready = sem("expert_xT_ready"), sem("expert_xT_copied")
        gu_ready, esig_ready, hd_ready = sem("expert_gate_up"), sem("expert_sigmoid"), sem("expert_hidden")
        hT_ready, hTs_ready = sem("expert_hiddenT"), sem("expert_hiddenT_copied")
        d_ready, y_ready = sem("expert_down"), sem("expert_y_copied")
        route_ready = sem("route_ready")
        zero_out, scatter_out = sem("zero_out"), sem("scatter_out")
        gather_in = [sem("gather_in_0"), sem("gather_in_1")]
        gated, halves_ready, summed, y_half = (sem("expert_" + n) for n in ("gated", "halves", "summed", "y_half"))
        ov = [{n: sem(f"over{i}_{n}") for n in ("x_in", "w_in", "xT", "xT_copied", "gate_up", "halves", "summed", "sigmoid", "gated", "y_half", "hidden",
                                               "hiddenT", "hiddenT_copied", "down", "y_copied", "y_out")}
              for i in range(DEPTH)]
        final_ready = sem("final_ready")
        result_out = sem("result_out")
        scratch_out = sem("scratch_out")
        low_saved, low_back = sem("x_low_saved"), sem("x_low_back")

        g_mla_a = Gemm(I["mla_w_a"][0], KD, columns(0, MLA_QR + MLA_KVR + ROT), LT)
        g_uq = Gemm(I["mla_w_uq"][0], MLA_QR // P, columns(0, MLA_H * MLA_DK), LT)
        g_ukv = Gemm(I["mla_w_ukv"][0], MLA_KVR // P, columns(0, MLA_H * (NOPE + MLA_V)), LT)
        g_mla_o = Gemm(I["mla_w_o"][0], KD, columns(0, D), LT, split=True)
        g_ff_in = [Gemm(I["ffn_w_in"][i], KD, columns(0, 2 * D_FF),
                        LT, split=True) for i in range(DEPTH)]
        g_ff_out = [Gemm(I["ffn_w_out"][i], D_FF // P, columns(0, D), LT, split=True) for i in range(DEPTH)]
        g_ple_g = [Gemm(I["ple_w_gate"][i], KD, columns(0, D), LT, split=True) for i in range(DEPTH)]
        g_ple_p = [Gemm(I["ple_w_proj"][i], D_PLE // P, columns(0, D), LT) for i in range(DEPTH)]
        g_dil = Gemm(I["dil_w_qkv"][0], KD, columns(0, DIL_G * 3 * D), LT, split=True)
        g_dil_o = Gemm(I["dil_w_o"][0], KD, columns(0, D), LT, split=True)
        ctx_tiles = [CT, 0]
        all_tiles = [LT + CT, LT]
        g_ada = [Gemm(I["w_ada_2"][i], KD, columns(0, 6 * D), 1) for i in range(DEPTH)]
        g_kv = [Gemm(I["w_in_2"][i], KD, columns(0, OFF_QA), MAX_TILES, split=True) for i in range(DEPTH)]
        g_qz = [Gemm(I["w_in_2"][i], KD, columns(OFF_QA, OFF_GATE), all_tiles[i], split=True) for i in range(DEPTH)]
        g_gate = [[Gemm(I["w_in_2"][i], KD, columns(OFF_GATE + b * D + n * BANK, OFF_GATE + b * D + (n + 1) * BANK),
                        all_tiles[i], split=True) for n in range(2) for b in range(3)] for i in range(DEPTH)]
        g_branch = [[Gemm(I["w_branch_2"][i, b], BANK // P, columns(n * BANK, (n + 1) * BANK), all_tiles[i])
                     for n in range(2) for b in range(3)] for i in range(DEPTH)]
        g_out = [Gemm(I["w_out_2"][i], KD, columns(0, D), all_tiles[i], split=True) for i in range(DEPTH)]

        STREAM = [g_mla_a, g_uq, g_ukv, g_mla_o, g_ff_in[0], g_ff_out[0], g_ple_g[0], g_ple_p[0],
                  g_dil, g_dil_o, g_ff_in[1], g_ff_out[1], g_ple_g[1], g_ple_p[1]]
        block_one = list(STREAM)
        for i in range(DEPTH):
            STREAM += [g_ada[i], g_kv[i], g_qz[i]]
            for a, b in zip(g_gate[i], g_branch[i]):
                STREAM += [a, b]
            STREAM += [g_out[i], ("experts", i)]

        chunks, marks, split_ends = 0, Tally(), []
        high_place, high_free = [], []
        for g in STREAM:
            if isinstance(g, tuple):
                chunks += 6 * NE
                marks.next(w_used, 4 * NE)
                continue
            g.first, g.first_split, g.ends = chunks, len(split_ends), []
            for _ in g.chunks:
                for n in range(len(g.groups)):
                    g.ends.append((acc_ready, marks.next(acc_ready, g.tiles)) if n == len(g.groups) - 1
                                  else (w_used, marks.next(w_used)))
            chunks += len(g.ends)
            if g.split:
                for end in g.ends:
                    s = len(split_ends)
                    b = s % 4 if g in block_one else s % 2
                    before = [j for j in range(s) if high_place[j] == b]
                    high_free.append(split_ends[before[-1]] if before else None)
                    high_place.append(b)
                    split_ends.append(end)

        KV, QT, KT, QROW, KROW, AROW = 0, 4096, 8192, 12288, 15360, 4096
        DQT, DKT, DV = 0, 6144, 12288
        HT = 0
        PLE, HL = 9216, 9728
        PSIG = 0
        KAT, QAT, KCT, QCT, VA, VC, U, VV, YC = (2048 * n for n in range(9))
        YA = VV
        YT = KAT
        MERGED_SIG = VC
        XL = QCT
        SG_W = YC
        BADA = 0
        E_X, E_XG, E_HD, E_HT, E_Y, E_SG, XTOK, RT = 0, 2048, 3072, 4096, 4608, 6656, 7168, 11264
        E_UP, E_SUM, E_YR = XTOK, XTOK + 1024, XTOK + 2048
        YG = 14336
        ROUTER = YC
        TMP = 5504

        class Unit:
            def __init__(self, maps, n_keys, scale, values, width, dest, bias=None, kind="", head=0, tile=0):
                self.maps, self.n_keys, self.scale, self.values = maps, n_keys, scale, values
                self.width, self.dest, self.bias, self.kind, self.head, self.tile = width, dest, bias, kind, head, tile

        def mla_units():
            units = []
            qT = ar(QT, 4096).rearrange("p (h t) -> p h t", h=MLA_H)
            kT = ar(KT, 4096).rearrange("p (h t) -> p h t", h=MLA_H)
            kv = ar(KV, 4096).rearrange("p (t h e) -> p t h e", t=LT, h=MLA_H)
            for h in range(MLA_H):
                for t in range(LT):
                    n = (t + 1) * P
                    maps = [[(0, n, qT[0:MLA_DK, h, t * P:(t + 1) * P], kT[0:MLA_DK, h, 0:n],
                              ident, causal[:, 2 * P - n:2 * P])]]
                    values = [kv[:, k, h, NOPE:NOPE + MLA_V] for k in range(t + 1)]
                    units.append(Unit(maps, n, MLA_DK ** -0.5, values, MLA_V,
                                      y_tile(t)[:, h * MLA_V:(h + 1) * MLA_V], head=h, tile=t))
            return place(units, True)

        def dil_units():
            units = []
            qT = ar(DQT, 6144).rearrange("p (g h t) -> p g h t", g=DIL_G, h=8)
            kT = ar(DKT, 6144).rearrange("p (g h t) -> p g h t", g=DIL_G, h=8)
            vv = ar(DV, 6144).rearrange("p (t g h e) -> p t g h e", t=LT, g=DIL_G, h=DIL_H)
            for h in range(DIL_H):
                a = 64 * (h % 2)
                bias = XT[:, 2048 + h % 2 * 768:2048 + h % 2 * 768 + 768].rearrange("p (g c) -> p g c", g=DIL_G)
                for t in range(LT):
                    n = (t + 1) * P
                    maps = [[(g * n, n,
                              qT[a:a + 64, g, h // 2, t * P:(t + 1) * P], kT[a:a + 64, g, h // 2, 0:n],
                              flip, bias[:, g, 2 * P - n:2 * P]) for g in range(DIL_G)]]
                    values = [vv[:, k, g, h, :] for g in range(DIL_G) for k in range(t + 1)]
                    units.append(Unit(maps, DIL_G * n, 1.0, values, 64, y_tile(t)[:, h * 64:(h + 1) * 64],
                                      bias="dil", head=h, tile=t))
            return place(units, True)

        qaT = ar(QAT, 2048).rearrange("p (h t) -> p h t", h=4)
        kaT = ar(KAT, 2048).rearrange("p (h t) -> p h t", h=4)
        qcT = ar(QCT, 2048).rearrange("p (h t) -> p h t", h=4)
        kcT = ar(KCT, 2048).rearrange("p (h t) -> p h t", h=4)
        va = ar(VA, 2048).rearrange("p (t h e) -> p t h e", t=4, h=4)
        vc = ar(VC, 2048).rearrange("p (t h e) -> p t h e", t=4, h=8)

        def na_bias(h, t):
            a = (h % 4 * LT + t) * SEQ
            return hs[:, a:a + SEQ]

        def second_units(layer):
            units = []
            tiles = list(range(all_tiles[layer]))
            for h in range(4):
                for t in tiles:
                    k0 = 0 if t < LT else LT * P
                    n = MAX_TILES * P - k0
                    maps = [[(m * BANK, n, qaT[64 * m:64 * m + 64, h, t * P:(t + 1) * P],
                              kaT[64 * m:64 * m + 64, h, k0:], None, None)] for m in range(2)]
                    values = [va[:, k, h, :] for k in range(k0 // P, MAX_TILES)]
                    units.append(Unit(maps, n, 1.0, values, P,
                                      ar(YA + t * 512, 512)[:, h * P:(h + 1) * P], kind="diff", head=h, tile=t))
            diff, units = place(units, False), []
            for h in range(NA_H):
                a = 64 * (h % 2)
                for t in tiles:
                    k0 = 0 if t < LT else LT * P
                    n = MAX_TILES * P - k0
                    if t < LT:
                        b = na_bias(h, t)
                        maps = [[(0, SEQ, qcT[a:a + 64, h // 2, t * P:(t + 1) * P], kcT[a:a + 64, h // 2, 0:SEQ],
                                  flip, b),
                                 (SEQ, SEQ, qcT[a:a + 64, h // 2, t * P:(t + 1) * P],
                                  kcT[a:a + 64, h // 2, SEQ:2 * SEQ], None, None)]]
                    else:
                        maps = [[(0, n, qcT[a:a + 64, h // 2, t * P:(t + 1) * P], kcT[a:a + 64, h // 2, k0:],
                                  None, None)]]
                    values = [vc[:, k, h, :] for k in range(k0 // P, MAX_TILES)]
                    units.append(Unit(maps, n, 1.0, values, 64,
                                      ar(YC + t * 512, 512)[:, h * 64:(h + 1) * 64],
                                      bias="na" if t < LT else None, head=h, tile=t))
            return diff, place(units, False)

        def wide(units):
            return max(len(unit.values) for unit in units) > BANK // P

        def turned_probs(units, u):
            return pair[2] if wide(units) else ps[4 + u % 2]

        def held(units):
            return 4 if all(len(unit.maps) == 1 and unit.n_keys <= BANK for unit in units) else 2

        def stat(units, u, m=0):
            return u % 8 if held(units) == 4 else 2 * (u % 4) + m

        def place(units, first):
            n = held(units)
            for u, unit in enumerate(units):
                unit.scores = ps[u % 4] if n == 4 else pair[u % 2]
                a = (2048 if first else 0) + u % n * (2048 // n)
                unit.probs = Y[:, a:a + 2048 // n]
                unit.pT = XT[:, u % 2 * 768:u % 2 * 768 + 768] if first else Y[:, 2048 + u % 2 * 768:2816 + u % 2 * 768]
            return units

        def counted(engine, value):
            if not isinstance(value, int):
                value = engine.snap(value)
                engine.wait_ge(const_in, 48)
            return value

        block = ctx.enter_context(nc.Block())

        @block.sync
        def _(sp):
            seen = Tally()
            freed = []

            def take_slot(c, i=0, per=None):
                if c >= RING:
                    s, v, k = freed[c - RING]
                    sp.wait_ge(s, counted(sp, v + (k * i if per else 0)))

            def stream(g):
                for col, width in g.chunks:
                    for n, (k0, kn) in enumerate(g.groups):
                        c = len(freed)
                        take_slot(c)
                        src = g.w[k0 * P:(k0 + kn) * P, :].rearrange("(k p) n -> p k n", p=P)[:, :, col:col + width]
                        dst = slot(c, kn, width)
                        sp.dma_start(dst, src).then_inc(w_in[c % RING], 16)
                        s, value = g.ends[c - g.first]
                        seen.next(s, value - seen.now(s))
                        freed.append((s, value, 0))

            def load_gate_up(layer, e, c, waits):
                for w, name in enumerate(("moe_w_gate_2", "moe_w_up_2")):
                    for half in range(2):
                        waits(c)
                        src = I[name][layer].rearrange("e (g k p) n -> e g p k n", p=P, k=KG)
                        sp.dma_start(slot(c, KG, BANK), src[e, half]).then_inc(w_in[c % RING], 16)
                        c += 1
                return c

            def load_down(layer, e, c, waits):
                for half in range(2):
                    waits(c)
                    src = I["moe_w_down_2"][layer].rearrange("e (k p) (g n) -> e g p k n", p=P, g=2)
                    sp.dma_start(slot(c, KG, BANK), src[e, half]).then_inc(w_in[c % RING], 16)
                    c += 1
                return c

            def experts(layer):
                c0 = len(freed)
                used0 = seen.now(w_used)
                gu0, d0 = layer * NE, layer * NE
                order = []
                for e in range(NE + 1):
                    if e < NE:
                        order += [("w", e), ("w", e), ("w", e), ("gu", e)]
                    if e > 0:
                        order += [("w", e - 1), ("d", e - 1)]
                used = used0
                for kind, e in order:
                    if kind == "w":
                        used += 1
                        freed.append((w_used, used, 8))
                    elif kind == "gu":
                        freed.append((gu_ready, gu0 + e + 1, 2))
                    else:
                        freed.append((d_ready, d0 + e + 1, 2))
                seen.next(w_used, used - used0)
                c = load_gate_up(layer, 0, c0, lambda c: take_slot(c))
                c = load_gate_up(layer, 1, c, lambda c: take_slot(c))
                c = load_down(layer, 0, c, lambda c: take_slot(c))
                c = load_gate_up(layer, 2, c, lambda c: take_slot(c))
                c = load_down(layer, 1, c, lambda c: take_slot(c))
                with sp.Fori(0, 14) as i:
                    k = load_gate_up(layer, 2 * i + 3, c, lambda c: take_slot(c, i, True))
                    k = load_down(layer, 2 * i + 2, k, lambda c: take_slot(c, i, True))
                    k = load_gate_up(layer, 2 * i + 4, k, lambda c: take_slot(c, i, True))
                    load_down(layer, 2 * i + 3, k, lambda c: take_slot(c, i, True))
                c += 14 * 12
                c = load_gate_up(layer, NE - 1, c, lambda c: take_slot(c))
                c = load_down(layer, NE - 2, c, lambda c: take_slot(c))
                load_down(layer, NE - 1, c, lambda c: take_slot(c))

                over, n_over = ov[layer], all_tiles[layer] * P * 2 // CAP
                sp.wait_ge(route_ready, layer + 1)
                some = sp.value_load(route_i[0:1, 0:1], min_val=0, max_val=n_over)
                with sp.If(some > 0):
                    sp.wait_ge(d_ready, (layer + 1) * NE)
                    with sp.Fori(0, n_over) as j:
                        e = sp.value_load(route_i[0:1, bass.ds(j + 1, 1)], min_val=0, max_val=NE - 1)
                        for n, name in enumerate(("moe_w_gate_2", "moe_w_up_2")):
                            src = I[name][layer].rearrange("e (g k p) n -> e g p k n", p=P, k=KG)
                            for half in range(2):
                                sp.dma_start(slot(2 * n + half, KG, BANK),
                                             src[bass.ds(e, 1), half][0]).then_inc(over["w_in"], 16)
                        src = I["moe_w_down_2"][layer].rearrange("e (k p) (g n) -> e g p k n", p=P, g=2)
                        for half in range(2):
                            sp.dma_start(over_down(half),
                                         src[bass.ds(e, 1), half][0]).then_inc(over["w_in"], 16)
                        sp.wait_ge(over["down"], counted(sp, j + 1))

            sp.dma_start(C[:], I["constants"]).then_inc(const_in, 16)
            sp.dma_start(V[:], I["vectors"]).then_inc(const_in, 16)
            sp.dma_start(posi[:], I["positions"]).then_inc(const_in, 16)
            sp.dma_start(H[:, :LT * D].rearrange("p (t d) -> p t d", t=LT),
                         I["x"][0].rearrange("(t p) d -> p t d", p=P)).then_inc(vec_in, 16)
            sp.dma_start(H[:, LT * D:].rearrange("p (t d) -> p t d", t=CT),
                         I["ctx_2"][0].rearrange("(t p) d -> p t d", p=P)).then_inc(vec_in, 16)
            for g in STREAM:
                if isinstance(g, tuple):
                    experts(g[1])
                else:
                    stream(g)
            sp.wait_ge(final_ready, 1)
            for t in range(LT):
                sp.dma_start(out[0, t * P:(t + 1) * P, :], y_tile(t)).then_inc(result_out, 16)
            sp.wait_ge(result_out, 16 * LT)

        @block.tensor
        def _(pe):
            seen, made = Tally(), Tally()
            chunk = [0]

            def next_chunk(i=0, per_turn=0):
                c = chunk[0]
                pe.wait_ge(w_in[c % RING], 16 * (c // RING + 1) + 16 * (per_turn // RING) * i)
                chunk[0] += 1
                return c

            def acc_bank():
                n = made.next(acc_ready) - 1
                if n >= 4:
                    pe.wait_ge(acc_used, n - 3)
                return ps[n % 4]

            def tr_bank():
                n = made.next(tr_ready) - 1
                if n >= 4:
                    pe.wait_ge(tr_used, n - 3)
                return ps[4 + n % 4]

            def copied():
                pe.wait_ge(tr_used, made.now(tr_ready))

            def group(g, lhs, banks, c, s, k0, kn, width):
                pe.wait_ge(high_ready, s + 1)
                wh, wl = high(s, kn, width), slot(c, kn, width, ring_r)
                for t in range(g.tiles):
                    if k0 == 0:
                        banks.append(acc_bank())
                    for k in range(kn):
                        xh, xl = lhs(k0 + k, t)
                        nc.tensor.matmul(banks[t][:, 0:width], xh, wh[:, k, :], start=k0 + k == 0, stop=False)
                        nc.tensor.matmul(banks[t][:, 0:width], xl, wh[:, k, :], start=False, stop=False)
                pe.wait_ge(low_ready, s + 1)
                for t in range(g.tiles):
                    for k in range(kn):
                        last = nc.tensor.matmul(banks[t][:, 0:width], lhs(k0 + k, t)[0], wl[:, k, :],
                                                start=False, stop=k0 + k == g.k_tiles - 1)
                    if k0 + kn == g.k_tiles:
                        last.then_inc(acc_ready, 1)
                if k0 + kn < g.k_tiles:
                    last.then_inc(w_used, 1)

            def product(g, lhs, after=None, m=P):
                for n, (col, width) in enumerate(g.chunks):
                    banks = []
                    for i, (k0, kn) in enumerate(g.groups):
                        if g.split:
                            group(g, lhs, banks, chunk[0], g.first_split + n * len(g.groups) + i, k0, kn, width)
                            chunk[0] += 1
                            continue
                        c = next_chunk()
                        w = slot(c, kn, width)
                        for t in range(g.tiles):
                            if k0 == 0:
                                banks.append(acc_bank())
                            for k in range(kn):
                                last = nc.tensor.matmul(banks[t][0:m, 0:width], lhs(k0 + k, t), w[:, k, :],
                                                        start=k0 + k == 0, stop=k0 + k == g.k_tiles - 1)
                            if k0 + kn == g.k_tiles:
                                last.then_inc(acc_ready, 1)
                        if k0 + kn < g.k_tiles:
                            last.then_inc(w_used, 1)
                    if after is not None and n > 0:
                        after(n - 1, made.now(acc_ready) - g.tiles)
                if after is not None:
                    after(len(g.chunks) - 1, made.now(acc_ready))

            def transposes(srcs, m=P):
                bank = tr_bank()
                for n, src in enumerate(srcs):
                    last = nc.tensor.transpose(bank[0:m, n * P:(n + 1) * P], src, ident)
                last.then_inc(tr_ready, 1)

            def turn_rows(tiles, k_tiles=KD):
                for t in range(tiles):
                    pe.wait_ge(src_ready, seen.next(src_ready))
                    for k in range(0, k_tiles, 4):
                        transposes([rows(t)[:, j * P:(j + 1) * P] for j in range(k, min(k + 4, k_tiles))])

            def turn_chunk(tiles, wanted):
                def after(n, done):
                    if wanted(n):
                        for t in range(tiles):
                            pe.wait_ge(acc_used, done - tiles + t + 1)
                            src = hs[:, (n * tiles + t) % 4 * BANK:((n * tiles + t) % 4 + 1) * BANK]
                            transposes([src[:, j * P:(j + 1) * P] for j in range(4)])
                return after

            def two_tiles(kt, t):
                return xT(kt, t, LT)

            def two_split(kt, t):
                a = (kt * LT + t) * P
                return XT_r[:, a:a + P], XT_r[:, 2048 + a:2048 + a + P]

            def x_early(kt, t):
                a = (kt * MAX_TILES + t) * P
                return XT_r[:, a:a + P], Y_r[:, a:a + P]

            def x_late(kt, t):
                a = (kt * MAX_TILES + t) * P
                return XT_r[:, a:a + P], A_r[:, XL + a:XL + a + P]

            def attention(units):
                base = {s.name: made.now(s) for s in (s_ready, pT_ready, o_ready)}
                n_held = held(units)
                pe.wait_ge(acc_used, made.now(acc_ready))
                pe.wait_ge(tr_used, made.now(tr_ready))

                def scores(u):
                    unit = units[u]
                    if u >= n_held:
                        pe.wait_ge(exp_ready, base[s_ready.name] + u - n_held + 1)
                    if unit.bias == "dil" and unit.tile == 0:
                        s = bias_in[unit.head % 2]
                        pe.wait_ge(s, seen.next(s, 16))
                    if unit.bias == "na":
                        pe.wait_ge(bias_ready, seen.next(bias_ready))
                    for parts in unit.maps:
                        for col, n, q, k, turn, bias in parts:
                            dst = unit.scores[:, col:col + n]
                            last = nc.tensor.matmul(dst, q, k, start=True, stop=bias is None)
                            if bias is not None:
                                last = nc.tensor.matmul(dst, turn, bias, start=False, stop=True)
                    last.then_inc(s_ready, 1)
                    made.next(s_ready)

                def values(u):
                    unit = units[u]
                    pe.wait_ge(pTs_ready, base[pT_ready.name] + u + 1)
                    if u >= 2:
                        pe.wait_ge(o_used, base[o_ready.name] + u - 1)
                    src = unit.pT
                    for k, v in enumerate(unit.values):
                        last = nc.tensor.matmul(ps[6 + u % 2][:, 0:unit.width], src[:, k * P:(k + 1) * P], v,
                                                start=k == 0, stop=k == len(unit.values) - 1)
                    last.then_inc(o_ready, 1)
                    made.next(o_ready)

                def turn_probs(u):
                    unit = units[u]
                    pe.wait_ge(exp_ready, base[s_ready.name] + u + 1)
                    if unit.kind == "diff":
                        pe.wait_ge(p_ready, seen.next(p_ready))
                    places = 1 if wide(units) else 2
                    if u >= places:
                        pe.wait_ge(pTs_ready, base[pT_ready.name] + u - places + 1)
                    for k in range(len(unit.values)):
                        last = nc.tensor.transpose(turned_probs(units, u)[:, k * P:(k + 1) * P],
                                                   unit.probs[:, k * P:(k + 1) * P], ident)
                    last.then_inc(pT_ready, 1)
                    made.next(pT_ready)

                ahead = n_held - 1
                for u in range(ahead):
                    scores(u)
                for u in range(len(units)):
                    if u + ahead < len(units):
                        scores(u + ahead)
                    if u >= 1 and wide(units):
                        values(u - 1)
                    turn_probs(u)
                    if u >= 1 and not wide(units):
                        values(u - 1)
                values(len(units) - 1)
                pe.wait_ge(o_used, made.now(o_ready))

            def experts(layer):
                tiles = all_tiles[layer]
                pe.wait_ge(acc_used, made.now(acc_ready))
                pe.wait_ge(tr_used, made.now(tr_ready))
                b = layer * NE

                def waiting_turn(dst, src):
                    return nc.tensor.matmul(dst, src, ident[0:CAP, 0:CAP], start=True, stop=True)

                def turn_x(e, i):
                    par = e % 2
                    pe.wait_ge(xs_in[par], counted(pe, 16 * (layer * NE // 2 + e // 2 + 1) + 16 * i))
                    if e >= 1:
                        pe.wait_ge(xg_ready, b + e + 2 * i)
                    last = waiting_turn(ps[4][:, 0:CAP], A[0:CAP, E_X + par * D:E_X + par * D + P])
                    for k in range(1, KD):
                        last = nc.tensor.transpose(ps[4][:, k * CAP:(k + 1) * CAP],
                                                   A[0:CAP, E_X + par * D + k * P:E_X + par * D + (k + 1) * P],
                                                   ident[0:CAP, 0:CAP])
                    last.then_inc(xt_ready, 1)

                def halves(bank, kt):
                    return bank[kt % 2 * CAP:(kt % 2 + 1) * CAP, :]

                def gate_up(e, m, i, per_turn):
                    par = e % 2
                    if m == 0:
                        pe.wait_ge(xg_ready, b + e + 1 + 2 * i)
                        if e >= 1:
                            pe.wait_ge(summed, b + e + 2 * i)
                    for half in range(2):
                        w = slot(next_chunk(i, per_turn), KG, BANK)
                        for k in range(KG):
                            kt = half * KG + k
                            x = A[:, E_XG + par * 512 + kt * CAP:E_XG + par * 512 + (kt + 1) * CAP]
                            last = nc.tensor.matmul(halves(ps[m], kt), x, w[:, k, :], start=kt < 2, stop=kt >= KD - 2)
                        last.then_inc(gu_ready if m == 1 and half == 1 else w_used, 1)

                def turn_hidden(e, i):
                    par = e % 2
                    pe.wait_ge(hd_ready, counted(pe, b + e + 1 + 2 * i))
                    last = waiting_turn(ps[5][:, 0:CAP], A[0:CAP, E_HD + par * 512:E_HD + par * 512 + P])
                    for k in range(1, 4):
                        last = nc.tensor.transpose(ps[5][:, k * CAP:(k + 1) * CAP],
                                                   A[0:CAP, E_HD + par * 512 + k * P:E_HD + par * 512 + (k + 1) * P],
                                                   ident[0:CAP, 0:CAP])
                    last.then_inc(hT_ready, 1)

                def down(e, i, per_turn):
                    par = e % 2
                    pe.wait_ge(hTs_ready, b + e + 1 + 2 * i)
                    if e >= 1:
                        pe.wait_ge(y_ready, b + e + 2 * i)
                    for half in range(2):
                        w = slot(next_chunk(i, per_turn), KG, BANK)
                        for k in range(4):
                            h = A[:, E_HT + par * 256 + k * CAP:E_HT + par * 256 + (k + 1) * CAP]
                            last = nc.tensor.matmul(halves(ps[2 + half], k), h, w[:, k, :], start=k < 2, stop=k >= 2)
                        last.then_inc(d_ready if half == 1 else w_used, 1)

                def stage(e, i, per_turn):
                    gate_up(e, 0, i, per_turn)
                    turn_hidden(e - 1, i)
                    gate_up(e, 1, i, per_turn)
                    if e < NE - 1:
                        turn_x(e + 1, i)
                    down(e - 1, i, per_turn)

                turn_x(0, 0)
                gate_up(0, 0, 0, 0)
                gate_up(0, 1, 0, 0)
                turn_x(1, 0)
                stage(1, 0, 0)
                stage(2, 0, 0)
                c0 = chunk[0]
                with pe.Fori(0, 14) as i:
                    stage(3, i, 12)
                    stage(4, i, 12)
                chunk[0] = c0 + 14 * 12
                stage(NE - 1, 0, 0)
                turn_hidden(NE - 1, 0)
                down(NE - 1, 0, 0)
                pe.wait_ge(y_ready, b + NE)
                made.next(w_used, 4 * NE)

                over, n_over = ov[layer], tiles * P * 2 // CAP
                pe.wait_ge(route_ready, layer + 1)
                some = pe.value_load(route_i[0:1, 0:1], min_val=0, max_val=n_over)
                with pe.If(some > 0):
                    with pe.Fori(0, n_over) as j:
                        pe.wait_ge(over["x_in"], counted(pe, 16 * j + 16))
                        last = waiting_turn(ps[4][:, 0:CAP], A[0:CAP, E_X:E_X + P])
                        for k in range(1, KD):
                            last = nc.tensor.transpose(ps[4][:, k * CAP:(k + 1) * CAP],
                                                       A[0:CAP, E_X + k * P:E_X + (k + 1) * P], ident[0:CAP, 0:CAP])
                        last.then_inc(over["xT"], 1)
                        pe.wait_ge(over["xT_copied"], j + 1)
                        pe.wait_ge(over["w_in"], 96 * j + 96)
                        for m in range(2):
                            for kt in range(KD):
                                w = slot(2 * m + kt // KG, KG, BANK)
                                last = nc.tensor.matmul(halves(ps[m], kt), A[:, E_XG + kt * CAP:E_XG + (kt + 1) * CAP],
                                                        w[:, kt % KG, :], start=kt < 2, stop=kt >= KD - 2)
                        last.then_inc(over["gate_up"], 1)
                        pe.wait_ge(over["hidden"], counted(pe, j + 1))
                        last = waiting_turn(ps[5][:, 0:CAP], A[0:CAP, E_HD:E_HD + P])
                        for k in range(1, 4):
                            last = nc.tensor.transpose(ps[5][:, k * CAP:(k + 1) * CAP],
                                                       A[0:CAP, E_HD + k * P:E_HD + (k + 1) * P], ident[0:CAP, 0:CAP])
                        last.then_inc(over["hiddenT"], 1)
                        pe.wait_ge(over["hiddenT_copied"], j + 1)
                        for half in range(2):
                            w = over_down(half)
                            for k in range(4):
                                last = nc.tensor.matmul(halves(ps[2 + half], k),
                                                        A[:, E_HT + k * CAP:E_HT + (k + 1) * CAP],
                                                        w[:, k, :], start=k < 2, stop=k >= 2)
                        last.then_inc(over["down"], 1)
                        pe.wait_ge(over["y_copied"], j + 1)

            pe.wait_ge(const_in, 48)
            pe.wait_ge(src_ready, seen.next(src_ready))
            for g in range(DIL_G):
                bank = tr_bank()
                nc.tensor.matmul(bank[0:DIL_H, 0:BIAS_LEN], A[0:64, 256 + g * DIL_H:256 + (g + 1) * DIL_H],
                                 A[0:64, 512 + g * BIAS_LEN:512 + (g + 1) * BIAS_LEN],
                                 start=True, stop=True).then_inc(tr_ready, 1)

            turn_rows(LT)
            copied()
            product(g_mla_a, two_tiles)
            turn_rows(LT, MLA_QR // P)
            turn_rows(LT, MLA_KVR // P)
            copied()
            product(g_uq, lambda kt, t: XT[:, 2048 + (kt * LT + t) * P:2048 + (kt * LT + t + 1) * P])
            product(g_ukv, lambda kt, t: XT[:, 2816 + (kt * LT + t) * P:2816 + (kt * LT + t + 1) * P])
            for place in (QROW, KROW):
                pe.wait_ge(src_ready, seen.next(src_ready))
                for t in range(LT):
                    for h in range(0, MLA_H, 4):
                        row = ar(place + t * MLA_H * MLA_DK, MLA_H * MLA_DK)
                        transposes([row[:, (h + j) * MLA_DK:(h + j + 1) * MLA_DK] for j in range(4)], m=MLA_DK)
            attention(mla_units())

            def close_block(i, g_o):
                turn_rows(LT)
                copied()
                product(g_o, two_split)
                turn_rows(LT)
                copied()

                def turn_hidden(n, done):
                    pe.wait_ge(acc_used, done)
                    transposes([hs[:, (n % 2 * 2 + t) * BANK + k * P:(n % 2 * 2 + t) * BANK + (k + 1) * P]
                                for k in range(2) for t in range(LT)])
                product(g_ff_in[i], two_split, turn_hidden)
                copied()
                product(g_ff_out[i], lambda kt, t: [A_r[:, a + (kt * LT + t) * P:a + (kt * LT + t + 1) * P]
                                                     for a in (HT, HL)])
                turn_rows(LT)
                copied()
                product(g_ple_g[i], two_split)
                pe.wait_ge(src_ready, seen.next(src_ready))
                product(g_ple_p[i], lambda kt, t: A[:, PLE + kt * SEQ + t * P:PLE + kt * SEQ + (t + 1) * P])

            close_block(0, g_mla_o)

            turn_rows(LT)
            copied()
            product(g_dil, two_split, turn_chunk(LT, lambda n: n % 6 < 4))
            attention(dil_units())
            close_block(1, g_dil_o)

            for i in range(DEPTH):
                tiles = all_tiles[i]
                pe.wait_ge(src_ready, seen.next(src_ready))

                def spread_ada(n, done):
                    pe.wait_ge(acc_used, done)
                    row = ada_row[0:2, n % 2 * BANK:(n % 2 + 1) * BANK]
                    if n // 2 in (2, 5):
                        for j in range(2):
                            bank = tr_bank()
                            nc.tensor.matmul(bank[:, :], C[0:2, C_SEL + j * P:C_SEL + (j + 1) * P], row,
                                             start=True, stop=True).then_inc(tr_ready, 1)
                    else:
                        bank = tr_bank()
                        for j in range(4):
                            last = nc.tensor.transpose(bank[:, 2 * j:2 * j + 2], row[:, j * P:(j + 1) * P],
                                                       ident[0:2, 0:2])
                        last.then_inc(tr_ready, 1)
                product(g_ada[i], lambda kt, t: small[:, 128 + 2 * kt:130 + 2 * kt], spread_ada, m=2)
                turn_rows(MAX_TILES)
                copied()
                product(g_kv[i], x_early, turn_chunk(MAX_TILES, lambda n: n in (0, 2)))
                product(g_qz[i], x_early, turn_chunk(tiles, lambda n: n < 2))
                for t in range(tiles):
                    pe.wait_ge(src_ready, seen.next(src_ready))
                    bank = tr_bank()
                    for g in range(4):
                        last = nc.tensor.matmul(bank[:, g * P:(g + 1) * P], ar(SG_W + g * P, P),
                                                ar(VV + t * 512 + g * P, P), start=True, stop=True)
                    last.then_inc(tr_ready, 1)
                for units in second_units(i):
                    attention(units)
                for t in range(tiles):
                    for b in range(3):
                        pe.wait_ge(src_ready, seen.next(src_ready))
                        transposes([ar((YA, U, YC)[b] + t * 512 + j * P, P) for j in range(4)])
                copied()
                pe.wait_ge(low_back, 16 * (i + 1))
                for n in range(6):
                    b = n % 3
                    product(g_gate[i][n], x_late)
                    product(g_branch[i][n], lambda kt, t, b=b: ar(YT + ((b * 4 + kt) * MAX_TILES + t) * P, P))
                turn_rows(tiles)
                copied()
                product(g_out[i], x_late)
                turn_rows(tiles)
                copied()
                for t in range(tiles):
                    for g in range(2):
                        transposes([xT(4 * g + j, t) for j in range(4)])
                pe.wait_ge(src_ready, seen.next(src_ready))
                bank = tr_bank()
                for t in range(tiles):
                    for kt in range(KD):
                        last = nc.tensor.matmul(bank[:, t * 36:(t + 1) * 36], xT(kt, t),
                                                ar(ROUTER + kt * 36, 36), start=kt == 0, stop=kt == KD - 1)
                last.then_inc(tr_ready, 1)
                pe.wait_ge(src_ready, seen.next(src_ready))
                bank = tr_bank()
                for t in range(tiles + 1):
                    for before in range(t):
                        last = nc.tensor.matmul(bank[:, t * NE:(t + 1) * NE], ones[:, :],
                                                ar(RT + before * NE, NE), start=before == 0,
                                                stop=t == tiles and before == t - 1)
                    if t < tiles:
                        last = nc.tensor.matmul(bank[:, t * NE:(t + 1) * NE], upper, ar(RT + t * NE, NE),
                                                start=t == 0, stop=True)
                last.then_inc(tr_ready, 1)
                experts(i)

        @block.scalar
        def _(act):
            seen, made = Tally(), Tally()
            steps = [0]
            u_base = [0]

            def link(ins):
                steps[0] += 1
                ins.then_inc(act_step, 1)
                act.wait_ge(act_step, steps[0])

            def answer(dst, src, func, scale=1.0):
                act.wait_ge(act_req, seen.next(act_req))
                nc.scalar.activation(dst, src, func, scale=scale).then_inc(act_rep, 1)

            def roots(n):
                answer(small[:, 32:32 + n], small[:, 16:16 + n], ACT.Sqrt)

            def high_parts(g, n):
                for i, (k0, kn) in enumerate(g.groups):
                    j = n * len(g.groups) + i
                    c, s, width = g.first + j, g.first_split + j, g.chunks[n][1]
                    act.wait_ge(w_in[c % RING], 16 * (c // RING + 1))
                    if high_free[s]:
                        act.wait_ge(*high_free[s])
                    nc.scalar.activation(high(s, kn, width), slot(c, kn, width), ACT.Copy).then_inc(high_ready, 1)

            def all_high_parts(g):
                for n in range(len(g.chunks)):
                    high_parts(g, n)
                seen.next(acc_ready, len(g.chunks) * g.tiles)

            def attention(units):
                base = u_base[0]

                def copy_probs(u):
                    unit = units[u]
                    act.wait_ge(pT_ready, base + u + 1)
                    if u >= 2:
                        act.wait_ge(o_ready, base + u - 1)
                    n = len(unit.values) * P
                    nc.scalar.activation(unit.pT[:, 0:n], turned_probs(units, u)[:, 0:n],
                                         ACT.Copy).then_inc(pTs_ready, 1)

                for u, unit in enumerate(units):
                    act.wait_ge(max_ready, base + u + 1)
                    if u >= held(units):
                        act.wait_ge(pT_ready, base + u - held(units) + 1)
                    for m in range(len(unit.maps)):
                        c = stat(units, u, m)
                        last = nc.scalar.activation(unit.probs[:, m * BANK:m * BANK + unit.n_keys],
                                                    unit.scores[:, m * BANK:m * BANK + unit.n_keys], ACT.Exp,
                                                    bias=small[:, 64 + c:65 + c], scale=unit.scale,
                                                    accum_out=small[:, 80 + c:81 + c])
                    last.then_inc(exp_ready, 1)
                    if u >= 1:
                        copy_probs(u - 1)
                copy_probs(len(units) - 1)
                u_base[0] += len(units)

            def close_block(i, g_o):
                all_high_parts(g_o)
                roots(LT)
                roots(LT)
                n_pieces = D_FF // FF_PIECE
                high_parts(g_ff_in[i], 0)
                for n in range(n_pieces):
                    if n + 1 < n_pieces:
                        high_parts(g_ff_in[i], n + 1)
                    for t in range(LT):
                        a = seen.next(acc_ready)
                        act.wait_ge(acc_ready, a)
                        c = (a - 1) % 4
                        nc.scalar.activation(ada_row[:, c * FF_PIECE:(c + 1) * FF_PIECE], ps[c][:, 0:FF_PIECE],
                                             ACT.Sigmoid).then_inc(sig_ready, 1)
                all_high_parts(g_ff_out[i])
                roots(LT)
                all_high_parts(g_ple_g[i])
                for n in range(2 * LT):
                    answer(ar(PSIG + n * BANK, BANK), ar(PSIG + n * BANK, BANK), ACT.Sigmoid)
                seen.next(acc_ready, 2 * LT)

            answer(ar(TMP + 64, 64), ar(TMP + 64, 64), ACT.Sin)
            roots(LT)
            roots(LT)
            roots(LT)
            seen.next(acc_ready, (2 + 3 + 4) * LT)
            act.wait_ge(zero_out, 32)
            attention(mla_units())
            close_block(0, g_mla_o)
            roots(LT)
            all_high_parts(g_dil)
            attention(dil_units())
            close_block(1, g_dil_o)

            def expert_halves(layer, e, i):
                act.wait_ge(gu_ready, layer * NE + e + 1 + 2 * i)
                if e >= 1:
                    act.wait_ge(summed, layer * NE + e + 2 * i)
                nc.scalar.activation(A[0:CAP, E_UP:E_UP + 2 * BANK], pair[0][CAP:2 * CAP, :],
                                     ACT.Copy).then_inc(halves_ready, 1)

            def expert_sigmoid(layer, e, i):
                act.wait_ge(summed, layer * NE + e + 1 + 2 * i)
                if e >= 1:
                    act.wait_ge(hd_ready, layer * NE + e + 2 * i)
                nc.scalar.activation(A[0:CAP, E_SG:E_SG + 512], A[0:CAP, E_SUM:E_SUM + 512],
                                     ACT.Sigmoid).then_inc(esig_ready, 1)

            def expert_y(layer, e, i):
                act.wait_ge(d_ready, layer * NE + e + 1 + 2 * i)
                if e >= 1:
                    act.wait_ge(y_ready, layer * NE + e + 2 * i)
                nc.scalar.activation(A[0:CAP, E_YR:E_YR + D], pair[1][CAP:2 * CAP, :],
                                     ACT.Copy).then_inc(y_half, 1)

            def expert_stage(layer, e, i):
                expert_halves(layer, e, i)
                expert_sigmoid(layer, e, i)
                expert_y(layer, e - 1, i)

            for layer in range(DEPTH):
                tiles = all_tiles[layer]
                if layer == 0:
                    answer(small[:, 144:160], V[:, V_COND:V_COND + 16], ACT.Sigmoid)
                answer(small[:, 98:100], small[:, 98:100], ACT.Exp)
                high_parts(g_kv[layer], 0)
                roots(MAX_TILES)
                for n in range(1, 4):
                    high_parts(g_kv[layer], n)
                for n in range(4):
                    high_parts(g_qz[layer], n)
                for u in range(2 * tiles):
                    y = rows(1)[:, u % 2 * BANK:(u % 2 + 1) * BANK]
                    count = g_qz[layer].ends[-1][1] - 2 * tiles + u
                    answer(y, ps[count % 4], ACT.Square)
                    answer(y, y, ACT.Sigmoid)
                roots(tiles)
                high_parts(g_gate[layer][0], 0)
                act.wait_ge(low_saved, 16 * (layer + 1))
                for units in second_units(layer):
                    attention(units)
                roots(4 * tiles)
                for n in range(6):
                    high_parts(g_gate[layer][n + 1] if n < 5 else g_out[layer], 0)
                    for t in range(tiles):
                        answer(ar(MERGED_SIG + t * 512, BANK), ar(MERGED_SIG + t * 512, BANK), ACT.Sigmoid)
                high_parts(g_out[layer], 1)
                roots(tiles)
                answer(ar(RT + 128, tiles * 4), ar(RT + 128, tiles * 4), ACT.Exp)
                answer(small[:, 104:104 + tiles], small[:, 104:104 + tiles], ACT.Exp)
                expert_halves(layer, 0, 0)
                expert_sigmoid(layer, 0, 0)
                expert_stage(layer, 1, 0)
                expert_stage(layer, 2, 0)
                with act.Fori(0, 14) as i:
                    expert_stage(layer, 3, i)
                    expert_stage(layer, 4, i)
                expert_stage(layer, NE - 1, 0)
                expert_y(layer, NE - 1, 0)
                over, n_over = ov[layer], tiles * P * 2 // CAP
                act.wait_ge(route_ready, layer + 1)
                some = act.value_load(route_i[0:1, 0:1], min_val=0, max_val=n_over)
                with act.If(some > 0):
                    with act.Fori(0, n_over) as j:
                        act.wait_ge(over["gate_up"], j + 1)
                        nc.scalar.activation(A[0:CAP, E_UP:E_UP + 2 * BANK], pair[0][CAP:2 * CAP, :],
                                             ACT.Copy).then_inc(over["halves"], 1)
                        act.wait_ge(over["summed"], j + 1)
                        nc.scalar.activation(A[0:CAP, E_SG:E_SG + 512], A[0:CAP, E_SUM:E_SUM + 512],
                                             ACT.Sigmoid).then_inc(over["sigmoid"], 1)
                        act.wait_ge(over["down"], j + 1)
                        nc.scalar.activation(A[0:CAP, E_YR:E_YR + D], pair[1][CAP:2 * CAP, :],
                                             ACT.Copy).then_inc(over["y_half"], 1)
                        act.wait_ge(over["y_out"], 16 * j + 16)
            roots(LT)

        @block.gpsimd
        def _(pool):
            seen = Tally()
            u_base, loads = [0], [2]

            def load(dst, src):
                pool.wait_ge(misc_ask, seen.next(misc_ask))
                nc.gpsimd.dma_start(dst, src).then_inc(misc_in[loads[0] % 4], 16)
                loads[0] += 1

            def row(src, width=D, at=0):
                load(brow[:, at:at + width], src.partition_broadcast(P))

            pool.wait_ge(misc_ask, seen.next(misc_ask))
            nc.gpsimd.dma_start(A[0:BUCKETS, 256:256 + DIL_G * DIL_H], I["rel_bias"]).then_inc(misc_in[0], 16)
            nc.gpsimd.dma_start(A[0:64, 512:512 + DIL_G * BIAS_LEN], I["hot"]).then_inc(misc_in[1], 16)
            for l in range(DEPTH):
                nc.gpsimd.dma_start(A[0:NA_H * RPB_R, l * P + 48:l * P + 48 + RPB_C],
                                    I["na_rpb_2"][l].rearrange("h a c -> (h a) c")).then_inc(pool_step, 16)
            pool.wait_ge(pool_step, 32)
            for l in range(DEPTH):
                nc.gpsimd.dma_start(rpb_dram[l], A[0:NA_H * RPB_R, l * P:l * P + RPB_W]).then_inc(scratch_out, 16)
            nc.gpsimd.dma_start(xs_dram.rearrange("(r p) d -> p r d", p=P),
                                Y[:, 2048:2048 + D].unsqueeze(1).broadcast_to([P, xs_dram.shape[0] // P, D])
                                ).then_inc(zero_out, 16)
            nc.gpsimd.dma_start(ys_dram[NE * CAP:, :].rearrange("(r p) d -> p r d", p=P),
                                Y[:, 2048:2048 + D].unsqueeze(1).broadcast_to([P, MAX_OVER * CAP // P, D])
                                ).then_inc(zero_out, 16)
            pool.wait_ge(misc_ask, seen.next(misc_ask))
            for g in range(DIL_G):
                nc.gpsimd.dma_start(rel_dram[g * DIL_H:(g + 1) * DIL_H, :],
                                    A[0:DIL_H, 3072 + g * BIAS_LEN:3072 + (g + 1) * BIAS_LEN]).then_inc(scratch_out, 16)
            pool.wait_ge(scratch_out, 16 * (DEPTH + DIL_G))

            def low_parts(g, only=None):
                for n, (_, width) in enumerate(g.chunks):
                    if only is not None and n not in only:
                        continue
                    for i, (k0, kn) in enumerate(g.groups):
                        j = n * len(g.groups) + i
                        c, s = g.first + j, g.first_split + j
                        pool.wait_ge(high_ready, s + 1)
                        nc.gpsimd.tensor_tensor(slot(c, kn, width, ring_r), slot(c, kn, width),
                                                high(s, kn, width), ALU.subtract).then_inc(low_ready, 1)

            def close_block(i, g_o):
                low_parts(g_o)
                row(I["norm_g"][i, 3])
                load(ar(PLE, 512).rearrange("p (k t) -> p k t", k=2), I["p_t"][i].rearrange("(k p) t -> p k t", p=P))
                low_parts(g_ff_in[i])
                low_parts(g_ff_out[i])
                if i == 0:
                    row(I["norm_g"][1, 1])
                low_parts(g_ple_g[i])

            u_base[0] += 2 * MLA_H
            row(I["norm_g"][0, 1])
            close_block(0, g_mla_o)
            low_parts(g_dil)
            for h in range(DIL_H):
                if h >= 2:
                    pool.wait_ge(s_ready, u_base[0] + 2 * (h - 1))
                else:
                    pool.wait_ge(misc_ask, seen.next(misc_ask))
                dst = XT[:, 2048 + h % 2 * 768:2048 + h % 2 * 768 + 768].rearrange("p (g c) -> p g c", g=DIL_G)
                src = bass.AP(tensor=rel_dram.tensor, offset=h * BIAS_LEN,
                              ap=[[1, P], [DIL_H * BIAS_LEN, DIL_G], [1, 2 * P]])
                nc.gpsimd.dma_start(dst, src).then_inc(bias_in[h % 2], 16)
            u_base[0] += 2 * DIL_H
            close_block(1, g_dil_o)

            for layer in range(DEPTH):
                tiles = all_tiles[layer]
                load(A[0:2, 0:6 * D], I["b_ada_2"][layer].partition_broadcast(2))
                row(I["da_lambda_2"][layer].rearrange("a b -> (a b)"), 256)
                low_parts(g_kv[layer], [0])
                pool.wait_ge(x_ready, layer + 1)
                nc.gpsimd.dma_start(low_dram, Y_r[:, :]).then_inc(low_saved, 16)
                low_parts(g_kv[layer], [1, 2, 3])
                low_parts(g_qz[layer])
                row(I["sg_ln_g_2"][layer], 512)
                row(I["sg_ln_b_2"][layer], 512, 512)
                load(ar(SG_W, 512).rearrange("q (g p) -> q g p", g=4), I["sg_wt"][layer].rearrange("g q p -> q g p"))
                low_parts(g_gate[layer][0])
                n_diff = 4 * tiles
                pool.wait_ge(low_saved, 16 * (layer + 1))
                for h in range(NA_H):
                    for t in range(LT):
                        if h == 0 and t == 0:
                            pool.wait_ge(misc_ask, seen.next(misc_ask))
                        elif h >= 4:
                            pool.wait_ge(s_ready, u_base[0] + n_diff + (h - 4) * tiles + t + 1)
                        for half in range(2):
                            dst = na_bias(h, t)[half * 64:(half + 1) * 64, :]
                            src = bass.AP(tensor=rpb_dram.tensor,
                                          offset=((layer * NA_H + h) * RPB_R + 6 - 2 * t + half) * RPB_W,
                                          ap=[[1, 64], [RPB_W, 4], [1, 64]])
                            nc.gpsimd.dma_start(dst.rearrange("p (r c) -> p r c", r=4), src).then_inc(
                                na_bias_in[h % 4 * LT + t], 16)
                u_base[0] += n_diff + NA_H * tiles
                pool.wait_ge(o_ready, u_base[0])
                nc.gpsimd.dma_start(A_r[:, XL:XL + KD * MAX_TILES * P], low_dram).then_inc(low_back, 16)
                row(I["da_subln_g_2"][layer], P)
                low_parts(g_gate[layer][1])
                load(ar(ROUTER, 36 * KD).rearrange("p (k n) -> p k n", k=KD), I["router_w"][layer].rearrange("(k p) n -> p k n", p=P))
                load(vrow[:, 0:36], I["router_b"][layer].partition_broadcast(P))
                for n in range(2, 6):
                    low_parts(g_gate[layer][n])
                low_parts(g_out[layer])
                pool.wait_ge(route_ready, layer + 1)
                if layer == 0:
                    pool.wait_ge(zero_out, 32)
                for t in range(tiles):
                    for k in range(2):
                        c = k * MAX_TILES + t
                        nc.gpsimd.indirect_dma_start(
                            out=xs_dram[:, :], out_offset=bass.IndirectOffsetOnAxis(ap=route_u[:, c:c + 1], axis=0),
                            in_=ar(XTOK + t * D, D), in_offset=None).then_inc(scatter_out, 16)
                pool.wait_ge(scatter_out, 16 * 2 * sum(all_tiles[:layer + 1]))
                b = layer * NE

                def fetch(e, i):
                    par = e % 2
                    if e >= 2:
                        pool.wait_ge(xt_ready, counted(pool, b + e - 1 + 2 * i))
                    nc.gpsimd.dma_start(A[0:CAP, E_X + par * D:E_X + (par + 1) * D],
                                        xs_dram.rearrange("(b s) d -> b s d", s=CAP)[e + 2 * i]
                                        if isinstance(i, int) else
                                        xs_dram.rearrange("(b s) d -> b s d", s=CAP)[bass.ds(2 * i + e, 1)][0]
                                        ).then_inc(xs_in[par], 16)

                def store(e, i):
                    par = e % 2
                    pool.wait_ge(y_ready, counted(pool, b + e + 1 + 2 * i))
                    nc.gpsimd.dma_start(ys_dram.rearrange("(b s) d -> b s d", s=CAP)[e + 2 * i]
                                        if isinstance(i, int) else
                                        ys_dram.rearrange("(b s) d -> b s d", s=CAP)[bass.ds(2 * i + e, 1)][0],
                                        A[0:CAP, E_Y + par * D:E_Y + (par + 1) * D]).then_inc(ys_out[par], 16)

                fetch(0, 0)
                fetch(1, 0)
                for e in (1, 2):
                    fetch(e + 1, 0)
                    store(e - 1, 0)
                with pool.Fori(0, 14) as i:
                    for e in (3, 4):
                        fetch(e + 1, i)
                        store(e - 1, i)
                store(NE - 2, 0)
                store(NE - 1, 0)
                for par in range(2):
                    pool.wait_ge(ys_out[par], 16 * (layer + 1) * NE // 2)
                over, n_over = ov[layer], tiles * P * 2 // CAP
                some = pool.value_load(route_i[0:1, 0:1], min_val=0, max_val=n_over)
                with pool.If(some > 0):
                    with pool.Fori(0, n_over) as j:
                        nc.gpsimd.dma_start(A[0:CAP, E_X:E_X + D],
                                            xs_dram.rearrange("(b s) d -> b s d", s=CAP)[bass.ds(j + NE, 1)][0]
                                            ).then_inc(over["x_in"], 16)
                        pool.wait_ge(over["y_copied"], counted(pool, j + 1))
                        nc.gpsimd.dma_start(ys_dram[bass.ds(j * CAP + NE * CAP, CAP), :],
                                            A[0:CAP, E_Y:E_Y + D]).then_inc(over["y_out"], 16)
                        pool.wait_ge(over["y_out"], counted(pool, 16 * j + 16))
                for t in range(tiles):
                    if t >= 2:
                        pool.wait_ge(misc_ask, seen.next(misc_ask))
                    for k in range(2):
                        c = k * MAX_TILES + t
                        nc.gpsimd.indirect_dma_start(
                            out=ar(YG + (t % 2 * 2 + k) * D, D), out_offset=None, in_=ys_dram[:, :],
                            in_offset=bass.IndirectOffsetOnAxis(ap=route_u[:, c:c + 1], axis=0)
                        ).then_inc(gather_in[t % 2], 16)
            row(I["g_final_2"])

        @block.vector
        def _(dve):
            seen, made = Tally(), Tally()
            tt, ts, stt = nc.vector.tensor_tensor, nc.vector.tensor_scalar, nc.vector.scalar_tensor_tensor
            copy, red = nc.vector.tensor_copy, nc.vector.tensor_reduce

            def v(ins, signal=dve_step):
                ins.then_inc(signal, 1)
                dve.wait_ge(signal, made.next(signal))

            def started(ins):
                ins.then_inc(dve_step, 1)
                made.next(dve_step)

            def say(signal):
                v(nc.vector.memset(small[:, 255:256], 0.0), signal)

            def product_bank():
                n = seen.next(acc_ready)
                dve.wait_ge(acc_ready, n)
                return ps[(n - 1) % 4]

            def turned_bank():
                n = seen.next(tr_ready)
                dve.wait_ge(tr_ready, n)
                return ps[4 + (n - 1) % 4]

            loads = [0]

            def loaded(n=1):
                for _ in range(n):
                    s = misc_in[loads[0] % 4]
                    dve.wait_ge(s, seen.next(s, 16))
                    loads[0] += 1

            def answered():
                dve.wait_ge(act_rep, seen.next(act_rep))

            def answered_all(n):
                dve.wait_ge(act_rep, seen.next(act_rep, n))

            def spread(col, n, width):
                return col.unsqueeze(2).broadcast_to([P, n, width])

            def square_sum(src, col, width):
                v(nc.vector.tensor_tensor_reduce(out=rows(1)[:, :width], in0=src, in1=src, scale=1.0, scalar=0.0,
                                                 op0=ALU.mult, op1=ALU.add, accum_out=small[:, col:col + 1]))

            def rstd(n, width):
                v(ts(small[:, 16:16 + n], small[:, 0:n], 1.0 / width, EPS, ALU.mult, ALU.add), act_req)
                answered()
                v(nc.vector.reciprocal(small[:, 48:48 + n], small[:, 32:32 + n]))

            def copy_turned(dst):
                bank = turned_bank()
                n = dst.shape[1]
                v(copy(dst, bank[0:dst.shape[0], 0:n * P].rearrange("p (k c) -> p k c", k=n)), tr_used)

            def parts(dst, low, src):
                v(copy(dst, src))
                v(tt(low, src, dst, ALU.subtract), tr_used)

            def turn(tiles, src, dst, k_tiles=KD, scaled=True, gain=None, shift=None, split=None):
                width = k_tiles * P
                for step in range(tiles + 1):
                    if step < tiles:
                        r = rows(step)[:, :width]
                        if scaled:
                            v(ts(r, src(step), small[:, 48 + step:49 + step], None, ALU.mult), src_ready)
                        else:
                            v(copy(r, src(step)), src_ready)
                    if step == 0:
                        continue
                    t = step - 1
                    for g in range(0, k_tiles, 4):
                        n = min(4, k_tiles - g)
                        d = dst(g // 4, t, n)
                        if gain is None and split is None:
                            copy_turned(d)
                            continue
                        bank = turned_bank()[:, 0:n * P].rearrange("p (k c) -> p k c", k=n)
                        if gain is None:
                            parts(*split(g // 4, t, n)[:2], bank)
                            continue
                        x = d if split is None else split(g // 4, t, n)[2]
                        done = dve_step if split is not None else tr_used
                        if shift is None:
                            v(tt(x, bank, spread(gain(t)[:, g:g + n], n, P), ALU.mult), done)
                        for k in range(n if shift is not None else 0):
                            ins = ts(x[:, k, :], bank[:, k, :], gain(t)[:, g + k:g + k + 1],
                                     shift(t)[:, g + k:g + k + 1], ALU.mult, ALU.add)
                            if k < n - 1:
                                started(ins)
                            else:
                                v(ins, done)
                        if split is not None:
                            parts(*split(g // 4, t, n)[:2], x)

            def norm_turn(tiles, src, dst, k_tiles=KD, gain=None, shift=None, split=None):
                for t in range(tiles):
                    square_sum(src(t), t, k_tiles * P)
                rstd(tiles, k_tiles * P)
                turn(tiles, src, dst, k_tiles, True, gain, shift, split)

            def x2(g, t, n):
                return xT4(g, t, LT, n)

            def x2_parts(g, t, n):
                return [m.rearrange("p (k t c) -> p k t c", k=KD, t=LT)[:, 4 * g:4 * g + n, t, :]
                        for m in (XT_r[:, 0:2048], XT_r[:, 2048:], XT[:, 2048:])]

            def x4(g, t, n):
                return xT4(g, t, MAX_TILES, n)

            def x4_parts(low_r, low):
                def places(g, t, n):
                    return [m.rearrange("p (k t c) -> p k t c", k=KD, t=MAX_TILES)[:, 4 * g:4 * g + n, t, :]
                            for m in (XT_r[:, :], low_r, low)]
                return places

            def attention(units):
                def mask_bias(u):
                    unit = units[u]
                    if unit.bias == "na":
                        s = na_bias_in[unit.head % 4 * LT + unit.tile]
                        dve.wait_ge(s, seen.next(s, 32))
                        b = na_bias(unit.head, unit.tile).rearrange("p (r c) -> p r c", r=4)
                        m = C[:, C_NAMASK:C_NAMASK + GRID_W].unsqueeze(1).broadcast_to([P, 4, GRID_W])
                        v(tt(b, b, m, ALU.add), bias_ready)

                def row_max(u):
                    unit = units[u]
                    dve.wait_ge(s_ready, seen.next(s_ready))
                    for m in range(len(unit.maps)):
                        c = 64 + stat(units, u, m)
                        last = m == len(unit.maps) - 1
                        scores = unit.scores[:, m * BANK:m * BANK + unit.n_keys]
                        v(red(small[:, c:c + 1], scores, X, ALU.max, negate=True),
                          max_ready if last and unit.scale == 1.0 else dve_step)
                        if unit.scale != 1.0:
                            v(ts(small[:, c:c + 1], small[:, c:c + 1], unit.scale, None, ALU.mult), max_ready)

                def combine(u):
                    unit = units[u]
                    dve.wait_ge(exp_ready, seen.next(exp_ready))
                    c = 80 + stat(units, u)
                    n = len(unit.maps)
                    v(nc.vector.reciprocal(small[:, c:c + n], small[:, c:c + n]))
                    if unit.kind == "diff":
                        n = unit.n_keys
                        v(tt(small[:, c + 1:c + 2], small[:, c + 1:c + 2], small[:, 96:97], ALU.mult))
                        v(ts(unit.probs[:, BANK:BANK + n], unit.probs[:, BANK:BANK + n], small[:, c + 1:c + 2], None,
                             ALU.mult))
                        v(stt(unit.probs[:, 0:n], unit.probs[:, 0:n], small[:, c:c + 1],
                              unit.probs[:, BANK:BANK + n], ALU.mult, ALU.add), p_ready)

                def finish(u):
                    unit = units[u]
                    dve.wait_ge(o_ready, seen.next(o_ready))
                    src = ps[6 + u % 2][:, 0:unit.width]
                    if unit.kind == "diff":
                        v(copy(unit.dest, src), o_used)
                    else:
                        c = 80 + stat(units, u)
                        v(ts(unit.dest, src, small[:, c:c + 1], None, ALU.mult), o_used)

                ahead = held(units) - 1
                for u in range(ahead + 1):
                    mask_bias(u)
                for u in range(ahead):
                    row_max(u)
                for u in range(len(units)):
                    if u + ahead + 1 < len(units):
                        mask_bias(u + ahead + 1)
                    if u + ahead < len(units):
                        row_max(u + ahead)
                    combine(u)
                    if u >= 1:
                        finish(u - 1)
                finish(len(units) - 1)

            def copy_product(g, dst):
                for n, (_, width) in enumerate(g.chunks):
                    for t in range(g.tiles):
                        bank = product_bank()
                        v(copy(dst(n, t), bank[:, 0:width]), acc_used)

            def residual():
                for t in range(LT):
                    square_sum(y_tile(t), t, D)
                rstd(LT, D)
                loaded()
                for t in range(LT):
                    v(stt(rows(0), y_tile(t), small[:, 48 + t:49 + t], brow[:, :], ALU.mult, ALU.mult))
                    v(tt(h_tile(t), h_tile(t), rows(0), ALU.add))

            def close_block(i, g_o):
                turn(LT, y_tile, x2, scaled=False, split=x2_parts)
                copy_product(g_o, lambda n, t: y_tile(t)[:, n * BANK:(n + 1) * BANK])
                residual()
                say(misc_ask)
                say(misc_ask)
                norm_turn(LT, h_tile, x2, gain=lambda t: V[:, V_NG2 + i * 8:V_NG2 + i * 8 + 8], split=x2_parts)
                n_pieces = D_FF // FF_PIECE
                for n in range(n_pieces + 1):
                    if n < n_pieces:
                        for t in range(LT):
                            c = seen.now(acc_ready) % 4
                            bank = product_bank()
                            dve.wait_ge(sig_ready, seen.next(sig_ready))
                            r = hs[:, (n % 2 * 2 + t) * BANK:]
                            sg = ada_row[:, c * FF_PIECE:(c + 1) * FF_PIECE]
                            v(tt(r[:, FF_PIECE:2 * FF_PIECE], bank[:, 0:FF_PIECE], sg, ALU.mult))
                            v(tt(r[:, 0:FF_PIECE], bank[:, FF_PIECE:2 * FF_PIECE], r[:, FF_PIECE:2 * FF_PIECE],
                                 ALU.mult), acc_used)
                    if n > 0:
                        parts(A_r[:, HT + (n - 1) * 512:HT + n * 512], A_r[:, HL + (n - 1) * 512:HL + n * 512],
                              turned_bank()[:, :])
                copy_product(g_ff_out[i], lambda n, t: y_tile(t)[:, n * BANK:(n + 1) * BANK])
                residual()
                if i == 0:
                    say(misc_ask)
                turn(LT, h_tile, x2, scaled=False, split=x2_parts)
                for n in range(2):
                    for t in range(LT):
                        bank = product_bank()
                        v(copy(ar(PSIG + (n * LT + t) * BANK, BANK), bank[:, :]), acc_used)
                        say(act_req)
                loaded()
                say(src_ready)
                answered_all(2 * LT)
                for n in range(2):
                    for t in range(LT):
                        bank = product_bank()
                        v(tt(rows(0)[:, 0:BANK], bank[:, :], ar(PSIG + (n * LT + t) * BANK, BANK), ALU.mult), acc_used)
                        part = h_tile(t)[:, n * BANK:(n + 1) * BANK]
                        v(tt(part, part, rows(0)[:, 0:BANK], ALU.add))

            v(nc.vector.memset(A[:, 0:256], 0.0))
            v(nc.vector.memset(A[0:64, 256:256 + DIL_G * DIL_H], 0.0))
            v(nc.vector.memset(A[BUCKETS:BUCKETS + 1, 256:256 + DIL_G * DIL_H], 1.0))
            v(nc.vector.memset(ones[:, :], 1.0))
            v(nc.vector.memset(Y[:, 2048:2048 + D], 0.0), misc_ask)
            loaded(2)
            say(src_ready)
            for g in range(DIL_G):
                v(copy(A[0:DIL_H, 3072 + g * BIAS_LEN:3072 + (g + 1) * BIAS_LEN], turned_bank()[0:DIL_H, 0:BIAS_LEN]),
                  tr_used)
            say(misc_ask)
            say(misc_ask)

            dve.wait_ge(const_in, 48)
            pos, ang, n_turns = ar(TMP, 2), ar(TMP + 64, 32), ar(TMP + 32, 32)
            v(copy(pos, posi[:, :]))
            for t in range(LT):
                v(ts(ang[:, t * 16:(t + 1) * 16], C[:, C_INV:C_INV + 16], pos[:, t:t + 1], None, ALU.mult))
            whole = 1.5 * 2.0 ** 23
            v(ts(n_turns, ang, 1.0 / (2 * math.pi), None, ALU.mult))
            v(ts(n_turns, n_turns, whole, None, ALU.add))
            v(ts(n_turns, n_turns, whole, None, ALU.subtract))
            c1 = 6.28125
            c2 = float(np.float32(np.float32((2 * math.pi - c1) * 2 ** 20).astype(np.int32)) * 2.0 ** -20)
            c3 = 2 * math.pi - c1 - c2
            for part in (c1, c2, c3):
                v(stt(ang, n_turns, -part, ang, ALU.mult, ALU.add))
            cosa = ar(TMP + 96, 32)
            v(ts(cosa, ang, math.pi / 2, None, ALU.add))
            v(ts(n_turns, cosa, math.pi, -2 * math.pi, ALU.is_gt, ALU.mult))
            v(tt(cosa, cosa, n_turns, ALU.add))
            pi = 3.1415925
            v(ts(ar(TMP + 64, 64), ar(TMP + 64, 64), pi, -pi, ALU.min, ALU.max), act_req)
            answered()
            dve.wait_ge(vec_in, 32)
            norm_turn(LT, h_tile, x2, gain=lambda t: V[:, V_NG0:V_NG0 + 8])
            dve.wait_ge(scratch_out, 16 * (DEPTH + DIL_G))
            wide = MLA_QR + MLA_KVR + ROT
            copy_product(g_mla_a, lambda n, t: ar(AROW + t * wide + n * BANK, min(BANK, wide - n * BANK)))
            norm_turn(LT, lambda t: ar(AROW + t * wide, MLA_QR),
                      lambda g, t, n: XT[:, 2048:2816].rearrange("p (k t c) -> p k t c", k=3, t=LT)[:, 0:3, t, :],
                      3, gain=lambda t: V[:, V_QN:V_QN + 3])
            norm_turn(LT, lambda t: ar(AROW + t * wide + MLA_QR, MLA_KVR),
                      lambda g, t, n: XT[:, 2816:3328].rearrange("p (k t c) -> p k t c", k=2, t=LT)[:, 0:2, t, :],
                      2, gain=lambda t: V[:, V_KVN:V_KVN + 2])
            copy_product(g_uq, lambda n, t: ar(QROW + t * 1536 + n * BANK, BANK))
            for t in range(LT):
                sin = ang[:, t * 16:(t + 1) * 16]
                cos = cosa[:, t * 16:(t + 1) * 16]
                q = ar(QROW + t * 1536, 1536).rearrange("p (h e) -> p h e", h=MLA_H)
                s3, c3_ = (a.unsqueeze(1).broadcast_to([P, MLA_H, 16]) for a in (sin, cos))
                t1, t2 = (rows(0)[:, n * 256:(n + 1) * 256].rearrange("p (h e) -> p h e", h=MLA_H) for n in range(2))
                x1, x2_ = q[:, :, NOPE:NOPE + 16], q[:, :, NOPE + 16:MLA_DK]
                v(tt(t1, x1, c3_, ALU.mult))
                v(tt(t2, x2_, s3, ALU.mult))
                v(tt(t1, t1, t2, ALU.subtract))
                v(tt(t2, x1, s3, ALU.mult))
                v(copy(x1, t1))
                v(tt(t1, x2_, c3_, ALU.mult))
                v(tt(x2_, t1, t2, ALU.add))
                a = ar(AROW + t * wide + MLA_QR + MLA_KVR, ROT)
                r = rows(1)[:, t * 64:(t + 1) * 64]
                v(tt(r[:, 0:16], a[:, 0:16], cos, ALU.mult))
                v(tt(r[:, 16:32], a[:, 16:32], sin, ALU.mult))
                v(tt(r[:, 32:48], r[:, 0:16], r[:, 16:32], ALU.subtract))
                v(tt(r[:, 0:16], a[:, 16:32], cos, ALU.mult))
                v(tt(r[:, 16:32], a[:, 0:16], sin, ALU.mult))
                v(tt(r[:, 48:64], r[:, 0:16], r[:, 16:32], ALU.add))
            say(src_ready)
            copy_product(g_ukv, lambda n, t: ar(KV + t * 2048 + n * BANK, BANK))
            for t in range(LT):
                r = rows(1)[:, t * 64:(t + 1) * 64]
                k = ar(KROW + t * 1536, 1536).rearrange("p (h e) -> p h e", h=MLA_H)
                kv = ar(KV + t * 2048, 2048).rearrange("p (h e) -> p h e", h=MLA_H)
                v(copy(k[:, :, 0:NOPE], kv[:, :, 0:NOPE]))
                v(copy(k[:, :, NOPE:MLA_DK], r[:, 32:64].unsqueeze(1).broadcast_to([P, MLA_H, ROT])))
            say(src_ready)
            for place in (QT, KT):
                for t in range(LT):
                    for h in range(0, MLA_H, 4):
                        dst = ar(place, 4096).rearrange("p (h t) -> p h t", h=MLA_H)
                        copy_turned(dst[0:MLA_DK, h:h + 4, t * P:(t + 1) * P])
            attention(mla_units())
            close_block(0, g_mla_o)

            norm_turn(LT, h_tile, x2, gain=lambda t: V[:, V_NG0 + 8:V_NG0 + 16], split=x2_parts)

            def dil_copy(n):
                g, part, half = n // 6, n % 6 // 2, n % 2
                if part < 2:
                    for t in range(LT):
                        dst = ar((DQT, DKT)[part], 6144).rearrange("p (g h t) -> p g h t", g=DIL_G, h=8)
                        copy_turned(dst[:, g, half * 4:half * 4 + 4, t * P:(t + 1) * P])
            for n in range(19):
                if n < 18:
                    g, part, half = n // 6, n % 6 // 2, n % 2
                    for t in range(LT):
                        bank = product_bank()
                        if part == 2:
                            v(copy(ar(DV + t * 3072 + g * D + half * BANK, BANK), bank[:, :]), acc_used)
                        else:
                            c = (n * LT + t) % 4 * BANK
                            v(ts(hs[:, c:c + BANK], bank[:, :], 0.125 if part == 0 else 1.0, None, ALU.mult), acc_used)
                if n > 0:
                    dil_copy(n - 1)
            say(misc_ask)
            say(misc_ask)
            attention(dil_units())
            for par in range(2):
                seen.next(bias_in[par], 16 * DIL_H // 2)
            close_block(1, g_dil_o)

            def rope_axial(dst, bank, t, scale):
                x = bank.rearrange("p (m a b e) -> p m a b e", m=8, a=2, b=2)
                r = rows(t % 2)
                t1 = brow[:, 0:512]
                t2 = brow[:, 512:1024].rearrange("p (m a b e) -> p m a b e", m=8, a=2, b=2)
                cos = C[:, C_COS + 64 * t:C_COS + 64 * t + 64].unsqueeze(1).broadcast_to([P, 8, 64])
                sin = C[:, C_SIN + 64 * t:C_SIN + 64 * t + 64].rearrange("p (a b e) -> p a b e", a=2, b=2)
                v(tt(t1.rearrange("p (m e) -> p m e", m=8), bank.rearrange("p (m e) -> p m e", m=8), cos, ALU.mult))
                for a in range(2):
                    for b in range(2):
                        s = sin[:, a, b, :].unsqueeze(1).broadcast_to([P, 8, 16])
                        v(tt(t2[:, :, a, b, :], x[:, :, a, 1 - b, :], s, ALU.mult))
                if scale == 1.0:
                    v(tt(dst, t1, brow[:, 512:1024], ALU.add), acc_used)
                else:
                    v(tt(t1, t1, brow[:, 512:1024], ALU.add))
                    v(ts(dst, t1, scale, None, ALU.mult), acc_used)

            def first_max(dst, src, iota, tiles, n, tmp, col):
                mx = small[:, col:col + tiles]
                v(red(mx, src, X, ALU.max))
                v(tt(tmp, src, spread(mx, tiles, n), ALU.is_equal))
                v(tt(tmp, tmp, iota, ALU.mult))
                mn = small[:, 160:160 + tiles]
                v(red(mn, tmp, X, ALU.min))
                v(tt(dst, spread(mn, tiles, n), iota, ALU.is_equal))

            def experts(layer):
                b = layer * NE

                def turned(e, i):
                    dve.wait_ge(xt_ready, b + e + 1 + 2 * i)
                    if e >= 2:
                        dve.wait_ge(gu_ready, b + e - 1 + 2 * i)
                    copy(A[:, E_XG + e % 2 * 512:E_XG + e % 2 * 512 + 512], ps[4][:, :]).then_inc(xg_ready, 1)

                def sums(e, i):
                    dve.wait_ge(halves_ready, b + e + 1 + 2 * i)
                    if e >= 1:
                        dve.wait_ge(hd_ready, b + e + 2 * i)
                    tt(A[0:CAP, E_SUM:E_SUM + 2 * BANK], pair[0][0:CAP, :], A[0:CAP, E_UP:E_UP + 2 * BANK],
                       ALU.add).then_inc(summed, 1)

                def hidden(e, i):
                    hd = A[0:CAP, E_HD + e % 2 * 512:E_HD + e % 2 * 512 + 512]
                    dve.wait_ge(summed, b + e + 1 + 2 * i)
                    dve.wait_ge(esig_ready, b + e + 1 + 2 * i)
                    if e >= 2:
                        dve.wait_ge(hT_ready, b + e - 1 + 2 * i)
                    tt(hd, A[0:CAP, E_SUM:E_SUM + 512], A[0:CAP, E_SG:E_SG + 512], ALU.mult).then_inc(gated, 1)
                    dve.wait_ge(gated, b + e + 1 + 2 * i)
                    tt(hd, A[0:CAP, E_SUM + 512:E_SUM + 1024], hd, ALU.mult).then_inc(hd_ready, 1)

                def y_sum(e, i):
                    par = e % 2
                    dve.wait_ge(y_half, b + e + 1 + 2 * i)
                    if e >= 2 or layer:
                        dve.wait_ge(ys_out[par], 16 * (b // 2 + e // 2) + 16 * i)
                    tt(A[0:CAP, E_Y + par * D:E_Y + (par + 1) * D], pair[1][0:CAP, :], A[0:CAP, E_YR:E_YR + D],
                       ALU.add).then_inc(y_ready, 1)

                def hidden_turned(e, i):
                    dve.wait_ge(hT_ready, b + e + 1 + 2 * i)
                    if e >= 2:
                        dve.wait_ge(d_ready, b + e - 1 + 2 * i)
                    copy(A[:, E_HT + e % 2 * 256:E_HT + e % 2 * 256 + 256], ps[5][:, 0:256]).then_inc(hTs_ready, 1)

                def stage(e, i):
                    hidden_turned(e - 1, i)
                    sums(e, i)
                    if e < NE - 1:
                        turned(e + 1, i)
                    hidden(e, i)
                    y_sum(e - 1, i)

                turned(0, 0)
                sums(0, 0)
                turned(1, 0)
                hidden(0, 0)
                stage(1, 0)
                stage(2, 0)
                with dve.Fori(0, 14) as i:
                    stage(3, i)
                    stage(4, i)
                stage(NE - 1, 0)
                hidden_turned(NE - 1, 0)
                y_sum(NE - 1, 0)
                over, n_over = ov[layer], all_tiles[layer] * P * 2 // CAP
                some = dve.value_load(route_i[0:1, 0:1], min_val=0, max_val=n_over)
                with dve.If(some > 0):
                    dve.wait_ge(y_ready, b + NE)
                    with dve.Fori(0, n_over) as j:
                        dve.wait_ge(over["xT"], j + 1)
                        copy(A[:, E_XG:E_XG + 512], ps[4][:, :]).then_inc(over["xT_copied"], 1)
                        dve.wait_ge(over["halves"], j + 1)
                        tt(A[0:CAP, E_SUM:E_SUM + 2 * BANK], pair[0][0:CAP, :], A[0:CAP, E_UP:E_UP + 2 * BANK],
                           ALU.add).then_inc(over["summed"], 1)
                        dve.wait_ge(over["summed"], j + 1)
                        dve.wait_ge(over["sigmoid"], j + 1)
                        hd = A[0:CAP, E_HD:E_HD + 512]
                        tt(hd, A[0:CAP, E_SUM:E_SUM + 512], A[0:CAP, E_SG:E_SG + 512],
                           ALU.mult).then_inc(over["gated"], 1)
                        dve.wait_ge(over["gated"], j + 1)
                        tt(hd, A[0:CAP, E_SUM + 512:E_SUM + 1024], hd, ALU.mult).then_inc(over["hidden"], 1)
                        dve.wait_ge(over["hiddenT"], j + 1)
                        copy(A[:, E_HT:E_HT + 256], ps[5][:, 0:256]).then_inc(over["hiddenT_copied"], 1)
                        dve.wait_ge(over["y_half"], j + 1)
                        tt(A[0:CAP, E_Y:E_Y + D], pair[1][0:CAP, :], A[0:CAP, E_YR:E_YR + D],
                           ALU.add).then_inc(over["y_copied"], 1)

            for layer in range(DEPTH):
                tiles = all_tiles[layer]
                lam_init = 0.8 - 0.6 * math.exp(-0.3 * layer)
                say(misc_ask)
                say(misc_ask)
                if layer == 0:
                    say(act_req)
                    answered()
                    v(tt(small[:, 128:144], V[:, V_COND:V_COND + 16], small[:, 144:160], ALU.mult))
                say(src_ready)
                loaded(2)
                for n in range(2):
                    v(tt(rows(0)[:, 0:64], brow[:, n * 128:n * 128 + 64], brow[:, n * 128 + 64:n * 128 + 128], ALU.mult))
                    v(red(small[:, 98 + n:99 + n], rows(0)[:, 0:64], X, ALU.add), act_req if n else dve_step)
                answered()
                v(tt(small[:, 96:97], small[:, 99:100], small[:, 98:99], ALU.subtract))
                v(ts(small[:, 96:97], small[:, 96:97], lam_init, None, ALU.subtract))
                def spread_ada(n):
                    part = n // 2
                    if part in (2, 5):
                        for j in range(2):
                            a = ((part // 5) * 2 + j) * D + n % 2 * BANK
                            v(copy(GT[:, a:a + BANK], turned_bank()[:, :]), tr_used)
                    else:
                        pi_ = (0, 1, None, 2, 3)[part]
                        a = (pi_ * 8 + n % 2 * 4) * 2
                        v(copy(mcol[:, a:a + 8], turned_bank()[:, 0:8]), tr_used)
                for n in range(12):
                    bank = product_bank()
                    v(tt(ada_row[0:2, n % 2 * BANK:(n % 2 + 1) * BANK], bank[0:2, :],
                         A[0:2, n * BANK:(n + 1) * BANK], ALU.add), acc_used)
                    if n > 0:
                        spread_ada(n - 1)
                spread_ada(11)
                for which in range(2):
                    gain = V[:, (V_MIX, V_FFN)[which] + layer * 8:(V_MIX, V_FFN)[which] + layer * 8 + 8]
                    m = mcol[:, :].rearrange("p (w k c) -> p w k c", w=4, k=8)
                    for cond in range(2):
                        c = ccol[:, (which * 2 + cond) * 8:(which * 2 + cond) * 8 + 8]
                        v(tt(c, m[:, 2 * which + 1, :, cond], gain, ALU.mult))
                        v(tt(c, c, gain, ALU.add))

                def gains(which):
                    return lambda t: ccol[:, (which * 2 + t // LT) * 8:(which * 2 + t // LT) * 8 + 8]

                def shifts(which):
                    return lambda t: mcol[:, :].rearrange("p (w k c) -> p w k c", w=4, k=8)[:, 2 * which, :, t // LT]

                norm_turn(MAX_TILES, h_tile, x4, gain=gains(0), shift=shifts(0), split=x4_parts(Y_r[:, :], Y[:, :]))
                say(x_ready)
                for n in range(4):
                    if n in (1, 3):
                        for t in range(MAX_TILES):
                            copy_turned((kaT if n == 1 else kcT)[:, :, t * P:(t + 1) * P])
                    for t in range(MAX_TILES):
                        bank = product_bank()
                        r = hs[:, (n * MAX_TILES + t) % 4 * BANK:(n * MAX_TILES + t) % 4 * BANK + BANK]
                        if n == 0 and t < LT:
                            rope_axial(r, bank, t, 1.0)
                        elif n in (0, 2):
                            v(copy(r, bank[:, :]), acc_used)
                        else:
                            v(copy(ar((VA if n == 1 else VC) + t * 512, 512), bank[:, :]), acc_used)
                gelu_banks = []

                def end_gelu(u):
                    answered()
                    y = rows(1)[:, u % 2 * BANK:(u % 2 + 1) * BANK]
                    t = u % tiles
                    if u < tiles:
                        v(tt(ar(U + t * 512, BANK), gelu_banks[u][:, :], y, ALU.mult), acc_used)
                    else:
                        v(nc.vector.tensor_tensor_reduce(
                            out=ar(VV + t * 512, BANK), in0=gelu_banks[u][:, :], in1=y, scale=1.0, scalar=0.0,
                            op0=ALU.mult, op1=ALU.add, accum_out=small[:, 112 + t:113 + t]), acc_used)
                for n in range(4):
                    if n in (1, 2):
                        for t in range(tiles):
                            copy_turned((qaT if n == 1 else qcT)[:, :, t * P:(t + 1) * P])
                    if n == 2:
                        say(misc_ask)
                        say(misc_ask)
                        say(misc_ask)
                    if n == 3:
                        end_gelu(tiles - 1)
                    for t in range(tiles):
                        bank = product_bank()
                        r = hs[:, (n * tiles + t) % 4 * BANK:(n * tiles + t) % 4 * BANK + BANK]
                        if n == 0 and t < LT:
                            rope_axial(r, bank, t, 0.125)
                        elif n < 2:
                            v(ts(r, bank[:, :], 0.125, None, ALU.mult), acc_used)
                        else:
                            u = (n - 2) * tiles + t
                            y = rows(1)[:, u % 2 * BANK:(u % 2 + 1) * BANK]
                            say(act_req)
                            if t > 0:
                                end_gelu(u - 1)
                            answered()
                            k = 2 * math.sqrt(2 / math.pi)
                            v(ts(y, y, k * 0.044715, k, ALU.mult, ALU.add))
                            v(tt(y, y, bank[:, :], ALU.mult), act_req)
                            gelu_banks.append(bank)
                end_gelu(2 * tiles - 1)
                for t in range(tiles):
                    vt = ar(VV + t * 512, BANK)
                    v(ts(small[:, 112 + t:113 + t], small[:, 112 + t:113 + t], 1.0 / BANK, None, ALU.mult))
                    v(ts(vt, vt, small[:, 112 + t:113 + t], None, ALU.subtract))
                    square_sum(vt, t, BANK)
                rstd(tiles, BANK)
                loaded(2)
                loaded()
                for t in range(tiles):
                    vt = ar(VV + t * 512, BANK)
                    v(stt(vt, vt, small[:, 48 + t:49 + t], brow[:, 0:512], ALU.mult, ALU.mult))
                    v(tt(vt, vt, brow[:, 512:1024], ALU.add), src_ready)
                for t in range(tiles):
                    bank = turned_bank()
                    sgb = V[:, V_SGB + layer * 4:V_SGB + layer * 4 + 4]
                    r = rows(0)[:, 0:BANK]
                    v(tt(r.rearrange("p (g c) -> p g c", g=4), bank[:, :].rearrange("p (g c) -> p g c", g=4),
                         spread(sgb, 4, P), ALU.add), tr_used)
                    ut = ar(U + t * 512, BANK)
                    v(tt(ut, ut, r, ALU.mult))
                say(misc_ask)
                dve.wait_ge(low_saved, 16 * (layer + 1))
                for units in second_units(layer):
                    attention(units)
                say(misc_ask)
                for t in range(tiles):
                    for h in range(4):
                        square_sum(ar(YA + t * 512 + h * P, P), t * 4 + h, P)
                rstd(4 * tiles, P)
                loaded()
                v(ts(brow[:, 0:P], brow[:, 0:P], 1.0 - lam_init, None, ALU.mult))
                for t in range(tiles):
                    for h in range(4):
                        y = ar(YA + t * 512 + h * P, P)
                        v(stt(y, y, small[:, 48 + t * 4 + h:49 + t * 4 + h], brow[:, 0:P], ALU.mult, ALU.mult))
                say_n = 3 * tiles
                for _ in range(say_n):
                    say(src_ready)
                for t in range(tiles):
                    for b in range(3):
                        dst = ar(YT, 6144).rearrange("p (k t c) -> p k t c", k=12, t=MAX_TILES)
                        copy_turned(dst[:, b * 4:b * 4 + 4, t, :])
                say(misc_ask)
                say(misc_ask)
                for n in range(6):
                    half, b = n // 3, n % 3
                    for t in range(tiles):
                        bank = product_bank()
                        v(copy(ar(MERGED_SIG + t * 512, BANK), bank[:, :]), acc_used)
                        say(act_req)
                    for t in range(tiles):
                        bank = product_bank()
                        answered()
                        y = y_tile(t)[:, half * BANK:(half + 1) * BANK]
                        sg = ar(MERGED_SIG + t * 512, BANK)
                        if b == 0:
                            v(tt(y, bank[:, :], sg, ALU.mult), acc_used)
                        else:
                            v(tt(rows(0)[:, 0:BANK], bank[:, :], sg, ALU.mult), acc_used)
                            v(tt(y, y, rows(0)[:, 0:BANK], ALU.add))
                turn(tiles, y_tile, x4, scaled=False, split=x4_parts(A_r[:, XL:XL + 4096], ar(XL, 4096)))

                def gate(which, t, half):
                    a = (which * 2 + t // LT) * D + half * BANK
                    return GT[:, a:a + BANK]
                for n in range(2):
                    for t in range(tiles):
                        bank = product_bank()
                        v(tt(rows(0)[:, 0:BANK], bank[:, :], gate(0, t, n), ALU.mult), acc_used)
                        part = h_tile(t)[:, n * BANK:(n + 1) * BANK]
                        v(tt(part, part, rows(0)[:, 0:BANK], ALU.add))
                norm_turn(tiles, h_tile, x4, gain=gains(1), shift=shifts(1))
                for t in range(tiles):
                    for g in range(2):
                        v(copy(ar(XTOK + t * D + g * BANK, BANK), turned_bank()[:, :]), tr_used)
                loaded(2)
                say(src_ready)

                def rt(n, width=NE):
                    return ar(RT + 128 * n, tiles * width).rearrange("p (t e) -> p t e", t=tiles)
                logits = ar(RT + 128 * 22, 144)[:, 0:tiles * 36].rearrange("p (t e) -> p t e", t=tiles)
                bank = turned_bank()
                v(tt(logits, bank[:, 0:tiles * 36].rearrange("p (t e) -> p t e", t=tiles),
                     vrow[:, 0:36].unsqueeze(1).broadcast_to([P, tiles, 36]), ALU.add), tr_used)
                iota = rt(2)
                e_idx = C[:, C_EIDX:C_EIDX + NE].unsqueeze(1).broadcast_to([P, tiles, NE])
                v(ts(iota, e_idx, -64.0, None, ALU.add))
                g_log = logits[:, :, 0:NGRP]
                hot_g, tmp_g = rt(3, NGRP), rt(4, NGRP)
                first_max(hot_g, g_log, iota[:, :, 0:NGRP], tiles, NGRP, tmp_g, 164)
                v(tt(rt(1, NGRP), g_log, spread(small[:, 164:164 + tiles], tiles, NGRP), ALU.subtract), act_req)
                answered()
                v(red(small[:, 168:168 + tiles], rt(1, NGRP), X, ALU.add))
                v(nc.vector.reciprocal(small[:, 168:168 + tiles], small[:, 168:168 + tiles]))
                masked, floor = rt(5), rt(6, NGRP)
                v(ts(floor, hot_g, -NEG, NEG, ALU.mult, ALU.add))
                for t in range(tiles):
                    m4 = masked[:, t, :].rearrange("p (g e) -> p g e", g=NGRP)
                    v(tt(m4, logits[:, t, NGRP:].rearrange("p (g e) -> p g e", g=NGRP),
                         spread(hot_g[:, t, :], NGRP, EPG), ALU.mult))
                    v(tt(m4, m4, spread(floor[:, t, :], NGRP, EPG), ALU.add))
                first, second, tmp, both = rt(7), rt(8), rt(9), rt(0)
                first_max(first, masked, iota, tiles, NE, tmp, 172)
                v(stt(masked, first, 2 * NEG, masked, ALU.mult, ALU.add))
                first_max(second, masked, iota, tiles, NE, tmp, 176)
                v(tt(both, first, second, ALU.add), src_ready)
                v(tt(small[:, 104:104 + tiles], small[:, 176:176 + tiles], small[:, 172:172 + tiles], ALU.subtract),
                  act_req)
                answered()
                v(ts(small[:, 180:180 + tiles], small[:, 104:104 + tiles], 1.0, None, ALU.add))
                v(nc.vector.reciprocal(small[:, 180:180 + tiles], small[:, 180:180 + tiles]))
                v(tt(route[:, 0:tiles], small[:, 180:180 + tiles], small[:, 168:168 + tiles], ALU.mult))
                v(tt(route[:, 4:4 + tiles], route[:, 0:tiles], small[:, 104:104 + tiles], ALU.mult))
                before, count = rt(10), ar(RT + 128 * 11, NE)
                bank = turned_bank()
                v(copy(ar(RT + 128 * 12, 160)[:, 0:(tiles + 1) * NE], bank[:, 0:(tiles + 1) * NE]), tr_used)
                before = ar(RT + 128 * 12, tiles * NE).rearrange("p (t e) -> p t e", t=tiles)
                count = ar(RT + 128 * 12 + tiles * NE, NE)
                n_blocks = tiles * P // CAP
                blocks, run, run2, t32 = (ar(RT + 128 * 15 + 32 * n, NE) for n in range(4))
                v(nc.vector.memset(blocks, 0.0))
                for j in range(1, n_blocks):
                    v(stt(blocks, count, float(j * CAP), blocks, ALU.is_gt, ALU.add))
                v(copy(run, blocks))
                a, b_ = run, run2
                for s in (1, 2, 4, 8, 16):
                    v(copy(b_[:, 0:s], a[:, 0:s]))
                    v(tt(b_[:, s:NE], a[:, s:NE], a[:, 0:NE - s], ALU.add))
                    a, b_ = b_, a
                run = a
                start = t32
                v(tt(start, run, blocks, ALU.subtract))
                for k, hot in enumerate((first, second)):
                    picked = small[:, 184 + 12 * k:196 + 12 * k]
                    for m, table in enumerate((before, e_idx, start.unsqueeze(1).broadcast_to([P, tiles, NE]))):
                        v(tt(tmp, hot, table, ALU.mult))
                        v(red(picked[:, 4 * m:4 * m + tiles], tmp, X, ALU.add))
                    place, expert_, begin = (picked[:, 4 * m:4 * m + tiles] for m in range(3))
                    q, past, row_ = (small[:, 208 + 4 * m:208 + 4 * m + tiles] for m in range(3))
                    v(nc.vector.memset(q, 0.0))
                    for j in range(1, n_blocks):
                        v(stt(q, place, float(j * CAP), q, ALU.is_ge, ALU.add))
                    v(tt(row_, expert_, q, ALU.subtract))
                    v(ts(row_, row_, float(CAP), None, ALU.mult))
                    v(tt(row_, row_, place, ALU.add))
                    v(tt(past, begin, expert_, ALU.subtract))
                    v(tt(past, past, q, ALU.add))
                    v(ts(past, past, float(NE - 1), float(CAP), ALU.add, ALU.mult))
                    v(ts(q, q, 0.0, None, ALU.is_gt))
                    v(tt(past, past, q, ALU.mult))
                    v(tt(row_, row_, past, ALU.add))
                    v(copy(route_u[:, k * MAX_TILES:k * MAX_TILES + tiles], row_))
                n_over = 2 * tiles * P // CAP
                table = ar(RT + 128 * 16, n_over * NE).rearrange("p (j e) -> p j e", j=n_over)
                v(tt(table, run.unsqueeze(1).broadcast_to([P, n_over, NE]),
                     spread(C[:, C_OIDX:C_OIDX + n_over], n_over, NE), ALU.is_le))
                ofs = small[:, 224:224 + n_over]
                v(red(ofs, table, X, ALU.add))
                v(ts(ofs, ofs, float(NE - 1), None, ALU.min))
                v(copy(route_i[:, 1:1 + n_over], ofs))
                v(copy(route_i[:, 0:1], run[:, NE - 1:NE]), route_ready)
                experts(layer)
                for t in range(tiles):
                    dve.wait_ge(gather_in[t % 2], seen.next(gather_in[t % 2], 32))
                    y1, y2 = (ar(YG + (t % 2 * 2 + k) * D, D) for k in range(2))
                    v(ts(y1, y1, route[:, t:t + 1], None, ALU.mult))
                    v(stt(y1, y2, route[:, 4 + t:5 + t], y1, ALU.mult, ALU.add))
                    v(tt(y1, y1, GT[:, (2 + t // LT) * D:(3 + t // LT) * D], ALU.mult))
                    v(tt(h_tile(t), h_tile(t), y1, ALU.add))
                    if t < tiles - 2:
                        say(misc_ask)
            say(misc_ask)
            for t in range(LT):
                square_sum(h_tile(t), t, D)
            rstd(LT, D)
            loaded()
            for t in range(LT):
                v(stt(y_tile(t), h_tile(t), small[:, 48 + t:49 + t], brow[:, :], ALU.mult, ALU.mult),
                  final_ready if t == LT - 1 else dve_step)


def kernel(**inputs):
    import concourse.bacc as bacc
    from concourse.bass_utils import run_bass_kernel_spmd

    a = {k: np.asarray(v) for k, v in inputs.items()}
    c, hot = constants()

    def cols(x):
        return x.reshape(-1, P).T

    v = [cols(a["norm_g"][i, 0]) for i in range(DEPTH)] + [cols(a["norm_g"][i, 2]) for i in range(DEPTH)]
    v += [cols(a["mla_q_norm"][0]), cols(a["mla_kv_norm"][0])]
    v += [cols(a["g_norm_mix_2"][i]) for i in range(DEPTH)] + [cols(a["g_norm_ffn_2"][i]) for i in range(DEPTH)]
    v += [np.stack([cols(a["c_2"][0]), cols(a["c_ctx_2"])], axis=2).reshape(P, 2 * KD)]
    v += [a["sg_b_2"][i].T for i in range(DEPTH)]
    arrays = {
        "constants": c,
        "hot": hot,
        "vectors": np.concatenate(v, axis=1),
        "positions": a["positions"].reshape(LT, P).T,
        "ffn_w_in": a["ffn_w_in"].reshape(DEPTH, D, 2, D_FF // FF_PIECE, FF_PIECE).transpose(0, 1, 3, 2, 4)
                                 .reshape(DEPTH, D, 2 * D_FF),
        "p_t": a["p"][:, 0].transpose(0, 2, 1),
        "sg_wt": a["sg_w_2"].transpose(0, 1, 3, 2),
        "router_w": np.concatenate([a["moe_w_group_2"], a["moe_w_router_2"]], axis=2),
        "router_b": np.concatenate([a["moe_b_group_2"], a["moe_b_router_2"]], axis=1),
    }
    for name in ("x", "ctx_2", "norm_g", "ffn_w_out", "ple_w_proj", "ple_w_gate", "rel_bias", "mla_w_a",
                 "mla_w_uq", "mla_w_ukv", "mla_w_o", "dil_w_qkv", "dil_w_o", "w_ada_2", "b_ada_2", "w_in_2",
                 "da_lambda_2", "da_subln_g_2", "sg_ln_g_2", "sg_ln_b_2", "na_rpb_2", "w_branch_2", "w_out_2",
                 "moe_w_gate_2", "moe_w_up_2", "moe_w_down_2", "g_final_2"):
        arrays[name] = a[name]

    nc = bacc.Bacc("TRN2", target_bir_lowering=False, num_devices=1)
    ins, feed = {}, {}
    for name, x in arrays.items():
        x = np.ascontiguousarray(x)
        feed[f"in_{name}"] = x
        ins[name] = nc.dram_tensor(f"in_{name}", x.shape, mybir.dt.from_np(x.dtype), kind="ExternalInput").ap()
    result = nc.dram_tensor("result", [1, SEQ, D], F32, kind="ExternalOutput").ap()
    build_program(nc, ins, result)
    r = run_bass_kernel_spmd(nc, [feed], core_ids=[0])
    return r.results[0]["result"]
```
